# Optimizing a Trainium2 kernel written in Bass

```python
import math
import jax, jax.numpy as jnp
from jax import lax
import numpy as np

D_MODEL = 1024
BATCH = 1
SEQ = 256
DEPTH = 2

CHUNK = 64
Q_BLOCK = 128

MLA_HEADS = 8
QK_NOPE_DIM = 64
QK_ROPE_DIM = 32
QK_HEAD_DIM = QK_NOPE_DIM + QK_ROPE_DIM
V_HEAD_DIM = 64
MLA_WIDTH = MLA_HEADS * V_HEAD_DIM
Q_LORA_RANK = 384
KV_LORA_RANK = 256
ROPE_THETA = 10000.0

SSM_WIDTH = 512
SSM_GROUP = 16
SSM_GROUPS = SSM_WIDTH // SSM_GROUP
SSM_STATE = 64
DT_MIN = 0.001
DT_MAX = 0.1

N_BRANCH = 2

COL_SPLITS = [
    Q_LORA_RANK,
    Q_LORA_RANK + KV_LORA_RANK,
    Q_LORA_RANK + KV_LORA_RANK + QK_ROPE_DIM,
    Q_LORA_RANK + KV_LORA_RANK + QK_ROPE_DIM + SSM_WIDTH,
]
IN_COLS = COL_SPLITS[-1] + N_BRANCH * D_MODEL

N_EXPERT_GROUPS = 4
EXPERTS_PER_GROUP = 8
N_EXPERTS = N_EXPERT_GROUPS * EXPERTS_PER_GROUP
TOP_K = 2
D_EXPERT = 256

EPS = 1e-6

kernel_name = "hybrid_mla_s5_hmoe_streaming"

def rmsnorm(x, g):
    xf = x.astype(jnp.float32)
    y = xf * lax.rsqrt(jnp.mean(xf * xf, axis=-1, keepdims=True) + EPS)
    return (y * g.astype(jnp.float32)).astype(x.dtype)

def rope_tables(positions):
    half = QK_ROPE_DIM // 2
    inv_freq = ROPE_THETA ** (-jnp.arange(half, dtype=jnp.float32) / half)
    ang = positions.astype(jnp.float32)[..., None] * inv_freq
    return jnp.cos(ang)[:, :, None, :], jnp.sin(ang)[:, :, None, :]

def apply_rope(x, cos, sin):
    half = QK_ROPE_DIM // 2
    x1, x2 = x[..., :half], x[..., half:]
    return jnp.concatenate([x1 * cos - x2 * sin, x2 * cos + x1 * sin], axis=-1).astype(x.dtype)

def mla_branch(q_c, kv_c, k_r, cos, sin, q_lora_g, w_uq, kv_lora_g, w_ukv,
               q_head_g, k_head_g, w_attn_proj):
    bsz, seq, _ = q_c.shape
    q = (rmsnorm(q_c, q_lora_g) @ w_uq).reshape(bsz, seq, MLA_HEADS, QK_HEAD_DIM)
    kv = (rmsnorm(kv_c, kv_lora_g) @ w_ukv).reshape(bsz, seq, MLA_HEADS, QK_NOPE_DIM + V_HEAD_DIM)
    k_nope, v = kv[..., :QK_NOPE_DIM], kv[..., QK_NOPE_DIM:]
    k_pe = jnp.broadcast_to(k_r[:, :, None, :], (bsz, seq, MLA_HEADS, QK_ROPE_DIM))
    k = jnp.concatenate([k_nope, k_pe], axis=-1)
    q = rmsnorm(q, q_head_g)
    k = rmsnorm(k, k_head_g)
    q = jnp.concatenate([q[..., :QK_NOPE_DIM], apply_rope(q[..., QK_NOPE_DIM:], cos, sin)], axis=-1)
    k = jnp.concatenate([k[..., :QK_NOPE_DIM], apply_rope(k[..., QK_NOPE_DIM:], cos, sin)], axis=-1)

    scale = QK_HEAD_DIM ** -0.5
    outs = []
    for qs in range(0, seq, Q_BLOCK):
        ke = qs + Q_BLOCK
        s = jnp.einsum('bqhd,bkhd->bhqk', q[:, qs:ke], k[:, :ke],
                       preferred_element_type=jnp.float32) * scale
        q_chunk = (qs + jnp.arange(Q_BLOCK)) // CHUNK
        k_chunk = jnp.arange(ke) // CHUNK
        mask = k_chunk[None, :] <= q_chunk[:, None]
        s = jnp.where(mask, s, jnp.finfo(jnp.float32).min)
        p = jax.nn.softmax(s, axis=-1).astype(v.dtype)
        outs.append(jnp.einsum('bhqk,bkhd->bqhd', p, v[:, :ke]))
    o = jnp.concatenate(outs, axis=1).reshape(bsz, seq, MLA_WIDTH)
    return o @ w_attn_proj

def _scan_combine(e1, e2):
    a1, b1 = e1
    a2, b2 = e2
    return a1 * a2, a2 * b1 + b2

def s5_branch(u, lam_re, lam_im, log_dt, b_re, b_im, c_re, c_im, d_skip, w_glu):
    bsz, seq, _ = u.shape
    uf = u.astype(jnp.float32).reshape(bsz, seq, SSM_GROUPS, SSM_GROUP)
    lam = lax.complex(lam_re.astype(jnp.float32), lam_im.astype(jnp.float32))
    dt = jnp.exp(log_dt.astype(jnp.float32))[:, None]
    lam_bar = jnp.exp(lam * dt)
    b = lax.complex(b_re.astype(jnp.float32), b_im.astype(jnp.float32))
    b_bar = ((lam_bar - 1.0) / lam)[..., None] * b
    bu = jnp.einsum('blgi,gpi->blgp', uf.astype(jnp.complex64), b_bar)
    a = jnp.broadcast_to(lam_bar[None, None], (1, seq, SSM_GROUPS, SSM_STATE))
    _, states = lax.associative_scan(_scan_combine, (a, bu), axis=1)
    c = lax.complex(c_re.astype(jnp.float32), c_im.astype(jnp.float32))
    y = jnp.einsum('blgp,gip->blgi', states, c).real + d_skip.astype(jnp.float32) * uf
    y = jax.nn.gelu(y.reshape(bsz, seq, SSM_WIDTH)).astype(u.dtype)
    vg = y @ w_glu
    val, gate = vg[..., :D_MODEL], vg[..., D_MODEL:]
    return val * jax.nn.sigmoid(gate)

def hier_moe(h, w_router_group, w_router_expert, w_exp_gate, w_exp_up, w_exp_down):
    bsz, seq, d = h.shape
    t = h.reshape(-1, d)
    n_tok = t.shape[0]
    g_prob = jax.nn.softmax((t @ w_router_group).astype(jnp.float32), axis=-1)
    g_idx = jnp.argmax(g_prob, axis=-1)
    g_w = jnp.take_along_axis(g_prob, g_idx[:, None], axis=-1)
    e_logits = (t @ w_router_expert).astype(jnp.float32).reshape(n_tok, N_EXPERT_GROUPS, EXPERTS_PER_GROUP)
    e_logits = jnp.take_along_axis(e_logits, g_idx[:, None, None], axis=1)[:, 0]
    e_prob = jax.nn.softmax(e_logits, axis=-1)
    top_w, top_i = lax.top_k(e_prob, TOP_K)
    top_w = top_w / jnp.sum(top_w, axis=-1, keepdims=True) * g_w
    eid = g_idx[:, None] * EXPERTS_PER_GROUP + top_i
    combine = jnp.sum(jax.nn.one_hot(eid, N_EXPERTS, dtype=jnp.float32) * top_w[..., None], axis=1)
    out = jnp.zeros((n_tok, d), jnp.float32)
    for e in range(N_EXPERTS):
        hidden = jax.nn.silu(t @ w_exp_gate[e]) * (t @ w_exp_up[e])
        out = out + (hidden @ w_exp_down[e]).astype(jnp.float32) * combine[:, e:e + 1]
    return out.astype(h.dtype).reshape(bsz, seq, d)

def setup_inputs(seed: int = 0) -> dict:
    key = jax.random.key(seed)
    ks = jax.random.split(key, 32)
    f32 = jnp.float32

    def nrm(k, shape, fan_in):
        return jax.random.normal(k, shape, f32) * (fan_in ** -0.5)

    def gain(k, shape):
        return 1.0 + 0.02 * jax.random.normal(k, shape, f32)

    x = jax.random.normal(ks[0], (BATCH, SEQ, D_MODEL), f32)
    offset = jax.random.randint(ks[1], (BATCH, 1), 0, 64, jnp.int32) * CHUNK
    positions = (offset + jnp.arange(SEQ, dtype=jnp.int32)[None, :]).astype(jnp.int32)

    n_idx = jnp.arange(SSM_STATE, dtype=f32)
    lam_re = -0.5 * (1.0 + 0.02 * jax.random.normal(ks[2], (DEPTH, SSM_GROUPS, SSM_STATE), f32))
    lam_im = math.pi * n_idx[None, None, :] + 0.01 * jax.random.normal(ks[3], (DEPTH, SSM_GROUPS, SSM_STATE), f32)
    log_dt = jax.random.uniform(ks[4], (DEPTH, SSM_GROUPS), f32, math.log(DT_MIN), math.log(DT_MAX))

    return {
        "x": x,
        "positions": positions,
        "norm_mix_g": gain(ks[5], (DEPTH, D_MODEL)),
        "w_in": nrm(ks[6], (DEPTH, D_MODEL, IN_COLS), D_MODEL),
        "q_lora_g": gain(ks[7], (DEPTH, Q_LORA_RANK)),
        "w_uq": nrm(ks[8], (DEPTH, Q_LORA_RANK, MLA_HEADS * QK_HEAD_DIM), Q_LORA_RANK),
        "kv_lora_g": gain(ks[9], (DEPTH, KV_LORA_RANK)),
        "w_ukv": nrm(ks[10], (DEPTH, KV_LORA_RANK, MLA_HEADS * (QK_NOPE_DIM + V_HEAD_DIM)), KV_LORA_RANK),
        "q_head_g": gain(ks[11], (DEPTH, QK_HEAD_DIM)),
        "k_head_g": gain(ks[12], (DEPTH, QK_HEAD_DIM)),
        "w_attn_proj": nrm(ks[13], (DEPTH, MLA_WIDTH, D_MODEL), MLA_WIDTH),
        "lam_re": lam_re,
        "lam_im": lam_im,
        "log_dt": log_dt,
        "b_re": nrm(ks[14], (DEPTH, SSM_GROUPS, SSM_STATE, SSM_GROUP), 2 * SSM_GROUP),
        "b_im": nrm(ks[15], (DEPTH, SSM_GROUPS, SSM_STATE, SSM_GROUP), 2 * SSM_GROUP),
        "c_re": nrm(ks[16], (DEPTH, SSM_GROUPS, SSM_GROUP, SSM_STATE), 2 * SSM_STATE),
        "c_im": nrm(ks[17], (DEPTH, SSM_GROUPS, SSM_GROUP, SSM_STATE), 2 * SSM_STATE),
        "d_skip": jax.random.normal(ks[18], (DEPTH, SSM_GROUPS, SSM_GROUP), f32),
        "w_glu": nrm(ks[19], (DEPTH, SSM_WIDTH, 2 * D_MODEL), SSM_WIDTH),
        "w_out": nrm(ks[20], (DEPTH, D_MODEL, D_MODEL), D_MODEL),
        "norm_ffn_g": gain(ks[21], (DEPTH, D_MODEL)),
        "w_router_group": nrm(ks[22], (DEPTH, D_MODEL, N_EXPERT_GROUPS), D_MODEL),
        "w_router_expert": nrm(ks[23], (DEPTH, D_MODEL, N_EXPERTS), D_MODEL),
        "w_exp_gate": nrm(ks[24], (DEPTH, N_EXPERTS, D_MODEL, D_EXPERT), D_MODEL),
        "w_exp_up": nrm(ks[25], (DEPTH, N_EXPERTS, D_MODEL, D_EXPERT), D_MODEL),
        "w_exp_down": nrm(ks[26], (DEPTH, N_EXPERTS, D_EXPERT, D_MODEL), D_EXPERT),
    }

def reference(x, positions, norm_mix_g, w_in, q_lora_g, w_uq, kv_lora_g, w_ukv,
              q_head_g, k_head_g, w_attn_proj, lam_re, lam_im, log_dt, b_re, b_im,
              c_re, c_im, d_skip, w_glu, w_out, norm_ffn_g, w_router_group,
              w_router_expert, w_exp_gate, w_exp_up, w_exp_down):
    bsz, seq, _ = x.shape
    cos, sin = rope_tables(positions)
    for l in range(DEPTH):
        h = rmsnorm(x, norm_mix_g[l])
        proj = h @ w_in[l]
        q_c, kv_c, k_r, u, gates = jnp.split(proj, COL_SPLITS, axis=-1)
        y_attn = mla_branch(q_c, kv_c, k_r, cos, sin, q_lora_g[l], w_uq[l], kv_lora_g[l],
                            w_ukv[l], q_head_g[l], k_head_g[l], w_attn_proj[l])
        y_ssm = s5_branch(u, lam_re[l], lam_im[l], log_dt[l], b_re[l], b_im[l],
                          c_re[l], c_im[l], d_skip[l], w_glu[l])
        g = jax.nn.sigmoid(gates).reshape(bsz, seq, N_BRANCH, D_MODEL)
        merged = g[:, :, 0, :] * y_attn + g[:, :, 1, :] * y_ssm
        x = x + merged @ w_out[l]
        h = rmsnorm(x, norm_ffn_g[l])
        x = x + hier_moe(h, w_router_group[l], w_router_expert[l], w_exp_gate[l],
                         w_exp_up[l], w_exp_down[l])
    return x


_drawn_inputs = setup_inputs


def setup_inputs(seed=0):
    import zlib

    import numpy as np

    out = dict(_drawn_inputs(seed))
    spreads = {}
    factors = {'norm_mix_g': 2.857,
     'q_lora_g': 6.72,
     'kv_lora_g': 3.587,
     'q_head_g': 6.216,
     'k_head_g': 4.421,
     'lam_re': 8.0}
    for name, (base, spread) in spreads.items():
        noise = np.random.default_rng([zlib.crc32(name.encode()), seed]).standard_normal(out[name].shape)
        drawn = base * np.exp(spread * noise) if base else spread * noise
        out[name] = __import__('jax').numpy.asarray(drawn.astype(out[name].dtype))
    for name, factor in factors.items():
        out[name] = (out[name] * factor).astype(out[name].dtype)
    return out
```

```python
import math
from contextlib import ExitStack

import numpy as np

import concourse.bass as bass
from concourse import mybir

ALU = mybir.AluOpType
ACT = mybir.ActivationFunctionType
AXX = mybir.AxisListType.X
F32 = mybir.dt.float32
I32 = mybir.dt.int32

P = 128
D = 1024
SEQ = 256
DEPTH = 2
TT = SEQ // P
KC = D // P

HEADS, NOPE, ROPE = 8, 64, 32
QKD = NOPE + ROPE
VD = 64
QR, KVR = 384, 256
QC, KVC = QR // P, KVR // P
CHUNK = 64
HALF = ROPE // 2
THETA = 10000.0
SCALE = QKD ** -0.5
MASKED = -1.0e30

SSM = 512
GRP = 16
GROUPS = SSM // GRP
NST = 64
STILES = GROUPS * NST // P
CH_T = SSM // P
QPT = STILES // CH_T

COLS = QR + KVR + ROPE + SSM + 2 * D
U0 = QR + KVR + ROPE
G0 = U0 + SSM
TAIL = U0 - 512

EG, EPG = 4, 8
NE = EG * EPG
NPAIR = NE // 2
DE = 256
SLOT = 64
PASSES = SEQ // SLOT
ROUTE = EG + NE
NPOS = 2 * SEQ
EPS = 1e-6

TWO_PI = 2.0 * math.pi
ROUND = 1.5 * 2.0 ** 23


def split_two_pi():
    parts, rest = [], TWO_PI
    for step in (2.0 ** -5, 2.0 ** -14):
        part = math.floor(rest / step) * step
        parts.append(part)
        rest -= part
    return parts + [rest]


A_SLOTS, B_SLOTS = 4, 4
A_SIZE, B_SIZE = 4096, 2048
A_U, A_Q, A_TAIL, A_G, A_GLU, A_AP, A_OUT = 0, 1, 2, 3, 7, 9, 10
A_MIX = 12
A_USES = (A_MIX + NE) // A_SLOTS
assert (A_MIX + NE) % A_SLOTS == 0 and A_MIX % A_SLOTS == 0


def bc(ap, axis, n):
    ap = ap.unsqueeze(axis)
    shape = list(ap.shape)
    shape[axis] = n
    return ap.broadcast_to(shape)


class Count:

    def __init__(self):
        self.n = 0

    def add(self):
        self.n += 1
        return 1


def build(nc, t, out):
    ctx = ExitStack()
    with ctx:
        def sb(name, shape, dt=F32):
            return ctx.enter_context(nc.sbuf_tensor(name, shape, dt))

        loaded_a = [ctx.enter_context(nc.semaphore(f"loaded_a{i}")) for i in range(A_SLOTS)]
        free_a = [ctx.enter_context(nc.semaphore(f"free_a{i}")) for i in range(A_SLOTS)]
        loaded_b = [ctx.enter_context(nc.semaphore(f"loaded_b{i}")) for i in range(B_SLOTS)]
        free_b = [ctx.enter_context(nc.semaphore(f"free_b{i}")) for i in range(B_SLOTS)]
        layer_left = ctx.enter_context(nc.semaphore("layer_left"))
        counted = ctx.enter_context(nc.semaphore("counted"))
        layer_open = ctx.enter_context(nc.semaphore("layer_open"))
        held = ctx.enter_context(nc.semaphore("held"))
        first_angle_ready = ctx.enter_context(nc.semaphore("first_angle_ready"))
        first_constants = ctx.enter_context(nc.semaphore("first_constants"))
        first_decay_ready = ctx.enter_context(nc.semaphore("first_decay_ready"))
        first_dt_ready = ctx.enter_context(nc.semaphore("first_dt_ready"))
        first_dt_wide = ctx.enter_context(nc.semaphore("first_dt_wide"))
        first_dve_chain = ctx.enter_context(nc.semaphore("first_dve_chain"))
        first_half_sine = ctx.enter_context(nc.semaphore("first_half_sine"))
        first_params_loaded = ctx.enter_context(nc.semaphore("first_params_loaded"))
        first_params_turned = ctx.enter_context(nc.semaphore("first_params_turned"))
        first_pool_chain = ctx.enter_context(nc.semaphore("first_pool_chain"))
        first_positions_loaded = ctx.enter_context(nc.semaphore("first_positions_loaded"))
        first_result_ready = ctx.enter_context(nc.semaphore("first_result_ready"))
        first_rho_ready = ctx.enter_context(nc.semaphore("first_rho_ready"))
        first_stored = ctx.enter_context(nc.semaphore("first_stored"))
        first_theta_turned = ctx.enter_context(nc.semaphore("first_theta_turned"))
        first_x_loaded = ctx.enter_context(nc.semaphore("first_x_loaded"))
        per_layer = []

        def of_layer(name):
            per_layer.append(ctx.enter_context(nc.semaphore(name)))
            return per_layer[-1]

        gains_loaded = of_layer("gains_loaded")
        head_gains_loaded = of_layer("head_gains_loaded")
        b_loaded = of_layer("b_loaded")
        c_loaded = of_layer("c_loaded")
        d_loaded = of_layer("d_loaded")
        router_loaded = of_layer("router_loaded")
        dve_chain = of_layer("dve_chain")
        pool_chain = of_layer("pool_chain")
        squares = of_layer("squares")
        h_ready = of_layer("h_ready")
        hT_psum = of_layer("hT_psum")
        hT_sbuf = of_layer("hT_sbuf")
        u_psum = of_layer("u_psum")
        u_sbuf = of_layer("u_sbuf")
        qkv_psum = of_layer("qkv_psum")
        qkv_sbuf = of_layer("qkv_sbuf")
        lora_squares = of_layer("lora_squares")
        lora_ready = of_layer("lora_ready")
        loraT_psum = of_layer("loraT_psum")
        loraT_sbuf = of_layer("loraT_sbuf")
        q_psum = of_layer("q_psum")
        kv_psum = of_layer("kv_psum")
        q_sbuf = of_layer("q_sbuf")
        v_sbuf = of_layer("v_sbuf")
        k_sbuf = of_layer("k_sbuf")
        qk_squares = of_layer("qk_squares")
        qk_ready = of_layer("qk_ready")
        qkT_psum = of_layer("qkT_psum")
        qkT_sbuf = of_layer("qkT_sbuf")
        scores_psum = of_layer("scores_psum")
        probs_shifted = of_layer("probs_shifted")
        probs_exp = of_layer("probs_exp")
        probs_ready = of_layer("probs_ready")
        probsT_psum = of_layer("probsT_psum")
        probsT_sbuf = of_layer("probsT_sbuf")
        o_psum = of_layer("o_psum")
        o_sbuf = of_layer("o_sbuf")
        b_scaled = of_layer("b_scaled")
        ssm_wT_psum = of_layer("ssm_wT_psum")
        ssm_b_sbuf = of_layer("ssm_b_sbuf")
        ssm_c_sbuf = of_layer("ssm_c_sbuf")
        key_shared = of_layer("key_shared")
        table_ready = of_layer("table_ready")
        bu_psum = of_layer("bu_psum")
        modulated = of_layer("modulated")
        turned_back = of_layer("turned_back")
        y_used = of_layer("y_used")
        y_psum = of_layer("y_psum")
        gelu_arg = of_layer("gelu_arg")
        gelu_tanh = of_layer("gelu_tanh")
        gelu_ready = of_layer("gelu_ready")
        gates_psum = of_layer("gates_psum")
        gates_sbuf = of_layer("gates_sbuf")
        glu_psum = of_layer("glu_psum")
        glu_gate_tanh = of_layer("glu_gate_tanh")
        glu_read = of_layer("glu_read")
        attn_proj_psum = of_layer("attn_proj_psum")
        merged_ready = of_layer("merged_ready")
        mergedT_psum = of_layer("mergedT_psum")
        mergedT_sbuf = of_layer("mergedT_sbuf")
        out_psum = of_layer("out_psum")
        x_mixed = of_layer("x_mixed")
        squares2 = of_layer("squares2")
        h2_ready = of_layer("h2_ready")
        h2T_psum = of_layer("h2T_psum")
        h2T_sbuf = of_layer("h2T_sbuf")
        logits_psum = of_layer("logits_psum")
        expo_ready = of_layer("expo_ready")
        routes_ready = of_layer("routes_ready")
        picked = of_layer("picked")
        rank_psum = of_layer("rank_psum")
        perm_ready = of_layer("perm_ready")
        offsets_ready = of_layer("offsets_ready")
        sorted_psum = of_layer("sorted_psum")
        sorted_sbuf = of_layer("sorted_sbuf")
        residual_psum = of_layer("residual_psum")
        pair_copied = of_layer("pair_copied")
        hidden_psum = of_layer("hidden_psum")
        gate_tanh_ready = of_layer("gate_tanh_ready")
        hidden_half = of_layer("hidden_half")
        hidden_ready = of_layer("hidden_ready")
        sel_half = of_layer("sel_half")
        sel_ready = of_layer("sel_ready")
        turned_psum = of_layer("turned_psum")
        hiddenT_sbuf = of_layer("hiddenT_sbuf")
        selT_sbuf = of_layer("selT_sbuf")
        down_psum = of_layer("down_psum")
        down_sbuf_lo = of_layer("down_sbuf_lo")
        down_sbuf_hi = of_layer("down_sbuf_hi")
        moe_psum = of_layer("moe_psum")
        x_ready = of_layer("x_ready")
        rank_shifted = of_layer("rank_shifted")
        more_free = of_layer("more_free")
        more_loaded = of_layer("more_loaded")
        nums = [s.num for s in per_layer]
        assert nums == list(range(nums[0], nums[0] + len(nums))), nums
        x = sb("x", [P, TT, D])
        hT = sb("hT", [P, KC, SEQ])
        ringA = sb("ringA", [P, A_SLOTS, A_SIZE])
        ringB = sb("ringB", [P, B_SLOTS, B_SIZE])
        ident = sb("ident", [P, P])
        before = sb("before", [P, P])
        ones = sb("ones", [P, P])
        iota = sb("iota", [P, NPOS])
        own_group = sb("own_group", [P, 2 * GRP])
        amask = sb("amask", [P, SEQ])
        cossin = sb("cossin", [P, 2, 2 * STILES + TT * HALF])
        rope = cossin[:, :, 2 * STILES:].rearrange("p i (t f) -> p i t f", t=TT)
        inv_freq = sb("inv_freq", [P, HALF])
        ssm_par = sb("ssm_par", [P, DEPTH, 3, STILES])
        ssm_now = sb("ssm_now", [P, 3, STILES])
        turn_lo = sb("turn_lo", [P, DEPTH, 2, STILES, 16])
        turn_hi = sb("turn_hi", [P, DEPTH, 2, STILES, 16])
        bT = sb("bT", [P, 2, CH_T, P])
        cT = sb("cT", [P, 3, CH_T, P])
        gains = sb("gains", [P, 2 * KC + QC + KVC])
        g_mix, g_ffn = gains[:, 0:KC], gains[:, KC:2 * KC]
        g_q, g_kv = gains[:, 2 * KC:2 * KC + QC], gains[:, 2 * KC + QC:]
        dskip = sb("dskip", [P, CH_T])
        wroute = sb("wroute", [P, KC, ROUTE])
        head_gain = sb("head_gain", [P, 2, QKD])
        norm = sb("norm", [P, 8, 32])

        ARENA = 21312
        arena = sb("arena", [P, ARENA])

        def at(lo, *shape):
            n = int(np.prod(shape))
            assert lo + n <= ARENA
            ap = arena[:, lo:lo + n]
            names = "abcd"[:len(shape)]
            if len(shape) > 1:
                ap = ap.rearrange(f"p ({' '.join(names)}) -> p {' '.join(names)}", **dict(zip(names, shape)))
            return ap

        gate_t = at(0, TT, 2 * D)
        uT = at(4096, CH_T, SEQ)
        qkv = at(5120, TT, U0)
        vtok = at(6464, TT, HEADS, VD)
        oT = at(5120, HEADS // 2, SEQ)
        tab_v = at(7488, 2, SEQ)
        garg = at(8000, SEQ)
        gtmp = at(8256, SEQ)
        turn = at(8512, 2, 2, SEQ)
        mulc = at(9536, 2, SEQ)
        muls = at(10048, 2, SEQ)
        driven = at(10560, 2, SEQ)
        state = at(11072, 2, SEQ)
        tab_u = at(11584, 2, SEQ)
        backc = at(12096, 2, 2, SEQ)
        backs = at(13120, 2, 2, SEQ)
        turn_tmp = at(20288, 4, DEPTH, STILES, 8)
        praw = at(17216, 3, P)
        dtraw = at(17600, 2)
        ppar = at(17604, 3, DEPTH * STILES)
        pang = at(17700, 4, 2 * STILES + TT * HALF)
        pwork = at(17956, 8, DEPTH * STILES)
        pos_f = at(18212, TT)
        braw = at(8512, 2, STILES, GRP)
        bbar = at(9024, 2, STILES, GRP)
        btmp = at(9536, 2, STILES, GRP)
        bwide = at(10048, 2, STILES, 2 * GRP)
        craw = at(12096, 2, CH_T, 2, NST)
        h = at(14144, TT, D)
        qk = at(14144, TT, 2 * HEADS, QKD)
        qkT = at(17216, 2, 4, SEQ)
        lora = at(17216, TT, U0)
        loraT = at(18560, QC + KVC, SEQ)
        sq = at(17216, TT, 2 * HEADS, QKD)
        probs = at(19264, 4, SEQ)
        probsT = at(20288, 4, 2, P)
        glu_t = at(14144, TT, D)
        merged = at(16192, TT, D)
        attn_m = at(18240, D)
        h2 = at(14144, TT, D)
        sortedT = at(0, KC, NPOS + SLOT)
        pairT = at(4608, 2, KC, 2 * SLOT)
        gtanh = at(6656, 2, DE)
        hidden = at(7168, 2, DE)
        hiddenT = at(7680, 2, P)
        sel = at(7936, 2, TT, 2 * SLOT)
        selT = at(8448, 2, SEQ)
        down = at(8960, D)
        perm = at(9984, TT, NPOS)
        rt = at(11008, 24, TT, NE)
        roff = sb("roff", [P, PASSES, NE], I32)
        rmany = sb("rmany", [P, DEPTH], I32)
        pos_i = sb("pos_i", [P, TT], I32)
        logits = at(12544, TT, ROUTE)
        expo_in = at(12624, TT, EG + 1)
        expo = at(12640, TT, EG + 1)
        r8 = at(12656, 10, TT, EPG)
        r4 = at(12816, 4, TT, EG)
        r1 = at(12848, 16, TT)
        count = at(12880, 3, NE)

        psum = ctx.enter_context(nc.psum_tensor("psum", [P, 8, 512], F32))

        def bank(i, lo=0, hi=512):
            return psum[:, i, lo:hi]

        def banks(i, n):
            return psum[:, i:i + n, :].rearrange("p b n -> p (b n)")

        w_in = t["w_in"].rearrange("l (p c) n -> l p c n", c=KC)
        w_uq = t["w_uq"].rearrange("l (p c) n -> l p c n", c=QC)
        w_ukv = t["w_ukv"].rearrange("l (p c) n -> l p c n", c=KVC)
        w_ap = t["w_attn_proj"].rearrange("l (c p) n -> l p c n", p=P)
        w_glu = t["w_glu"].rearrange("l (c p) n -> l p c n", p=P)
        w_out = t["w_out"].rearrange("l (p c) n -> l p c n", c=KC)
        w_gate = t["w_exp_gate"].rearrange("l e (p c) n -> (l e) p (c n)", c=KC)
        w_up = t["w_exp_up"].rearrange("l e (p c) n -> (l e) p (c n)", c=KC)
        w_down = t["w_exp_down"].rearrange("l e (p c) n -> (l e) p (c n)", c=2)

        def layer_of(ap, l):
            ap = ap[bass.ds(l, 1)]
            names = " ".join("bcdef"[:ap.ndim - 1])
            first_, rest = names.split(" ", 1) if " " in names else (names, "")
            return ap.rearrange(f"a {names} -> (a {first_}) {rest}")

        def slotA(a):
            return ringA[:, a % A_SLOTS, :]

        def slotA_kc(a):
            return slotA(a).rearrange("p (c n) -> p c n", c=KC)

        wtail = slotA(A_TAIL)[:, 0:KC * (U0 - 512)].rearrange("p (c n) -> p c n", c=KC)
        wuq = slotA(A_TAIL)[:, KC * (U0 - 512):KC * (U0 - 512) + QC * HEADS * QKD].rearrange("p (c n) -> p c n", c=QC)
        wukv = ringB[:, 0, :].rearrange("p (c n) -> p c n", c=KVC)

        def b_use(l, s, it):
            per = NE // B_SLOTS
            return l * (per + 1) + it + 1 if s == 0 else l * per + it

        def leave_layer(eng, l, clears=False):
            eng.drain().then_inc(layer_left, 1)
            if clears:
                eng.wait_ge(layer_left, l * 4 + 4)
                eng.sem_inc(held, 1)
                eng.sem_clear(range(nums[0], nums[-1] + 1))
                eng.drain().then_inc(layer_open, 1)
            eng.wait_ge(layer_open, l + 1)
            eng.sem_inc(held, 1)

        def crowded(eng, l):
            eng.wait_ge(counted, l + 1)
            eng.sem_inc(held, 1)
            return eng.value_load(rmany[0:1, bass.ds(l, 1)], min_val=0, max_val=1)

        def further_steps(eng, step, each_pass=None):
            with eng.Fori(1, PASSES) as r:
                if each_pass:
                    each_pass(r)
                with eng.Fori(0, NPAIR) as pair:
                    step(r * NPAIR + pair, pair, r)

        block = ctx.enter_context(nc.Block())

        @block.sync
        def _(sp):
            for tt in range(TT):
                sp.dma_start(x[:, tt, :], t["x"][0, tt * P:(tt + 1) * P, :]).then_inc(first_x_loaded, 16)
            with sp.Fori(0, DEPTH) as l:
                use = sp.snap(l * A_USES)
                layer_at = {k: layer_of(v, l) for k, v in (("in", w_in), ("uq", w_uq), ("ukv", w_ukv),
                                                           ("ap", w_ap), ("glu", w_glu), ("out", w_out))}

                def load_a(a, dst0, src0, dst1, src1):
                    s = a % A_SLOTS
                    sp.wait_ge(free_a[s], use + a // A_SLOTS + 1)
                    sp.sem_inc(held, 1)
                    sp.dma_start(dst0, src0).then_inc(loaded_a[s], 16)
                    sp.dma_start(dst1, src1).then_inc(loaded_a[s], 16)

                def load_a_cols(a, w, c0):
                    v = slotA_kc(a)
                    load_a(a, v[:, 0:KC // 2, :], w[:, 0:KC // 2, c0:c0 + 512],
                           v[:, KC // 2:KC, :], w[:, KC // 2:KC, c0:c0 + 512])

                load_a_cols(A_U, layer_at["in"], U0)
                load_a_cols(A_Q, layer_at["in"], 0)
                load_a(A_TAIL, wtail, layer_at["in"][:, :, 512:U0], wuq, layer_at["uq"])
                sp.wait_ge(free_b[0], l * (NE // B_SLOTS + 1) + 1)
                sp.sem_inc(held, 1)
                sp.dma_start(wukv, layer_at["ukv"]).then_inc(loaded_b[0], 16)
                for g in range(4):
                    load_a_cols(A_G + g, layer_at["in"], G0 + g * 512)
                for g in range(2):
                    v = slotA(A_GLU + g).rearrange("p (c n) -> p c n", c=CH_T)
                    src = layer_at["glu"][:, :, g * D:(g + 1) * D]
                    load_a(A_GLU + g, v[:, 0:2, :], src[:, 0:2, :], v[:, 2:4, :], src[:, 2:4, :])
                v = slotA(A_AP).rearrange("p (c n) -> p c n", c=CH_T)
                load_a(A_AP, v[:, 0:2, :], layer_at["ap"][:, 0:2, :], v[:, 2:4, :], layer_at["ap"][:, 2:4, :])
                for g in range(2):
                    load_a_cols(A_OUT + g, layer_at["out"], g * 512)

                with sp.Fori(0, NE // A_SLOTS) as it:
                    e0 = sp.snap(l * NE + it * A_SLOTS)
                    for s in range(A_SLOTS):
                        src = [w[bass.ds(e0 + s, 1)].rearrange("a p n -> (a p) n") for w in (w_gate, w_up, w_down)]
                        sp.wait_ge(free_a[s], l * A_USES + A_MIX // A_SLOTS + it + 1)
                        sp.sem_inc(held, 1)
                        sp.dma_start(ringA[:, s, 0:2048], src[0]).then_inc(loaded_a[s], 16)
                        sp.dma_start(ringA[:, s, 2048:4096], src[1]).then_inc(loaded_a[s], 16)
                        sp.wait_ge(free_b[s], b_use(l, s, it) + 1)
                        sp.sem_inc(held, 1)
                        sp.dma_start(ringB[:, s, :], src[2]).then_inc(loaded_b[s], 16)

                def reload(p, pair, r):
                    sp.wait_ge(more_free, p - (NPAIR - 1))
                    sp.sem_inc(held, 1)
                    e0 = sp.snap(l * NE + pair * 2)
                    for s in range(2):
                        src = [w[bass.ds(e0 + s, 1)].rearrange("a p n -> (a p) n") for w in (w_gate, w_up, w_down)]
                        sp.dma_start(ringA[:, s, 0:2048], src[0]).then_inc(more_loaded, 16)
                        sp.dma_start(ringA[:, s, 2048:4096], src[1]).then_inc(more_loaded, 16)
                        sp.dma_start(ringB[:, s, :], src[2]).then_inc(more_loaded, 16)

                with sp.If(crowded(sp, l) > 0):
                    further_steps(sp, reload)
                    sp.wait_ge(layer_open, l + 1)
                    sp.sem_inc(held, 1)
            for tt in range(TT):
                sp.wait_ge(first_result_ready, tt + 1)
                sp.dma_start(out[0, tt * P:(tt + 1) * P, :], x[:, tt, :]).then_inc(first_stored, 16)
            sp.wait_ge(first_stored, 16 * TT)

        @block.gpsimd
        def _(pool):
            c = first_constants
            pool.memset(ident[:, :], 0.0).then_inc(c, 1)
            pool.memset(before[:, :], 1.0).then_inc(c, 1)
            pool.memset(ones[:, :], 1.0).then_inc(c, 1)
            pool.memset(own_group[:, :], 1.0).then_inc(c, 1)
            pool.memset(amask[:, :], 0.0).then_inc(c, 1)
            for j in range(HALF):
                pool.memset(inv_freq[:, j:j + 1], float(np.float32(THETA) ** np.float32(-j / HALF))).then_inc(c, 1)
            pool.iota(iota[:, :], pattern=[[1, NPOS]], base=0, channel_multiplier=0,
                      allow_small_or_imprecise_dtypes=True).then_inc(c, 1)
            n = 6 + HALF
            pool.wait_ge(c, n)
            pool.affine_select(out=ident[:, :], in_=ident[:, :], compare_op=ALU.not_equal, fill=1.0, base=0,
                               pattern=[[-1, P]], channel_multiplier=1).then_inc(c, 1)
            pool.affine_select(out=before[:, :], in_=before[:, :], compare_op=ALU.is_gt, fill=0.0, base=0,
                               pattern=[[1, P]], channel_multiplier=-1).then_inc(c, 1)
            pool.affine_select(out=own_group[:, 0:GRP], in_=own_group[:, 0:GRP], compare_op=ALU.is_ge, fill=0.0,
                               base=NST - 1, pattern=[[0, GRP]], channel_multiplier=-1).then_inc(c, 1)
            pool.affine_select(out=own_group[:, GRP:], in_=own_group[:, GRP:], compare_op=ALU.is_ge, fill=0.0,
                               base=-NST, pattern=[[0, GRP]], channel_multiplier=1).then_inc(c, 1)
            pool.affine_select(out=amask[:, SEQ - CHUNK:], in_=amask[:, SEQ - CHUNK:], compare_op=ALU.is_ge,
                               fill=MASKED, base=-CHUNK, pattern=[[0, CHUNK]], channel_multiplier=1).then_inc(c, 1)

            done = Count()

            def shape(ap, n):
                return ap if n == 1 else ap.broadcast_to([P, DEPTH, STILES, n])

            def cmul(oc, os, a, b, n):
                tmp = [turn_tmp[:, i, :, :, 0:n] for i in range(4)]
                bcs = [shape(v, n) for v in b]
                pool.tensor_tensor(tmp[0], a[0], bcs[0], ALU.mult).then_inc(first_pool_chain, done.add())
                pool.tensor_tensor(tmp[1], a[1], bcs[1], ALU.mult).then_inc(first_pool_chain, done.add())
                pool.tensor_tensor(tmp[2], a[0], bcs[1], ALU.mult).then_inc(first_pool_chain, done.add())
                pool.tensor_tensor(tmp[3], a[1], bcs[0], ALU.mult).then_inc(first_pool_chain, done.add())
                pool.wait_ge(first_pool_chain, done.n)
                pool.tensor_tensor(oc, tmp[0], tmp[1], ALU.subtract).then_inc(first_pool_chain, done.add())
                pool.tensor_tensor(os, tmp[2], tmp[3], ALU.add).then_inc(first_pool_chain, done.add())
                pool.wait_ge(first_pool_chain, done.n)

            def parts(tab, b0, b1):
                return [tab[:, :, i, :, b0:b1] for i in range(2)]

            pool.wait_ge(first_theta_turned, 2)
            for tab in (turn_lo, turn_hi):
                for i in range(2):
                    pool.memset(tab[:, :, i, :, 0:1], 1.0 - i).then_inc(first_pool_chain, done.add())
            for i in range(2):
                pool.tensor_copy(turn_lo[:, :, i, :, 1:2], cossin[:, i, 0:2 * STILES].rearrange("p (l j o) -> p l j o", l=DEPTH, o=1)).then_inc(first_pool_chain, done.add())
            pool.wait_ge(first_pool_chain, done.n)
            for k, tab in enumerate((turn_lo, turn_hi)):
                for n in (2, 4, 8):
                    oc, os = parts(tab, n, n + 1)
                    cmul(oc, os, parts(tab, n // 2, n // 2 + 1), parts(tab, n // 2, n // 2 + 1), 1)
                    oc, os = parts(tab, n + 1, 2 * n)
                    cmul(oc, os, parts(tab, 1, n), parts(tab, n, n + 1), n - 1)
                if k == 0:
                    oc, os = parts(turn_hi, 1, 2)
                    cmul(oc, os, parts(tab, 8, 9), parts(tab, 8, 9), 1)

            with pool.Fori(0, DEPTH) as l:
                done = Count()

                lo = turn_lo[:, bass.ds(l, 1)].rearrange("p l i j b -> p (l i) j b")
                hi = turn_hi[:, bass.ds(l, 1)].rearrange("p l i j b -> p (l i) j b")
                for j in range(STILES):
                    if j == 0:
                        pool.wait_ge(ssm_wT_psum, 4)
                    if j >= 2:
                        pool.wait_ge(turned_back, j - 1)
                    a = bc(hi[:, :, j, :], 3, 16)
                    for k, dst in enumerate((tab_u, tab_v)):
                        b = bc(bc(lo[:, k, j, :], 1, 16), 1, 2)
                        pool.tensor_tensor(dst.rearrange("p i (a b) -> p i a b", b=16), a, b, ALU.mult).then_inc(pool_chain, done.add())
                    pool.wait_ge(pool_chain, done.n)
                    pool.tensor_tensor(turn[:, j % 2, 0, :], tab_u[:, 0, :], tab_v[:, 1, :],
                                       ALU.subtract).then_inc(table_ready, 1)
                    pool.tensor_tensor(turn[:, j % 2, 1, :], tab_u[:, 1, :], tab_v[:, 0, :],
                                       ALU.add).then_inc(table_ready, 1)
                    pool.wait_ge(table_ready, 2 * j + 2)

                pool.wait_ge(offsets_ready, 1)
                pool.wait_ge(sorted_sbuf, KC)

                def copy_pair(p, par, first_uses):
                    for i in range(2):
                        off = pool.value_load(roff[0:1, 0, bass.ds(p * 2 + i, 1)], min_val=0, max_val=NPOS)
                        if i == 0 and not first_uses:
                            pool.wait_ge(hidden_psum, p - 1)
                            pool.sem_inc(held, 1)
                        last = pool.tensor_copy(pairT[:, par, :, i * SLOT:(i + 1) * SLOT], sortedT[:, :, bass.ds(off, SLOT)])
                        last.then_inc(pair_copied, 1)

                for p in range(2):
                    copy_pair(p, p, True)
                with pool.Fori(1, NPAIR // 2) as i:
                    for par in range(2):
                        copy_pair(i * 2 + par, par, False)

                def copy_more(p, pair, r):
                    pool.wait_ge(x_ready, (p - (NPAIR - 1)) * TT)
                    pool.sem_inc(held, 1)
                    for i in range(2):
                        off = pool.value_load(roff[0:1, bass.ds(r, 1), bass.ds(pair * 2 + i, 1)], min_val=0, max_val=NPOS)
                        pool.tensor_copy(pairT[:, 0, :, i * SLOT:(i + 1) * SLOT],
                                         sortedT[:, :, bass.ds(off, SLOT)]).then_inc(pair_copied, 1)

                with pool.If(crowded(pool, l) > 0):
                    further_steps(pool, copy_more)
                leave_layer(pool, l, clears=True)

        @block.scalar
        def _(act):
            act.dma_start(praw[0:2 * STILES, 0, :], t["lam_re"].rearrange("l (j g) p -> (l j) (g p)", g=2)).then_inc(first_params_loaded, 16)
            act.dma_start(praw[0:2 * STILES, 1, :], t["lam_im"].rearrange("l (j g) p -> (l j) (g p)", g=2)).then_inc(first_params_loaded, 16)
            act.dma_start(dtraw[0:2 * STILES, :], t["log_dt"].rearrange("l (j g) -> (l j) g", g=2)).then_inc(first_params_loaded, 16)
            act.dma_start(pos_i[:, :], t["positions"].rearrange("b (t p) -> p (b t)", p=P),
                          allow_slow_non_contiguous=True).then_inc(first_positions_loaded, 16)
            act.wait_ge(first_params_loaded, 48)
            act.activation(dtraw[0:2 * STILES, :], dtraw[0:2 * STILES, :], ACT.Exp).then_inc(first_dt_ready, 1)
            act.wait_ge(first_decay_ready, 1)
            act.activation(pwork[:, 0, :], pwork[:, 1, :], ACT.Exp).then_inc(first_rho_ready, 1)
            act.wait_ge(first_angle_ready, 1)
            act.activation(cossin[:, 1, :], pang[:, 0, :], ACT.Sin).then_inc(first_theta_turned, 1)
            act.activation(pang[:, 3, :], pang[:, 0, :], ACT.Sin, scale=0.5).then_inc(first_half_sine, 1)

            with act.Fori(0, DEPTH) as l:
                def vec(ap, cc):
                    return ap[bass.ds(l, 1), :].rearrange("a (p c) -> (a p) c", c=cc)

                act.dma_start(g_mix, vec(t["norm_mix_g"], KC)).then_inc(gains_loaded, 16)
                act.dma_start(g_ffn, vec(t["norm_ffn_g"], KC)).then_inc(gains_loaded, 16)
                act.dma_start(g_q, vec(t["q_lora_g"], QC)).then_inc(gains_loaded, 16)
                act.dma_start(g_kv, vec(t["kv_lora_g"], KVC)).then_inc(gains_loaded, 16)
                for i, k in enumerate(("b_re", "b_im")):
                    act.dma_start(braw[:, i, :, :], layer_of(t[k], l).rearrange("(j g) p i -> (g p) j i", g=2)).then_inc(b_loaded, 16)
                for i, k in enumerate(("c_re", "c_im")):
                    for half in range(2):
                        act.dma_start(craw[:, i, :, half, :], layer_of(t[k], l).rearrange("(m g) i p -> (g i) m p", m=CH_T)).then_inc(c_loaded, 16)
                act.dma_start(dskip[:, :], layer_of(t["d_skip"], l).rearrange("(m g) i -> (g i) m", m=CH_T), allow_slow_non_contiguous=True).then_inc(d_loaded, 16)
                for i, k in enumerate(("q_head_g", "k_head_g")):
                    act.dma_start(head_gain[:, i, :], t[k][bass.ds(l, 1), :].broadcast_to([P, QKD])).then_inc(head_gains_loaded, 16)
                act.dma_start(wroute[:, :, 0:EG], layer_of(t["w_router_group"], l).rearrange("(p c) n -> p c n", c=KC)).then_inc(router_loaded, 16)
                act.dma_start(wroute[:, :, EG:], layer_of(t["w_router_expert"], l).rearrange("(p c) n -> p c n", c=KC)).then_inc(router_loaded, 16)

                act.wait_ge(first_x_loaded, 16 * TT)
                for tt in range(TT):
                    act.activation(h[:, tt, :], x[:, tt, :], ACT.Square, accum_out=norm[:, 0, tt:tt + 1]).then_inc(squares, 1)
                act.wait_ge(gains_loaded, 64)
                for c in range(KC):
                    act.wait_ge(hT_psum, c // 2 + 1)
                    act.activation(hT[:, c, :], bank(c // 2 % 2, c % 2 * SEQ, c % 2 * SEQ + SEQ), ACT.Copy,
                                   scale=g_mix[:, c:c + 1]).then_inc(hT_sbuf, 1)
                for m in range(CH_T):
                    act.wait_ge(u_psum, m + 1)
                    act.activation(uT[:, m, :], bank(2 + m, 0, SEQ), ACT.Copy).then_inc(u_sbuf, 1)
                for i in range(2):
                    act.wait_ge(ssm_wT_psum, i + 1)
                    act.activation(bT[:, i, :, :], bank(2 + i).rearrange("p (m s) -> p m s", m=CH_T), ACT.Copy).then_inc(ssm_b_sbuf, 1)

                def lora_norm():
                    for tt in range(TT):
                        act.wait_ge(qkv_sbuf, 2 * tt + 2)
                        act.activation(lora[:, tt, 0:QR], qkv[:, tt, 0:QR], ACT.Square, accum_out=norm[:, 2, tt:tt + 1]).then_inc(lora_squares, 1)
                        act.activation(lora[:, tt, QR:QR + KVR], qkv[:, tt, QR:QR + KVR], ACT.Square, accum_out=norm[:, 3, tt:tt + 1]).then_inc(lora_squares, 1)

                def lora_turn():
                    for c in range(QC + KVC):
                        act.wait_ge(loraT_psum, c + 1)
                        g = g_q[:, c:c + 1] if c < QC else g_kv[:, c - QC:c - QC + 1]
                        act.activation(loraT[:, c, :], bank(6 + c % 2, 0, SEQ), ACT.Copy, scale=g).then_inc(loraT_sbuf, 1)

                def q_out(tt):
                    act.wait_ge(q_psum, tt + 1)
                    for i in range(2):
                        act.activation(qk[:, tt, 4 * i:4 * i + 4, :], bank(6 + i, 0, 4 * QKD).rearrange("p (h d) -> p h d", h=4),
                                       ACT.Copy).then_inc(q_sbuf, 1)

                def kv_out(tt):
                    act.wait_ge(kv_psum, tt + 1)
                    for i in range(2):
                        src = bank(6 + i).rearrange("p (h d) -> p h d", h=4)
                        act.activation(qk[:, tt, HEADS + 4 * i:HEADS + 4 * i + 4, 0:NOPE], src[:, :, 0:NOPE], ACT.Copy).then_inc(k_sbuf, 1)
                        act.activation(vtok[:, tt, 4 * i:4 * i + 4, :], src[:, :, NOPE:], ACT.Copy).then_inc(v_sbuf, 1)

                def qk_square():
                    act.wait_ge(k_sbuf, 4)
                    act.wait_ge(key_shared, TT)
                    act.wait_ge(q_sbuf, 4)
                    for tt in range(TT):
                        act.activation(sq[:, tt, :, :], qk[:, tt, :, :], ACT.Square).then_inc(qk_squares, 1)

                def qkT_out(hg):
                    for i in range(4):
                        n = 4 * hg + i
                        act.wait_ge(qkT_psum, n + 1)
                        act.activation(qkT[0:QKD, i // 2, 2 * (i % 2):2 * (i % 2) + 2, :],
                                       psum[0:QKD, 6 + i % 2, :].rearrange("p (h s) -> p h s", h=2), ACT.Copy).then_inc(qkT_sbuf, 1)

                def exps(c, qb):
                    act.wait_ge(probs_shifted, c + 1)
                    w = P * (qb + 1)
                    act.activation(probs[:, :, 0:w], probs[:, :, 0:w], ACT.Exp).then_inc(probs_exp, 1)

                def probsT_out(c, qb):
                    act.wait_ge(probsT_psum, c + 1)
                    act.activation(probsT[:, :, 0:qb + 1, :],
                                   banks(6, 2)[:, 0:4 * (qb + 1) * P].rearrange("p (h k q) -> p h k q", h=4, k=qb + 1),
                                   ACT.Copy).then_inc(probsT_sbuf, 1)

                def o_out(c, hg, qb):
                    act.wait_ge(o_psum, c + 1)
                    act.activation(oT[:, 2 * hg:2 * hg + 2, qb * P:(qb + 1) * P],
                                   bank(5, 0, 2 * P).rearrange("p (c q) -> p c q", c=2), ACT.Copy).then_inc(o_sbuf, 1)

                def gate(g):
                    act.wait_ge(gates_psum, g + 1)
                    act.activation(gate_t[:, g % 2, (g // 2) * 512:(g // 2 + 1) * 512], bank(4), ACT.Tanh, scale=0.5).then_inc(gates_sbuf, 1)

                def gelu(m):
                    act.wait_ge(gelu_arg, m + 1)
                    act.activation(gtmp, garg, ACT.Tanh, scale=math.sqrt(2.0 / math.pi)).then_inc(gelu_tanh, 1)

                for j in range(STILES):
                    attention(j, dict(lora=lambda: (lora_norm(), lora_turn()), q=lambda: (q_out(0), q_out(1)),
                                      kv=lambda: (kv_out(0), kv_out(1)), qk=qk_square, turn=qkT_out,
                                      scores=lambda c, hg, qb: exps(c, qb), probs=lambda c, hg, qb: probsT_out(c, qb),
                                      values=o_out))
                    if j % 2 == 0:
                        gate(j // 2)
                    if j % QPT == 0 and j:
                        gelu(j // QPT - 1)
                gelu(CH_T - 1)

                for tt in range(TT):
                    act.wait_ge(glu_psum, 1 + 2 * tt)
                    act.activation(glu_t[:, tt, :], banks(2 + 2 * tt, 2), ACT.Tanh, scale=0.25).then_inc(glu_gate_tanh, 1)
                for tt in range(TT):
                    for i in range(2):
                        act.wait_ge(mergedT_psum, 2 * tt + i + 1)
                        act.activation(hT[:, 4 * i:4 * i + 4, tt * P:(tt + 1) * P],
                                       bank(4 + 2 * tt + i).rearrange("p (c s) -> p c s", c=4), ACT.Copy).then_inc(mergedT_sbuf, 1)

                for tt in range(TT):
                    act.wait_ge(x_mixed, tt + 1)
                    act.activation(h2[:, tt, :], x[:, tt, :], ACT.Square, accum_out=norm[:, 1, tt:tt + 1]).then_inc(squares2, 1)
                for c in range(KC):
                    act.wait_ge(h2T_psum, c // 2 + 1)
                    act.activation(hT[:, c, :], bank(4 + c // 2, c % 2 * SEQ, c % 2 * SEQ + SEQ), ACT.Copy,
                                   scale=g_ffn[:, c:c + 1]).then_inc(h2T_sbuf, 1)
                act.wait_ge(picked, 1)
                act.activation(expo, expo_in, ACT.Exp).then_inc(expo_ready, 1)
                for c in range(KC):
                    act.wait_ge(sorted_psum, c + 1)
                    act.activation(sortedT[:, c, 0:NPOS], bank(c % 4), ACT.Copy, scale=g_ffn[:, c:c + 1]).then_inc(sorted_sbuf, 1)

                def gate_tanh(p, par):
                    act.wait_ge(hidden_psum, p + 1)
                    act.sem_inc(held, 1)
                    act.activation(gtanh[:, par, :], bank(par, 0, DE), ACT.Tanh, scale=0.5).then_inc(gate_tanh_ready, 1)

                def turned(p, par):
                    act.wait_ge(turned_psum, p + 1)
                    act.sem_inc(held, 1)
                    act.activation(hiddenT[:, :, :], bank(par, 0, 2 * P).rearrange("p (c s) -> p c s", c=2), ACT.Copy).then_inc(hiddenT_sbuf, 1)

                def down_lo(p):
                    act.wait_ge(down_psum, p + 1)
                    act.sem_inc(held, 1)
                    act.activation(down[:, 0:512], bank(2), ACT.Copy).then_inc(down_sbuf_lo, 1)

                gate_tanh(0, 0)

                def step(p, par, last=False):
                    turned(p, par)
                    down_lo(p)
                    if not last:
                        gate_tanh(p + 1, 1 - par)

                with act.Fori(0, NPAIR // 2 - 1) as i:
                    for par in range(2):
                        step(i * 2 + par, par)
                step(NPAIR - 2, 0)
                step(NPAIR - 1, 1, last=True)

                def more(p, pair, r):
                    gate_tanh(p, 0)
                    turned(p, 0)
                    down_lo(p)

                with act.If(crowded(act, l) > 0):
                    further_steps(act, more)
                leave_layer(act, l)

        @block.vector
        def _(dve):
            TS, TTN, STT = dve.tensor_scalar, dve.tensor_tensor, dve.scalar_tensor_tensor

            def rsqrt(done, dst, src, scale, w):
                v, y, a = src[3], src[4], src[5]
                TS(v, src[0], scale, EPS, ALU.mult, ALU.add).then_inc(dve_chain, done.add())
                dve.wait_ge(dve_chain, done.n)
                TS(y.bitcast(I32), v.bitcast(I32), 1, None, ALU.logical_shift_right).then_inc(dve_chain, done.add())
                dve.wait_ge(dve_chain, done.n)
                TS(a.bitcast(I32), y.bitcast(I32), -1.0, float(0x5F3759DF), ALU.mult, ALU.add).then_inc(dve_chain, done.add())
                dve.wait_ge(dve_chain, done.n)
                y, a = a, y
                for k in range(4):
                    TTN(a, y, y, ALU.mult).then_inc(dve_chain, done.add())
                    dve.wait_ge(dve_chain, done.n)
                    TTN(a, a, v, ALU.mult).then_inc(dve_chain, done.add())
                    dve.wait_ge(dve_chain, done.n)
                    TS(a, a, -0.5, 1.5, ALU.mult, ALU.add).then_inc(dve_chain, done.add())
                    dve.wait_ge(dve_chain, done.n)
                    TTN(dst if k == 3 else y, y, a, ALU.mult).then_inc(dve_chain, done.add())
                    dve.wait_ge(dve_chain, done.n)

            done = Count()
            NW = DEPTH * STILES
            dtx = praw[0:NW, 2, :].rearrange("p (g s) -> p g s", g=2)
            dve.wait_ge(first_dt_ready, 1)
            dve.tensor_copy(dtx, bc(dtraw[0:NW, :], 2, NST)).then_inc(first_dt_wide, 1)
            dve.wait_ge(first_params_turned, 1)
            dve.tensor_copy(ppar[:, :, :], bank(7, 0, 3 * NW).rearrange("p (i w) -> p i w", i=3)).then_inc(first_dve_chain, done.add())
            dve.wait_ge(first_dve_chain, done.n)
            re, im, dt = (ppar[:, i, :] for i in range(3))
            TTN(pwork[:, 1, :], re, dt, ALU.mult).then_inc(first_decay_ready, 1)
            TTN(pang[:, 1, 0:NW], im, dt, ALU.mult).then_inc(first_dve_chain, done.add())
            dve.wait_ge(first_positions_loaded, 16)
            dve.tensor_copy(pos_f, pos_i[:, :]).then_inc(first_dve_chain, done.add())
            dve.wait_ge(first_dve_chain, done.n)
            dve.wait_ge(first_constants, 6 + HALF + 5)
            TTN(pang[:, 1, NW:].rearrange("p (t f) -> p t f", t=TT), bc(pos_f, 2, HALF), bc(inv_freq[:, :], 1, TT), ALU.mult).then_inc(first_dve_chain, done.add())
            dve.wait_ge(first_dve_chain, done.n)
            ang, whole, r = pang[:, 1, :], pang[:, 2, :], pang[:, 0, :]
            TS(whole, ang, 1.0 / TWO_PI, ROUND, ALU.mult, ALU.add).then_inc(first_dve_chain, done.add())
            dve.wait_ge(first_dve_chain, done.n)
            TS(whole, whole, ROUND, None, ALU.subtract).then_inc(first_dve_chain, done.add())
            dve.wait_ge(first_dve_chain, done.n)
            src = ang
            for part in split_two_pi():
                STT(out=r, in0=whole, scalar=-part, in1=src, op0=ALU.mult, op1=ALU.add).then_inc(first_dve_chain, done.add())
                dve.wait_ge(first_dve_chain, done.n)
                src = r
            pi = float(np.nextafter(np.float32(math.pi), np.float32(0)))
            TS(r, r, pi, -pi, ALU.min, ALU.max).then_inc(first_angle_ready, 1)
            dve.wait_ge(first_half_sine, 1)
            TTN(pang[:, 2, :], pang[:, 3, :], pang[:, 3, :], ALU.mult).then_inc(first_dve_chain, done.add())
            dve.wait_ge(first_dve_chain, done.n)
            TS(cossin[:, 0, :], pang[:, 2, :], -2.0, 1.0, ALU.mult, ALU.add).then_inc(first_theta_turned, 1)
            dve.wait_ge(first_theta_turned, 2)
            dve.wait_ge(first_rho_ready, 1)
            rho = pwork[:, 0, :]
            lr, li, den, t0, t1 = (pwork[:, i, :] for i in range(2, 7))

            def par_of(i):
                return ssm_par[:, :, i, :]

            def lj(ap):
                return ap.rearrange("p (l j) -> p l j", l=DEPTH)

            dve.tensor_copy(par_of(0), lj(rho)).then_inc(first_dve_chain, done.add())
            TTN(lr, rho, cossin[:, 0, 0:NW], ALU.mult).then_inc(first_dve_chain, done.add())
            TTN(li, rho, cossin[:, 1, 0:NW], ALU.mult).then_inc(first_dve_chain, done.add())
            TTN(t0, re, re, ALU.mult).then_inc(first_dve_chain, done.add())
            TTN(t1, im, im, ALU.mult).then_inc(first_dve_chain, done.add())
            dve.wait_ge(first_dve_chain, done.n)
            TTN(den, t0, t1, ALU.add).then_inc(first_dve_chain, done.add())
            TS(lr, lr, 1.0, None, ALU.subtract).then_inc(first_dve_chain, done.add())
            dve.wait_ge(first_dve_chain, done.n)
            dve.reciprocal(den, den).then_inc(first_dve_chain, done.add())
            TTN(t0, lr, re, ALU.mult).then_inc(first_dve_chain, done.add())
            TTN(t1, li, im, ALU.mult).then_inc(first_dve_chain, done.add())
            dve.wait_ge(first_dve_chain, done.n)
            TTN(t0, t0, t1, ALU.add).then_inc(first_dve_chain, done.add())
            dve.wait_ge(first_dve_chain, done.n)
            TTN(par_of(1), lj(t0), lj(den), ALU.mult).then_inc(first_dve_chain, done.add())
            dve.wait_ge(first_dve_chain, done.n)
            TTN(t0, li, re, ALU.mult).then_inc(first_dve_chain, done.add())
            TTN(t1, lr, im, ALU.mult).then_inc(first_dve_chain, done.add())
            dve.wait_ge(first_dve_chain, done.n)
            TTN(t0, t0, t1, ALU.subtract).then_inc(first_dve_chain, done.add())
            dve.wait_ge(first_dve_chain, done.n)
            TTN(par_of(2), lj(t0), lj(den), ALU.mult).then_inc(first_dve_chain, done.add())
            dve.wait_ge(first_dve_chain, done.n)

            with dve.Fori(0, DEPTH) as l:
                done = Count()

                def nrm(i, w):
                    return [norm[:, i, 0:w], None, None, norm[:, 4, 0:w], norm[:, 5, 0:w], norm[:, 6, 0:w]]

                dve.tensor_copy(ssm_now[:, :, :], ssm_par[:, bass.ds(l, 1), :, :].rearrange("p a i j -> p (a i) j")).then_inc(dve_chain, done.add())
                dve.wait_ge(squares, TT)
                rsqrt(done, norm[:, 7, 0:TT], nrm(0, TT), 1.0 / D, TT)
                for tt in range(TT):
                    TS(h[:, tt, :], x[:, tt, :], norm[:, 7, tt:tt + 1], None, ALU.mult).then_inc(h_ready, 1)

                dve.wait_ge(b_loaded, 32)
                f_re, f_im = (bc(ssm_now[:, i, :], 2, GRP) for i in (1, 2))
                b_re, b_im = braw[:, 0, :, :], braw[:, 1, :, :]
                for dst, fa, fb, op in ((0, f_re, f_im, ALU.subtract), (1, f_im, f_re, ALU.add)):
                    TTN(bbar[:, dst, :, :], b_re, fa, ALU.mult).then_inc(dve_chain, done.add())
                    TTN(btmp[:, dst, :, :], b_im, fb, ALU.mult).then_inc(dve_chain, done.add())
                    dve.wait_ge(dve_chain, done.n)
                    TTN(bbar[:, dst, :, :], bbar[:, dst, :, :], btmp[:, dst, :, :], op).then_inc(dve_chain, done.add())
                    dve.wait_ge(dve_chain, done.n)
                    TTN(bwide[:, dst, :, :].rearrange("p j (g i) -> p j g i", g=2), bc(bbar[:, dst, :, :], 2, 2),
                        bc(own_group[:, :].rearrange("p (g i) -> p g i", g=2), 1, STILES), ALU.mult).then_inc(b_scaled, 1)

                for tt in range(TT):
                    dve.wait_ge(qkv_psum, tt + 1)
                    b0 = (6, 0)[tt]
                    dve.tensor_copy(qkv[:, tt, 0:512], bank(b0)).then_inc(qkv_sbuf, 1)
                    dve.tensor_copy(qkv[:, tt, 512:U0], bank(b0 + 1, 0, U0 - 512)).then_inc(qkv_sbuf, 1)

                own = bc(own_group[:, :], 1, CH_T * QPT)
                for i in range(2):
                    dve.wait_ge(ssm_wT_psum, 3 + i)
                    src = bank(4 + i).rearrange("p (q s) -> p q s", s=2 * GRP)
                    dst = cT[:, 2 * i, :, :].rearrange("p m (q s) -> p (m q) s", s=2 * GRP)
                    STT(out=dst, in0=src, scalar=1.0 - 2 * i, in1=own, op0=ALU.mult, op1=ALU.mult).then_inc(ssm_c_sbuf, 1)
                dve.wait_ge(ssm_c_sbuf, 1)
                TS(cT[:, 1, :, :], cT[:, 0, :, :], -1.0, None, ALU.mult).then_inc(ssm_c_sbuf, 1)

                def lora_scale():
                    dve.wait_ge(lora_squares, 2 * TT)
                    rsqrt(done, norm[:, 7, 2:4], nrm(2, TT), 1.0 / QR, TT)
                    rsqrt(done, norm[:, 7, 4:6], nrm(3, TT), 1.0 / KVR, TT)
                    for tt in range(TT):
                        TS(lora[:, tt, 0:QR], qkv[:, tt, 0:QR], norm[:, 7, 2 + tt:3 + tt], None, ALU.mult).then_inc(lora_ready, 1)
                        TS(lora[:, tt, QR:QR + KVR], qkv[:, tt, QR:QR + KVR], norm[:, 7, 4 + tt:5 + tt], None, ALU.mult).then_inc(lora_ready, 1)

                def shared_key():
                    dve.wait_ge(hT_psum, 4)
                    for tt in range(TT):
                        dve.tensor_copy(qk[:, tt, HEADS:, NOPE:], bc(qkv[:, tt, QR + KVR:U0], 1, HEADS)).then_inc(key_shared, 1)
                    for tt in range(TT):
                        dve.wait_ge(qk_squares, tt + 1)
                        dve.tensor_reduce(norm[:, 2, tt * 16:tt * 16 + 16], sq[:, tt, :, :], AXX, ALU.add).then_inc(dve_chain, done.add())
                    dve.wait_ge(dve_chain, done.n)
                    W = TT * 2 * HEADS
                    rsqrt(done, norm[:, 3, 0:W], nrm(2, W), 1.0 / QKD, W)
                    dve.wait_ge(head_gains_loaded, 32)
                    for tt in range(TT):
                        TTN(qk[:, tt, :, :], qk[:, tt, :, :], bc(norm[:, 3, tt * 16:tt * 16 + 16], 2, QKD), ALU.mult).then_inc(dve_chain, done.add())
                    dve.wait_ge(dve_chain, done.n)
                    for tt in range(TT):
                        for i in range(2):
                            TTN(qk[:, tt, i * HEADS:(i + 1) * HEADS, :], qk[:, tt, i * HEADS:(i + 1) * HEADS, :],
                                   bc(head_gain[:, i, :], 1, HEADS), ALU.mult).then_inc(dve_chain, done.add())
                    dve.wait_ge(dve_chain, done.n)
                    for tt in range(TT):
                        half = qk[:, tt, :, NOPE:].rearrange("p h (i f) -> p h i f", i=2)
                        cos, sin = (bc(bc(rope[:, i, tt, :], 1, 2), 1, 2 * HEADS) for i in range(2))
                        ca = sq[:, 0, :, 0:ROPE].rearrange("p h (i f) -> p h i f", i=2)
                        sa = sq[:, 1, :, 0:ROPE].rearrange("p h (i f) -> p h i f", i=2)
                        TTN(ca, half, cos, ALU.mult).then_inc(dve_chain, done.add())
                        TTN(sa, half, sin, ALU.mult).then_inc(dve_chain, done.add())
                        dve.wait_ge(dve_chain, done.n)
                        TTN(half[:, :, 0, :], ca[:, :, 0, :], sa[:, :, 1, :], ALU.subtract).then_inc(dve_chain, done.add())
                        TTN(half[:, :, 1, :], ca[:, :, 1, :], sa[:, :, 0, :], ALU.add).then_inc(dve_chain, done.add())
                        dve.wait_ge(dve_chain, done.n)
                    dve.engine_nop().then_inc(qk_ready, 1)

                def softmax(c, hg, qb):
                    w = P * (qb + 1)
                    pr = probs[:, :, 0:w]
                    sc = banks(6, 2)[:, 0:4 * w].rearrange("p (h k) -> p h k", h=4)
                    mask = bc(amask[:, SEQ - w:], 1, 4)
                    dve.wait_ge(scores_psum, c + 1)
                    STT(out=pr, in0=sc, scalar=SCALE, in1=mask, op0=ALU.mult, op1=ALU.add).then_inc(dve_chain, done.add())
                    dve.wait_ge(dve_chain, done.n)
                    dve.tensor_reduce(norm[:, 2, 0:4], pr, AXX, ALU.max).then_inc(dve_chain, done.add())
                    dve.wait_ge(dve_chain, done.n)
                    TTN(pr, pr, bc(norm[:, 2, 0:4], 2, w), ALU.subtract).then_inc(probs_shifted, 1)

                def shares(c, hg, qb):
                    w = P * (qb + 1)
                    pr = probs[:, :, 0:w]
                    dve.wait_ge(probs_exp, c + 1)
                    dve.tensor_reduce(norm[:, 2, 4:8], pr, AXX, ALU.add).then_inc(dve_chain, done.add())
                    dve.wait_ge(dve_chain, done.n)
                    dve.reciprocal(norm[:, 2, 8:12], norm[:, 2, 4:8]).then_inc(dve_chain, done.add())
                    dve.wait_ge(dve_chain, done.n)
                    TTN(pr, pr, bc(norm[:, 2, 8:12], 2, w), ALU.mult).then_inc(probs_ready, 1)

                def drive(j):
                    bu = bank(j % 2).rearrange("p (i s) -> p i s", i=2)
                    cos, sin = (bc(turn[:, j % 2, i, :], 1, 2) for i in range(2))
                    dve.wait_ge(table_ready, 2 * j + 2)
                    dve.wait_ge(bu_psum, j + 1)
                    TTN(mulc, bu, cos, ALU.mult).then_inc(dve_chain, done.add())
                    TTN(muls, bu, sin, ALU.mult).then_inc(dve_chain, done.add())
                    dve.wait_ge(dve_chain, done.n)
                    TTN(driven[:, 0, :], mulc[:, 0, :], muls[:, 1, :], ALU.add).then_inc(modulated, 1)
                    TTN(driven[:, 1, :], mulc[:, 1, :], muls[:, 0, :], ALU.subtract).then_inc(modulated, 1)
                    dve.wait_ge(modulated, 2 * j + 2)
                    decay = ssm_now[:, 0, j:j + 1].broadcast_to([P, SEQ])
                    for i in range(2):
                        dve.tensor_tensor_scan(state[:, i, :], decay, driven[:, i, :], 0.0, ALU.mult, ALU.add).then_inc(dve_chain, done.add())
                    dve.wait_ge(dve_chain, done.n)

                def back(j):
                    cos, sin = (bc(turn[:, j % 2, i, :], 1, 2) for i in range(2))
                    if j >= 2:
                        dve.wait_ge(y_used, j - 1)
                    TTN(backc[:, j % 2, :, :], state, cos, ALU.mult).then_inc(dve_chain, done.add())
                    TTN(backs[:, j % 2, :, :], state, sin, ALU.mult).then_inc(turned_back, 1)

                def skip(m):
                    dve.wait_ge(y_psum, m + 1)
                    dve.wait_ge(d_loaded, 16)
                    y = uT[:, m, :]
                    STT(out=y, in0=y, scalar=dskip[:, m:m + 1], in1=bank(2 + m % 2, 0, SEQ), op0=ALU.mult, op1=ALU.add).then_inc(dve_chain, done.add())
                    dve.wait_ge(dve_chain, done.n)
                    TTN(garg, y, y, ALU.mult).then_inc(dve_chain, done.add())
                    dve.wait_ge(dve_chain, done.n)
                    TS(garg, garg, 0.044715, 1.0, ALU.mult, ALU.add).then_inc(dve_chain, done.add())
                    dve.wait_ge(dve_chain, done.n)
                    TTN(garg, garg, y, ALU.mult).then_inc(gelu_arg, 1)

                def gelu(m):
                    dve.wait_ge(gelu_tanh, m + 1)
                    STT(out=uT[:, m, :], in0=gtmp, scalar=1.0, in1=uT[:, m, :], op0=ALU.add, op1=ALU.mult).then_inc(gelu_ready, 1)

                for j in range(STILES):
                    drive(j)
                    back(j)
                    attention(j, dict(lora=lora_scale, qk=shared_key, scores=softmax, probs=shares))
                    if j % QPT == 0 and j:
                        skip(j // QPT - 1)
                    if j % QPT == 1 and j > 1:
                        gelu(j // QPT - 1)
                skip(CH_T - 1)
                gelu(CH_T - 1)

                for tt in range(TT):
                    vbank, abank = ((0, 6), (2, 0))[tt]
                    dve.wait_ge(glu_gate_tanh, tt + 1)
                    dve.wait_ge(glu_psum, (2, 4)[tt])
                    STT(out=merged[:, tt, :], in0=glu_t[:, tt, :], scalar=1.0, in1=banks(vbank, 2), op0=ALU.add, op1=ALU.mult).then_inc(glu_read, 1)
                    dve.wait_ge(gates_sbuf, 8)
                    dve.wait_ge(attn_proj_psum, tt + 1)
                    if tt:
                        dve.wait_ge(merged_ready, tt)
                    STT(out=attn_m, in0=gate_t[:, tt, 0:D], scalar=1.0, in1=banks(abank, 2), op0=ALU.add, op1=ALU.mult).then_inc(dve_chain, done.add())
                    dve.wait_ge(glu_read, tt + 1)
                    STT(out=merged[:, tt, :], in0=gate_t[:, tt, D:], scalar=1.0, in1=merged[:, tt, :], op0=ALU.add, op1=ALU.mult).then_inc(dve_chain, done.add())
                    dve.wait_ge(dve_chain, done.n)
                    STT(out=merged[:, tt, :], in0=merged[:, tt, :], scalar=0.25, in1=attn_m, op0=ALU.mult, op1=ALU.add).then_inc(merged_ready, 1)
                for tt in range(TT):
                    dve.wait_ge(out_psum, tt + 1)
                    STT(out=x[:, tt, :], in0=banks(2 * tt, 2), scalar=0.5, in1=x[:, tt, :], op0=ALU.mult, op1=ALU.add).then_inc(x_mixed, 1)

                dve.wait_ge(squares2, TT)
                rsqrt(done, norm[:, 7, 0:TT], nrm(1, TT), 1.0 / D, TT)
                for tt in range(TT):
                    TS(h2[:, tt, :], x[:, tt, :], norm[:, 7, tt:tt + 1], None, ALU.mult).then_inc(h2_ready, 1)

                def red(dst, src, op):
                    dve.tensor_reduce(dst, src, AXX, op).then_inc(dve_chain, done.add())
                    dve.wait_ge(dve_chain, done.n)

                def first_of(dst, is_it, tmp, least, n):
                    idx = bc(iota[:, 0:n], 1, TT)
                    STT(out=tmp, in0=idx, scalar=-64.0, in1=is_it, op0=ALU.add, op1=ALU.mult).then_inc(dve_chain, done.add())
                    dve.wait_ge(dve_chain, done.n)
                    red(least, tmp, ALU.min)
                    STT(out=dst, in0=idx, scalar=-64.0, in1=bc(least, 2, n), op0=ALU.add, op1=ALU.is_equal).then_inc(dve_chain, done.add())
                    dve.wait_ge(dve_chain, done.n)

                dve.memset(sortedT[:, :, NPOS:], 0.0).then_inc(offsets_ready, 1)
                dve.wait_ge(logits_psum, 1)
                dve.tensor_copy(logits, bank(0, 0, 2 * 64).rearrange("p (t n) -> p t n", t=TT)[:, :, 0:ROUTE]).then_inc(dve_chain, done.add())
                dve.wait_ge(dve_chain, done.n)
                lg, le = logits[:, :, 0:EG], logits[:, :, EG:].rearrange("p t (g e) -> p t g e", g=EG)
                v = [r1[:, i, :] for i in range(16)]
                red(v[0], lg, ALU.max)
                TTN(expo_in[:, :, 0:EG], lg, bc(v[0], 2, EG), ALU.subtract).then_inc(dve_chain, done.add())
                TTN(r4[:, 0, :, :], lg, bc(v[0], 2, EG), ALU.is_equal).then_inc(dve_chain, done.add())
                dve.wait_ge(dve_chain, done.n)
                group = r4[:, 2, :, :]
                first_of(group, r4[:, 0, :, :], r4[:, 1, :, :], v[1], EG)
                big = rt[:, 0, :, :].rearrange("p t (g e) -> p t g e", g=EG)
                TTN(big, le, bc(group, 3, EPG), ALU.mult).then_inc(dve_chain, done.add())
                dve.wait_ge(dve_chain, done.n)
                el, second = r8[:, 0, :, :], r8[:, 5, :, :]
                red(el, rt[:, 0, :, :].rearrange("p t (g e) -> p t e g", g=EG), ALU.add)
                red(v[2], el, ALU.max)
                TTN(r8[:, 1, :, :], el, bc(v[2], 2, EPG), ALU.subtract).then_inc(dve_chain, done.add())
                TTN(r8[:, 2, :, :], el, bc(v[2], 2, EPG), ALU.is_equal).then_inc(dve_chain, done.add())
                dve.wait_ge(dve_chain, done.n)
                top1, top2 = r8[:, 3, :, :], r8[:, 4, :, :]
                first_of(top1, r8[:, 2, :, :], r8[:, 6, :, :], v[3], EPG)
                STT(out=second, in0=top1, scalar=MASKED, in1=r8[:, 1, :, :], op0=ALU.mult, op1=ALU.add).then_inc(dve_chain, done.add())
                dve.wait_ge(dve_chain, done.n)
                red(v[4], second, ALU.max)
                dve.tensor_copy(expo_in[:, :, EG:EG + 1], v[4].unsqueeze(2)).then_inc(dve_chain, done.add())
                dve.wait_ge(dve_chain, done.n)
                dve.engine_nop().then_inc(picked, 1)
                TTN(r8[:, 7, :, :], second, bc(v[4], 2, EPG), ALU.is_equal).then_inc(dve_chain, done.add())
                dve.wait_ge(dve_chain, done.n)
                first_of(top2, r8[:, 7, :, :], r8[:, 6, :, :], v[5], EPG)
                oh1, oh2, routed, weight, place, tmp, rank1 = (rt[:, i, :, :] for i in range(1, 8))

                def over(ap):
                    return ap.rearrange("p t (g e) -> p t g e", g=EG)

                TTN(over(oh1), bc(group, 3, EPG), bc(top1, 2, EG), ALU.mult).then_inc(dve_chain, done.add())
                TTN(over(oh2), bc(group, 3, EPG), bc(top2, 2, EG), ALU.mult).then_inc(dve_chain, done.add())
                dve.wait_ge(dve_chain, done.n)
                TTN(routed, oh1, oh2, ALU.add).then_inc(routes_ready, 1)
                dve.wait_ge(expo_ready, 1)
                red(v[6], expo[:, :, 0:EG], ALU.add)
                TS(v[7], expo[:, :, EG:EG + 1].rearrange("p t o -> p (t o)"), 1.0, None, ALU.add).then_inc(dve_chain, done.add())
                dve.wait_ge(dve_chain, done.n)
                TTN(v[8], v[6], v[7], ALU.mult).then_inc(dve_chain, done.add())
                dve.wait_ge(dve_chain, done.n)
                dve.reciprocal(v[9], v[8]).then_inc(dve_chain, done.add())
                dve.wait_ge(dve_chain, done.n)
                TTN(v[10], v[9], expo[:, :, EG:EG + 1].rearrange("p t o -> p (t o)"), ALU.mult).then_inc(dve_chain, done.add())
                dve.wait_ge(dve_chain, done.n)
                TTN(weight, oh1, bc(v[9], 2, NE), ALU.mult).then_inc(dve_chain, done.add())
                TTN(tmp, oh2, bc(v[10], 2, NE), ALU.mult).then_inc(dve_chain, done.add())
                dve.wait_ge(dve_chain, done.n)
                TTN(weight, weight, tmp, ALU.add).then_inc(dve_chain, done.add())
                dve.wait_ge(rank_psum, 1)
                rank = bank(1, 0, TT * NE).rearrange("p (t e) -> p t e", t=TT)
                dve.tensor_copy(count[:, 0, :], bank(1, TT * NE, TT * NE + NE)).then_inc(dve_chain, done.add())
                TS(rank1, rank, 1.0, None, ALU.add).then_inc(dve_chain, done.add())
                dve.wait_ge(dve_chain, done.n)
                dve.tensor_tensor_scan(count[:, 1, :], ones[:, 0:NE], count[:, 0, :], 0.0, ALU.mult, ALU.add).then_inc(dve_chain, done.add())
                dve.wait_ge(dve_chain, done.n)
                TTN(count[:, 2, :], count[:, 1, :], count[:, 0, :], ALU.subtract).then_inc(dve_chain, done.add())
                dve.wait_ge(dve_chain, done.n)
                for r in range(PASSES):
                    TS(roff[:, r, :], count[:, 2, :], float(SLOT * r), float(NPOS), ALU.add, ALU.min).then_inc(offsets_ready, 1)
                dve.tensor_reduce(v[15][:, 0:1], count[:, 0, :], AXX, ALU.max).then_inc(dve_chain, done.add())
                dve.wait_ge(dve_chain, done.n)
                TS(rmany[:, bass.ds(l, 1)], v[15][:, 0:1], float(SLOT), None, ALU.is_gt).then_inc(counted, 1)
                TTN(place, rank1, bc(count[:, 2, :], 1, TT), ALU.add).then_inc(dve_chain, done.add())
                TTN(tmp, rank1, routed, ALU.mult).then_inc(dve_chain, done.add())
                dve.wait_ge(dve_chain, done.n)
                TS(rank1, tmp, 1.0, None, ALU.subtract).then_inc(dve_chain, done.add())
                dve.wait_ge(dve_chain, done.n)
                for i, oh in enumerate((oh1, oh2)):
                    TTN(tmp, oh, place, ALU.mult).then_inc(dve_chain, done.add())
                    dve.wait_ge(dve_chain, done.n)
                    red(v[11 + i], tmp, ALU.add)
                for tt in range(TT):
                    TS(v[13][:, tt:tt + 1], v[11][:, tt:tt + 1], 1.0, None, ALU.subtract).then_inc(dve_chain, done.add())
                    TS(v[14][:, tt:tt + 1], v[12][:, tt:tt + 1], 1.0, None, ALU.subtract).then_inc(dve_chain, done.add())
                dve.wait_ge(dve_chain, done.n)
                for tt in range(TT):
                    TS(perm[:, tt, :], iota[:, :], v[13][:, tt:tt + 1], None, ALU.is_equal).then_inc(dve_chain, done.add())
                dve.wait_ge(dve_chain, done.n)
                for tt in range(TT):
                    STT(out=perm[:, tt, :], in0=iota[:, :], scalar=v[14][:, tt:tt + 1], in1=perm[:, tt, :],
                        op0=ALU.is_equal, op1=ALU.add).then_inc(perm_ready, 1)

                def select(p, par, pair=None):
                    if pair is None and (not isinstance(p, int) or p >= 2):
                        dve.wait_ge(turned_psum, p - 1)
                        dve.sem_inc(held, 1)
                    dst = sel[:, par, :, :].rearrange("p t (e s) -> p t e s", e=2)
                    e0 = (p if pair is None else pair) * 2
                    pick = [bc(a[:, :, bass.ds(e0, 2)], 3, SLOT) for a in (rank1, weight)]
                    TTN(dst, bc(bc(iota[:, 0:SLOT], 1, 2), 1, TT), pick[0], ALU.is_equal).then_inc(sel_half, 1)
                    dve.wait_ge(sel_half, p + 1)
                    dve.sem_inc(held, 1)
                    TTN(dst, dst, pick[1], ALU.mult).then_inc(sel_ready, 1)

                def swiglu(p, par):
                    dve.wait_ge(gate_tanh_ready, p + 1)
                    dve.sem_inc(held, 1)
                    STT(out=hidden[:, par, :], in0=gtanh[:, par, :], scalar=1.0, in1=bank(par, 0, DE), op0=ALU.add, op1=ALU.mult).then_inc(hidden_half, 1)
                    dve.wait_ge(hidden_half, p + 1)
                    dve.sem_inc(held, 1)
                    STT(out=hidden[:, par, :], in0=hidden[:, par, :], scalar=0.5, in1=bank(par, DE, 2 * DE), op0=ALU.mult, op1=ALU.mult).then_inc(hidden_ready, 1)

                def sel_out(p, par):
                    dve.wait_ge(hiddenT_sbuf, p + 1)
                    dve.sem_inc(held, 1)
                    dve.tensor_copy(selT[:, par, :], bank(par, 2 * P, 4 * P)).then_inc(selT_sbuf, 1)

                def down_hi(p):
                    dve.wait_ge(down_psum, p + 1)
                    dve.sem_inc(held, 1)
                    dve.tensor_copy(down[:, 512:], bank(3)).then_inc(down_sbuf_hi, 1)

                def step(p, par, last=False):
                    if not last:
                        select(p + 1, 1 - par)
                    sel_out(p, par)
                    down_hi(p)
                    if not last:
                        swiglu(p + 1, 1 - par)

                select(0, 0)
                swiglu(0, 0)
                step(0, 0)
                with dve.Fori(0, NPAIR // 2 - 1) as i:
                    for k in range(2):
                        step(i * 2 + 1 + k, (1 + k) % 2)
                step(NPAIR - 1, 1, last=True)
                for tt in range(TT):
                    dve.wait_ge(moe_psum, tt + 1)
                    dve.tensor_copy(x[:, tt, :], banks(4 + 2 * tt, 2)).then_inc(x_ready, 1)

                def shift_ranks(r):
                    dve.wait_ge(sel_ready, r * NPAIR)
                    dve.sem_inc(held, 1)
                    dve.tensor_scalar(rank1, rank1, float(SLOT), None, ALU.subtract).then_inc(rank_shifted, 1)
                    dve.wait_ge(rank_shifted, r)
                    dve.sem_inc(held, 1)

                def more(p, pair, r):
                    select(p, 0, pair)
                    swiglu(p, 0)
                    sel_out(p, 0)
                    down_hi(p)
                    for tt in range(TT):
                        dve.wait_ge(moe_psum, (p - (NPAIR - 1)) * TT + tt + 1)
                        dve.sem_inc(held, 1)
                        dve.tensor_copy(x[:, tt, :], banks(4 + 2 * tt, 2)).then_inc(x_ready, 1)

                with dve.If(crowded(dve, l) > 0):
                    further_steps(dve, more, shift_ranks)
                leave_layer(dve, l)
            dve.drain().then_inc(first_result_ready, TT)

        @block.tensor
        def _(pe):
            mm = pe.matmul

            def group(dst, lhs, rhs, n, then=None, **kw):
                for c in range(n):
                    last = mm(dst, lhs(c), rhs(c), start=c == 0, stop=c == n - 1, **kw)
                return last

            for semaphore in free_a + free_b:
                pe.sem_inc(semaphore, 1)
            pe.wait_ge(first_constants, 6 + HALF + 5)
            pe.wait_ge(first_params_loaded, 48)
            pe.wait_ge(first_dt_wide, 1)
            NW = DEPTH * STILES
            for i in range(3):
                last = pe.transpose(bank(7, i * NW, (i + 1) * NW), praw[0:NW, i, :], ident[0:NW, 0:NW])
            last.then_inc(first_params_turned, 1)

            with pe.Fori(0, DEPTH) as l:
                def a_ready(a):
                    pe.wait_ge(loaded_a[a % A_SLOTS], (l * A_USES + a // A_SLOTS + 1) * 32)
                    pe.sem_inc(held, 1)

                for i in range(KC // 2):
                    pe.wait_ge(h_ready, TT)
                    if i >= 2:
                        pe.wait_ge(hT_sbuf, 2 * i - 2)
                    for c in (2 * i, 2 * i + 1):
                        for tt in range(TT):
                            last = pe.transpose(bank(i % 2, (c % 2) * SEQ + tt * P, (c % 2) * SEQ + (tt + 1) * P),
                                                h[:, tt, c::KC], ident[:, :])
                    last.then_inc(hT_psum, 1)
                pe.wait_ge(hT_sbuf, KC)
                a_ready(A_U)
                w = slotA_kc(A_U)
                for m in range(CH_T):
                    last = group(bank(2 + m, 0, SEQ), lambda c: w[:, c, m * P:(m + 1) * P], lambda c: hT[:, c, :], KC)
                    last.then_inc(u_psum, 1)
                a_ready(A_Q)
                w = slotA_kc(A_Q)
                for tt in range(TT):
                    b0 = (6, 0)[tt]
                    group(bank(b0), lambda c: hT[:, c, tt * P:(tt + 1) * P], lambda c: w[:, c, :], KC)
                    if tt == 0:
                        a_ready(A_TAIL)
                    last = group(bank(b0 + 1, 0, U0 - 512), lambda c: hT[:, c, tt * P:(tt + 1) * P], lambda c: wtail[:, c, :], KC)
                    last.then_inc(qkv_psum, 1)
                pe.drain().then_inc(free_a[A_U % A_SLOTS], 1)
                pe.sem_inc(free_a[A_Q % A_SLOTS], 1)
                pe.wait_ge(u_sbuf, CH_T)
                for i in range(2):
                    pe.wait_ge(b_scaled, i + 1)
                    for m in range(CH_T):
                        last = pe.transpose(bank(2 + i, m * P, (m + 1) * P),
                                            bwide[:, i, m * QPT:(m + 1) * QPT, :].rearrange("p j s -> p (j s)"), ident[:, :])
                    last.then_inc(ssm_wT_psum, 1)
                pe.wait_ge(c_loaded, 64)
                for i in range(2):
                    for m in range(CH_T):
                        last = pe.transpose(bank(4 + i, m * P, (m + 1) * P),
                                            craw[:, i, m, :, :].rearrange("p d s -> p (d s)"), ident[:, :])
                    last.then_inc(ssm_wT_psum, 1)

                def lora_turn():
                    pe.wait_ge(lora_ready, 2 * TT)
                    pe.wait_ge(qkv_sbuf, 2 * TT)
                    for c in range(QC + KVC):
                        if c >= 2:
                            pe.wait_ge(loraT_sbuf, c - 1)
                        for tt in range(TT):
                            src = lora[:, tt, c:QR:QC] if c < QC else lora[:, tt, QR + c - QC:QR + KVR:KVC]
                            last = pe.transpose(bank(6 + c % 2, tt * P, (tt + 1) * P), src, ident[:, :])
                        last.then_inc(loraT_psum, 1)

                def q_up():
                    pe.wait_ge(loraT_sbuf, QC + KVC)
                    for tt in range(TT):
                        if tt:
                            pe.wait_ge(q_sbuf, 2 * tt)
                        for i in range(2):
                            last = group(bank(6 + i, 0, 4 * QKD), lambda c: loraT[:, c, tt * P:(tt + 1) * P],
                                         lambda c: wuq[:, c, i * 4 * QKD:(i + 1) * 4 * QKD], QC)
                        last.then_inc(q_psum, 1)
                    pe.drain().then_inc(free_a[A_TAIL % A_SLOTS], 1)

                def kv_up():
                    pe.wait_ge(loaded_b[0], (l * (NE // B_SLOTS + 1) + 1) * 16)
                    pe.sem_inc(held, 1)
                    pe.wait_ge(q_sbuf, 4)
                    for tt in range(TT):
                        if tt:
                            pe.wait_ge(k_sbuf, 2 * tt)
                            pe.wait_ge(v_sbuf, 2 * tt)
                        for i in range(2):
                            last = group(bank(6 + i), lambda c: loraT[:, QC + c, tt * P:(tt + 1) * P],
                                         lambda c: wukv[:, c, i * 512:(i + 1) * 512], KVC)
                        last.then_inc(kv_psum, 1)
                    pe.drain().then_inc(free_b[0], 1)

                def qk_turn(hg):
                    pe.wait_ge(qk_ready, 1)
                    pe.wait_ge(v_sbuf, 4)
                    for i in range(4):
                        n = 4 * hg + i
                        if i >= 2:
                            pe.wait_ge(qkT_sbuf, n - 1)
                        for k in range(2):
                            head = (i // 2) * HEADS + hg * 4 + 2 * (i % 2) + k
                            for tt in range(TT):
                                last = pe.transpose(psum[0:QKD, 6 + i % 2, k * SEQ + tt * P:k * SEQ + (tt + 1) * P],
                                                    qk[:, tt, head, :], ident[:, :])
                        last.then_inc(qkT_psum, 1)

                def scores(c, hg, qb):
                    pe.wait_ge(qkT_sbuf, 4 * hg + 4)
                    w = P * (qb + 1)
                    for hh in range(4):
                        last = mm(banks(6, 2)[:, hh * w:(hh + 1) * w], qkT[0:QKD, 0, hh, qb * P:(qb + 1) * P],
                                  qkT[0:QKD, 1, hh, 0:w], start=True, stop=True)
                    last.then_inc(scores_psum, 1)

                def probs_turn(c, hg, qb):
                    pe.wait_ge(probs_ready, c + 1)
                    for hh in range(4):
                        for k in range(qb + 1):
                            i = hh * (qb + 1) + k
                            last = pe.transpose(banks(6, 2)[:, i * P:(i + 1) * P], probs[:, hh, k * P:(k + 1) * P], ident[:, :])
                    last.then_inc(probsT_psum, 1)

                def values(c, hg, qb):
                    pe.wait_ge(probsT_sbuf, c + 1)
                    if c:
                        pe.wait_ge(o_sbuf, c)
                    for hh in range(4):
                        lo = hh % 2 * VD
                        for k in range(qb + 1):
                            last = mm(psum[lo:lo + VD, 5, hh // 2 * P:(hh // 2 + 1) * P], vtok[:, k, hg * 4 + hh, :],
                                      probsT[:, hh, k, :], start=k == 0, stop=k == qb)
                    last.then_inc(o_psum, 1)

                def gate(g):
                    a = A_G + g // 2
                    if g % 2 == 0:
                        a_ready(a)
                    pe.wait_ge(ssm_b_sbuf, 2)
                    pe.wait_ge(ssm_c_sbuf, 3)
                    if g:
                        pe.wait_ge(gates_sbuf, g)
                    w, tt = slotA_kc(a), g % 2
                    last = group(bank(4), lambda c: hT[:, c, tt * P:(tt + 1) * P], lambda c: w[:, c, :], KC)
                    last.then_inc(gates_psum, 1)
                    if g % 2:
                        pe.drain().then_inc(free_a[a % A_SLOTS], 1)

                def inputs(j):
                    m, q = j // QPT, j % QPT
                    rows = slice(32 * q, 32 * q + 32)
                    if j >= 2:
                        pe.wait_ge(modulated, 2 * j - 2)
                    for i in range(2):
                        last = mm(bank(j % 2, i * SEQ, (i + 1) * SEQ), bT[rows, i, m, :], uT[rows, m, :], start=True, stop=True)
                    last.then_inc(bu_psum, 1)

                def outputs(j):
                    m, q = j // QPT, j % QPT
                    pe.wait_ge(turned_back, j + 1)
                    if q == 0 and m >= 2:
                        pe.wait_ge(gelu_arg, m - 1)
                    dst = psum[32 * q:32 * q + 32, 2 + m % 2, 0:SEQ]
                    cols = slice(32 * q, 32 * q + 32)
                    terms = ((0, backc, 0), (1, backs, 1), (2, backc, 1), (2, backs, 0))
                    for k, (ci, src, i) in enumerate(terms):
                        last = mm(dst, cT[:, ci, m, cols], src[:, j % 2, i, :], start=k == 0, stop=k == 3)
                    last.then_inc(y_used, 1)
                    if q == QPT - 1:
                        pe.drain().then_inc(y_psum, 1)

                pe.wait_ge(ssm_b_sbuf, 2)
                pe.wait_ge(ssm_c_sbuf, 3)
                inputs(0)
                for j in range(STILES):
                    if j + 1 < STILES:
                        inputs(j + 1)
                    attention(j, dict(lora=lora_turn, q=q_up, kv=kv_up, turn=qk_turn, scores=scores, probs=probs_turn, values=values))
                    if j % 2 == 0:
                        gate(j // 2)
                    outputs(j)

                def glu(half, tt, b):
                    w = slotA(A_GLU + half).rearrange("p (c n) -> p c n", c=CH_T)
                    for i in range(2):
                        last = group(bank(b + i), lambda c: uT[:, c, tt * P:(tt + 1) * P], lambda c: w[:, c, i * 512:(i + 1) * 512], CH_T)
                    last.then_inc(glu_psum, 1)

                def attn_proj(tt, b):
                    w = slotA(A_AP).rearrange("p (c n) -> p c n", c=CH_T)
                    for i in range(2):
                        last = group(bank(b + i), lambda c: oT[:, c, tt * P:(tt + 1) * P], lambda c: w[:, c, i * 512:(i + 1) * 512], HEADS // 2)
                    last.then_inc(attn_proj_psum, 1)

                a_ready(A_AP)
                pe.wait_ge(o_sbuf, 4)
                attn_proj(0, 6)
                a_ready(A_GLU)
                a_ready(A_GLU + 1)
                pe.wait_ge(gelu_ready, CH_T)
                pe.wait_ge(gates_sbuf, 8)
                glu(1, 0, 2)
                glu(0, 0, 0)
                glu(1, 1, 4)
                pe.wait_ge(glu_gate_tanh, 1)
                glu(0, 1, 2)
                pe.wait_ge(glu_read, 1)
                attn_proj(1, 0)
                pe.drain().then_inc(free_a[A_GLU % A_SLOTS], 1)
                pe.sem_inc(free_a[(A_GLU + 1) % A_SLOTS], 1)
                pe.sem_inc(free_a[A_AP % A_SLOTS], 1)

                pe.wait_ge(glu_gate_tanh, 2)
                for tt in range(TT):
                    pe.wait_ge(merged_ready, tt + 1)
                    for i in range(2):
                        for c in range(4 * i, 4 * i + 4):
                            last = pe.transpose(bank(4 + 2 * tt + i, (c % 4) * P, (c % 4 + 1) * P), merged[:, tt, c::KC], ident[:, :])
                        last.then_inc(mergedT_psum, 1)
                a_ready(A_OUT)
                a_ready(A_OUT + 1)
                for tt in range(TT):
                    pe.wait_ge(mergedT_sbuf, 2 * tt + 2)
                    for g in range(2):
                        w = slotA_kc(A_OUT + g)
                        last = group(bank(2 * tt + g), lambda c: hT[:, c, tt * P:(tt + 1) * P], lambda c: w[:, c, :], KC)
                    last.then_inc(out_psum, 1)
                pe.drain().then_inc(free_a[A_OUT % A_SLOTS], 1)
                pe.sem_inc(free_a[(A_OUT + 1) % A_SLOTS], 1)

                pe.wait_ge(h2_ready, TT)
                pe.wait_ge(mergedT_sbuf, 4)
                for i in range(KC // 2):
                    for c in (2 * i, 2 * i + 1):
                        for tt in range(TT):
                            last = pe.transpose(bank(4 + i, (c % 2) * SEQ + tt * P, (c % 2) * SEQ + (tt + 1) * P),
                                                h2[:, tt, c::KC], ident[:, :])
                    last.then_inc(h2T_psum, 1)
                pe.wait_ge(h2T_sbuf, KC)
                pe.wait_ge(router_loaded, 32)
                for tt in range(TT):
                    last = group(bank(0, tt * 64, tt * 64 + ROUTE), lambda c: hT[:, c, tt * P:(tt + 1) * P], lambda c: wroute[:, c, :], KC)
                last.then_inc(logits_psum, 1)
                for tt in range(TT):
                    for i in range(2):
                        mm(bank(4 + 2 * tt + i), ident[:, :], x[:, tt, i * 512:(i + 1) * 512], start=True, stop=False)
                pe.wait_ge(routes_ready, 1)
                routed = rt[:, 3, :, :]
                mm(bank(1, 0, NE), before[:, :], routed[:, 0, :], start=True, stop=True)
                mm(bank(1, NE, 2 * NE), before[:, :], routed[:, 1, :], start=True, stop=False)
                mm(bank(1, NE, 2 * NE), ones[:, :], routed[:, 0, :], start=False, stop=True)
                mm(bank(1, 2 * NE, 3 * NE), ones[:, :], routed[:, 0, :], start=True, stop=False)
                mm(bank(1, 2 * NE, 3 * NE), ones[:, :], routed[:, 1, :], start=False, stop=True).then_inc(rank_psum, 1)
                pe.wait_ge(perm_ready, TT)
                for c in range(KC):
                    if c >= 4:
                        pe.wait_ge(sorted_sbuf, c - 3)
                    last = group(bank(c % 4), lambda tt: h2[:, tt, c::KC], lambda tt: perm[:, tt, :], TT)
                    last.then_inc(sorted_psum, 1)

                def gate_up(p, par, turn=None):
                    pe.wait_ge(pair_copied, p * 2 + 2)
                    pe.sem_inc(held, 1)
                    if turn is not None:
                        if not isinstance(p, int) or p >= 2:
                            pe.wait_ge(hiddenT_sbuf, p - 1)
                            pe.sem_inc(held, 1)
                            pe.wait_ge(selT_sbuf, p - 1)
                            pe.sem_inc(held, 1)
                        use = l * A_USES + A_MIX // A_SLOTS + turn
                        for e in range(2):
                            pe.wait_ge(loaded_a[2 * par + e], (use + 1) * 32)
                            pe.sem_inc(held, 1)
                    for c in range(KC):
                        for e in range(2):
                            w = ringA[:, 2 * par + e, :].rearrange("p (u c n) -> p u c n", u=2, c=KC)
                            last = mm(psum[e * SLOT:(e + 1) * SLOT, par, :], pairT[:, par, c, e * SLOT:(e + 1) * SLOT],
                                      w[:, :, c, :], start=c == 0, stop=c == KC - 1)
                            if c == KC - 1 and turn is not None:
                                last.then_inc(free_a[2 * par + e], 1)
                    pe.drain().then_inc(hidden_psum, 1)

                def turn_pair(p, par):
                    pe.wait_ge(hidden_ready, p + 1)
                    pe.sem_inc(held, 1)
                    for c in range(2):
                        pe.transpose(bank(par, c * P, (c + 1) * P), hidden[:, par, c::2], ident[:, :])
                    pe.wait_ge(sel_ready, p + 1)
                    pe.sem_inc(held, 1)
                    for tt in range(TT):
                        last = pe.transpose(bank(par, (2 + tt) * P, (3 + tt) * P), sel[:, par, tt, :], ident[:, :])
                    last.then_inc(turned_psum, 1)

                def scatter(p, par, start=False, end=False):
                    pe.wait_ge(selT_sbuf, p + 1)
                    pe.sem_inc(held, 1)
                    pe.wait_ge(down_sbuf_lo, p + 1)
                    pe.sem_inc(held, 1)
                    pe.wait_ge(down_sbuf_hi, p + 1)
                    pe.sem_inc(held, 1)
                    for tt in range(TT):
                        for i in range(2):
                            if start:
                                mm(bank(4 + 2 * tt + i), ident[:, :], x[:, tt, i * 512:(i + 1) * 512], start=True, stop=False)
                            last = mm(bank(4 + 2 * tt + i), selT[:, par, tt * P:(tt + 1) * P], down[:, i * 512:(i + 1) * 512],
                                      start=False, stop=end)
                        if end:
                            last.then_inc(moe_psum, 1)

                def down_mm(p, par, turn=None):
                    pe.wait_ge(hiddenT_sbuf, p + 1)
                    pe.sem_inc(held, 1)
                    for e in range(2 if turn is not None else 0):
                        s = 2 * par + e
                        pe.wait_ge(loaded_b[s], (b_use(l, s, turn) + 1) * 16)
                        pe.sem_inc(held, 1)
                    for i in range(2):
                        for c in range(2):
                            for e in range(2):
                                s = 2 * par + e
                                w = ringB[:, s, :].rearrange("p (c n) -> p c n", c=2)
                                last = mm(psum[e * SLOT:(e + 1) * SLOT, 2 + i, :], hiddenT[:, c, e * SLOT:(e + 1) * SLOT],
                                          w[:, c, i * 512:(i + 1) * 512], start=c == 0, stop=c == 1)
                                if i == 1 and c == 1 and turn is not None:
                                    last.then_inc(free_b[s], 1)
                    pe.drain().then_inc(down_psum, 1)

                pe.wait_ge(sorted_sbuf, KC)
                gate_up(0, 0, 0)
                gate_up(1, 1, 0)
                turn_pair(0, 0)
                down_mm(0, 0, 0)
                with pe.Fori(0, NPAIR // 2 - 1) as i:
                    for k in range(2):
                        par = (1 + k) % 2
                        p = i * 2 + 1 + k
                        gate_up(p + 1, 1 - par, i + 1)
                        turn_pair(p, par)
                        scatter(p - 1, 1 - par)
                        down_mm(p, par, i + k)
                turn_pair(NPAIR - 1, 1)
                scatter(NPAIR - 2, 0)
                down_mm(NPAIR - 1, 1, NPAIR // 2 - 1)
                scatter(NPAIR - 1, 1, end=True)

                def more(p, pair, r):
                    pe.wait_ge(x_ready, (p - (NPAIR - 1)) * TT)
                    pe.sem_inc(held, 1)
                    pe.sem_inc(more_free, 1)
                    pe.wait_ge(more_loaded, (p - (NPAIR - 1)) * 96)
                    pe.sem_inc(held, 1)
                    gate_up(p, 0)
                    turn_pair(p, 0)
                    down_mm(p, 0)
                    scatter(p, 0, start=True, end=True)

                with pe.If(crowded(pe, l) > 0):
                    further_steps(pe, more)
                leave_layer(pe, l)


def attention(slot, do):
    stages = {0: [("lora",)], 1: [("q",)], 2: [("kv",), ("qk",)], 3: [("turn", 0)],
              4: [("scores", 0, 0, 0)], 5: [("probs", 0, 0, 0)], 6: [("values", 0, 0, 0), ("scores", 1, 0, 1)],
              7: [("probs", 1, 0, 1)], 8: [("values", 1, 0, 1), ("turn", 1)], 9: [("scores", 2, 1, 0)],
              10: [("probs", 2, 1, 0)], 11: [("values", 2, 1, 0), ("scores", 3, 1, 1)], 12: [("probs", 3, 1, 1)],
              13: [("values", 3, 1, 1)]}
    for name, *args in stages.get(slot, []):
        if name in do:
            do[name](*args)


_INS = ["x", "positions", "norm_mix_g", "w_in", "q_lora_g", "w_uq", "kv_lora_g", "w_ukv", "q_head_g", "k_head_g",
        "w_attn_proj", "lam_re", "lam_im", "log_dt", "b_re", "b_im", "c_re", "c_im", "d_skip", "w_glu", "w_out",
        "norm_ffn_g", "w_router_group", "w_router_expert", "w_exp_gate", "w_exp_up", "w_exp_down"]


def kernel(**inputs):
    import numpy as _np
    import concourse.bacc as _bacc
    from concourse import mybir as _mybir
    from concourse.bass_utils import run_bass_kernel_spmd as _run

    nc = _bacc.Bacc("TRN2", target_bir_lowering=False, num_devices=1, dynamic_dma_scratch_size=256)
    arrays, tensors = {}, {}
    for name in _INS:
        a = _np.ascontiguousarray(inputs[name])
        arrays[f"in_{name}"] = a
        tensors[name] = nc.dram_tensor(f"in_{name}", a.shape, _mybir.dt.from_np(a.dtype), kind="ExternalInput").ap()
    out = nc.dram_tensor("out_0", (1, SEQ, D), F32, kind="ExternalOutput").ap()
    build(nc, tensors, out)
    r = _run(nc, [arrays], core_ids=[0])
    return r.results[0]["out_0"]
```

```python
import math
from contextlib import ExitStack

import numpy as np

import concourse.bass as bass
from concourse import mybir

ALU = mybir.AluOpType
ACT = mybir.ActivationFunctionType
AXX = mybir.AxisListType.X
F32 = mybir.dt.float32
I32 = mybir.dt.int32

P = 128
D = 1024
SEQ = 256
DEPTH = 2
TT = SEQ // P
KC = D // P

HEADS, NOPE, ROPE = 8, 64, 32
QKD = NOPE + ROPE
VD = 64
QR, KVR = 384, 256
QC, KVC = QR // P, KVR // P
CHUNK = 64
HALF = ROPE // 2
THETA = 10000.0
SCALE = QKD ** -0.5
MASKED = -1.0e30

SSM = 512
GRP = 16
GROUPS = SSM // GRP
NST = 64
STILES = GROUPS * NST // P
CH_T = SSM // P
QPT = STILES // CH_T

COLS = QR + KVR + ROPE + SSM + 2 * D
U0 = QR + KVR + ROPE
G0 = U0 + SSM
TAIL = U0 - 512

EG, EPG = 4, 8
NE = EG * EPG
NPAIR = NE // 2
DE = 256
SLOT = 64
PASSES = SEQ // SLOT
ROUTE = EG + NE
NPOS = 2 * SEQ
EPS = 1e-6

TWO_PI = 2.0 * math.pi
ROUND = 1.5 * 2.0 ** 23


def split_two_pi():
    parts, rest = [], TWO_PI
    for step in (2.0 ** -5, 2.0 ** -14):
        part = math.floor(rest / step) * step
        parts.append(part)
        rest -= part
    return parts + [rest]


A_SLOTS, B_SLOTS = 4, 4
A_SIZE, B_SIZE = 4096, 2048
A_U, A_Q, A_TAIL, A_G, A_GLU, A_AP, A_OUT = 0, 1, 2, 3, 7, 9, 10
A_MIX = 12
A_FIRST = A_MIX // A_SLOTS
OWN_PAIR = 2
A_USES = [A_FIRST + NPAIR // 2] * 2 + [A_FIRST + NPAIR // 2 - 1] * 2
assert A_MIX % A_SLOTS == 0


def bc(ap, axis, n):
    ap = ap.unsqueeze(axis)
    shape = list(ap.shape)
    shape[axis] = n
    return ap.broadcast_to(shape)


class Count:

    def __init__(self):
        self.n = 0

    def add(self):
        self.n += 1
        return 1


def build(nc, t, out):
    ctx = ExitStack()
    with ctx:
        def sb(name, shape, dt=F32):
            return ctx.enter_context(nc.sbuf_tensor(name, shape, dt))

        loaded_a = [ctx.enter_context(nc.semaphore(f"loaded_a{i}")) for i in range(A_SLOTS)]
        free_a = [ctx.enter_context(nc.semaphore(f"free_a{i}")) for i in range(A_SLOTS)]
        loaded_b = [ctx.enter_context(nc.semaphore(f"loaded_b{i}")) for i in range(B_SLOTS)]
        free_b = [ctx.enter_context(nc.semaphore(f"free_b{i}")) for i in range(B_SLOTS)]
        layer_left = ctx.enter_context(nc.semaphore("layer_left"))
        counted = ctx.enter_context(nc.semaphore("counted"))
        layer_open = ctx.enter_context(nc.semaphore("layer_open"))
        held = ctx.enter_context(nc.semaphore("held"))
        first_angle_ready = ctx.enter_context(nc.semaphore("first_angle_ready"))
        first_constants = ctx.enter_context(nc.semaphore("first_constants"))
        first_decay_ready = ctx.enter_context(nc.semaphore("first_decay_ready"))
        first_dt_ready = ctx.enter_context(nc.semaphore("first_dt_ready"))
        first_dt_wide = ctx.enter_context(nc.semaphore("first_dt_wide"))
        first_dve_chain = ctx.enter_context(nc.semaphore("first_dve_chain"))
        first_half_sine = ctx.enter_context(nc.semaphore("first_half_sine"))
        first_params_loaded = ctx.enter_context(nc.semaphore("first_params_loaded"))
        first_params_turned = ctx.enter_context(nc.semaphore("first_params_turned"))
        first_pool_chain = ctx.enter_context(nc.semaphore("first_pool_chain"))
        first_positions_loaded = ctx.enter_context(nc.semaphore("first_positions_loaded"))
        first_result_ready = ctx.enter_context(nc.semaphore("first_result_ready"))
        first_rho_ready = ctx.enter_context(nc.semaphore("first_rho_ready"))
        first_stored = ctx.enter_context(nc.semaphore("first_stored"))
        first_theta_turned = ctx.enter_context(nc.semaphore("first_theta_turned"))
        first_x_loaded = ctx.enter_context(nc.semaphore("first_x_loaded"))
        per_layer = []

        def of_layer(name):
            per_layer.append(ctx.enter_context(nc.semaphore(name)))
            return per_layer[-1]

        gains_loaded = of_layer("gains_loaded")
        head_gains_loaded = of_layer("head_gains_loaded")
        nope_gains_loaded = of_layer("nope_gains_loaded")
        b_loaded = of_layer("b_loaded")
        c_loaded = of_layer("c_loaded")
        d_loaded = of_layer("d_loaded")
        router_loaded = of_layer("router_loaded")
        dve_chain = of_layer("dve_chain")
        pool_chain = of_layer("pool_chain")
        squares = of_layer("squares")
        row_scales_ready = of_layer("row_scales_ready")
        scale_row_psum = of_layer("scale_row_psum")
        scale_row_sbuf = of_layer("scale_row_sbuf")
        hT_psum = of_layer("hT_psum")
        hT_sbuf = of_layer("hT_sbuf")
        u_psum = of_layer("u_psum")
        u_sbuf = of_layer("u_sbuf")
        qkv_psum = of_layer("qkv_psum")
        qkv_sbuf = of_layer("qkv_sbuf")
        lora_squares = of_layer("lora_squares")
        lora_ready = of_layer("lora_ready")
        loraT_psum = of_layer("loraT_psum")
        loraT_sbuf = of_layer("loraT_sbuf")
        q_psum = of_layer("q_psum")
        kv_psum = of_layer("kv_psum")
        q_sbuf = of_layer("q_sbuf")
        v_sbuf = of_layer("v_sbuf")
        k_sbuf = of_layer("k_sbuf")
        qk_squares = of_layer("qk_squares")
        qk_ready = of_layer("qk_ready")
        qkT_psum = of_layer("qkT_psum")
        qkT_sbuf = of_layer("qkT_sbuf")
        scores_psum = of_layer("scores_psum")
        row_max_ready = of_layer("row_max_ready")
        row_sum_inverted = of_layer("row_sum_inverted")
        probs_exp = of_layer("probs_exp")
        probs_ready = of_layer("probs_ready")
        probsT_psum = of_layer("probsT_psum")
        probsT_sbuf = of_layer("probsT_sbuf")
        o_psum = of_layer("o_psum")
        o_sbuf = of_layer("o_sbuf")
        b_scaled = of_layer("b_scaled")
        ssm_wT_psum = of_layer("ssm_wT_psum")
        ssm_b_sbuf = of_layer("ssm_b_sbuf")
        ssm_c_sbuf = of_layer("ssm_c_sbuf")
        key_shared = of_layer("key_shared")
        table_ready = of_layer("table_ready")
        bu_psum = of_layer("bu_psum")
        modulated = of_layer("modulated")
        turned_back = of_layer("turned_back")
        y_used = of_layer("y_used")
        y_psum = of_layer("y_psum")
        gelu_arg = of_layer("gelu_arg")
        gelu_tanh = of_layer("gelu_tanh")
        gelu_ready = of_layer("gelu_ready")
        gates_psum = of_layer("gates_psum")
        gates_sbuf = of_layer("gates_sbuf")
        glu_psum = of_layer("glu_psum")
        glu_gate_tanh = of_layer("glu_gate_tanh")
        glu_read = of_layer("glu_read")
        attn_proj_psum = of_layer("attn_proj_psum")
        merged_ready = of_layer("merged_ready")
        mergedT_psum = of_layer("mergedT_psum")
        mergedT_sbuf = of_layer("mergedT_sbuf")
        out_psum = of_layer("out_psum")
        x_mixed = of_layer("x_mixed")
        squares2 = of_layer("squares2")
        h2T_psum = of_layer("h2T_psum")
        h2T_sbuf = of_layer("h2T_sbuf")
        h2T_sbuf_second = of_layer("h2T_sbuf_second")
        logits_psum = of_layer("logits_psum")
        expo_ready = of_layer("expo_ready")
        routes_ready = of_layer("routes_ready")
        picked = of_layer("picked")
        rank_psum = of_layer("rank_psum")
        perm_ready = of_layer("perm_ready")
        offsets_ready = of_layer("offsets_ready")
        sorted_psum = of_layer("sorted_psum")
        sorted_sbuf = of_layer("sorted_sbuf")
        residual_psum = of_layer("residual_psum")
        pair_copied = of_layer("pair_copied")
        hidden_psum = of_layer("hidden_psum")
        gate_tanh_ready = of_layer("gate_tanh_ready")
        hidden_half = of_layer("hidden_half")
        hidden_ready = of_layer("hidden_ready")
        sel_half = of_layer("sel_half")
        sel_ready = of_layer("sel_ready")
        turned_psum = of_layer("turned_psum")
        hiddenT_sbuf = of_layer("hiddenT_sbuf")
        selT_sbuf = of_layer("selT_sbuf")
        down_psum = of_layer("down_psum")
        down_sbuf_lo = of_layer("down_sbuf_lo")
        down_sbuf_hi = of_layer("down_sbuf_hi")
        own_pair_loaded = of_layer("own_pair_loaded")
        moe_psum = of_layer("moe_psum")
        x_ready = of_layer("x_ready")
        rank_shifted = of_layer("rank_shifted")
        more_free = of_layer("more_free")
        more_loaded = of_layer("more_loaded")
        nums = [s.num for s in per_layer]
        assert nums == list(range(nums[0], nums[0] + len(nums))), nums
        x = sb("x", [P, TT, D])
        hT = sb("hT", [P, KC, SEQ])
        ringA = sb("ringA", [P, A_SLOTS, A_SIZE])
        ringB = sb("ringB", [P, B_SLOTS, B_SIZE])
        ident = sb("ident", [P, P])
        before = sb("before", [P, P])
        ones = sb("ones", [P, P])
        iota = sb("iota", [P, NPOS])
        own_group = sb("own_group", [P, 2 * GRP])
        amask = sb("amask", [P, CHUNK])
        cossin = sb("cossin", [P, 2, 2 * STILES + TT * HALF])
        rope = cossin[:, :, 2 * STILES:].rearrange("p i (t f) -> p i t f", t=TT)
        inv_freq = sb("inv_freq", [P, HALF])
        ssm_par = sb("ssm_par", [P, DEPTH, 3, STILES])
        ssm_now = sb("ssm_now", [P, 3, STILES])
        turn_lo = sb("turn_lo", [P, DEPTH, 2, STILES, 16])
        turn_hi = sb("turn_hi", [P, DEPTH, 2, STILES, 16])
        bT = sb("bT", [P, 2, CH_T, P])
        cT = sb("cT", [P, 3, CH_T, P])
        gains = sb("gains", [P, 2 * KC + QC + KVC])
        g_mix, g_ffn = gains[:, 0:KC], gains[:, KC:2 * KC]
        g_q, g_kv = gains[:, 2 * KC:2 * KC + QC], gains[:, 2 * KC + QC:]
        dskip = sb("dskip", [P, CH_T])
        wroute = sb("wroute", [P, KC, ROUTE])
        head_gain = sb("head_gain", [P, 2, ROPE])
        turn_gain = sb("turn_gain", [P, 2, TT, 2, ROPE])
        nope_gain = sb("nope_gain", [P, 2])
        norm = sb("norm", [P, 8, 32])

        ARENA = 21312
        arena = sb("arena", [P, ARENA])

        def at(lo, *shape):
            n = int(np.prod(shape))
            assert lo + n <= ARENA
            ap = arena[:, lo:lo + n]
            names = "abcd"[:len(shape)]
            if len(shape) > 1:
                ap = ap.rearrange(f"p ({' '.join(names)}) -> p {' '.join(names)}", **dict(zip(names, shape)))
            return ap

        gate_t = at(0, TT, 2 * D)
        uT = at(4096, CH_T, SEQ)
        qkv = at(5120, TT, U0)
        vtok = at(6464, TT, HEADS, VD)
        oT = at(5120, HEADS // 2, SEQ)
        tab_v = at(7488, 2, SEQ)
        garg = at(8000, SEQ)
        gtmp = at(8256, SEQ)
        turn = at(8512, 2, 2, SEQ)
        mulc = at(9536, 2, SEQ)
        muls = at(10048, 2, SEQ)
        driven = at(10560, 2, SEQ)
        state = at(11072, 2, SEQ)
        tab_u = at(11584, 2, SEQ)
        backc = at(12096, 2, 2, SEQ)
        backs = at(13120, 2, 2, SEQ)
        turn_tmp = at(20288, 4, DEPTH, STILES, 8)
        praw = at(17216, 3, P)
        dtraw = at(17600, 2)
        ppar = at(17604, 3, DEPTH * STILES)
        pang = at(17700, 4, 2 * STILES + TT * HALF)
        pwork = at(17956, 8, DEPTH * STILES)
        pos_f = at(18212, TT)
        braw = at(8512, 2, STILES, GRP)
        bbar = at(9024, 2, STILES, GRP)
        btmp = at(9536, 2, STILES, GRP)
        bwide = at(10048, 2, STILES, 2 * GRP)
        craw = at(12096, 2, CH_T, 2, NST)
        squared = at(14144, TT, D)
        diag = at(16192, TT, P)
        scale_row = at(16448, SEQ)
        qk = at(14144, TT, 2 * HEADS, QKD)
        qkT = at(17216, 2, 4, SEQ)
        lora = at(17216, TT, U0)
        loraT = at(18560, QC + KVC, SEQ)
        sq = at(17216, TT, 2 * HEADS, QKD)
        probs = at(19264, 4, SEQ)
        probsT = at(20288, 4, 2, P)
        glu_t = at(14144, TT, D)
        merged = at(16192, TT, D)
        attn_m = at(18240, D)
        squared2 = at(8960, TT, D)
        perm2 = hT[:, 0:2 * TT, :].rearrange("p (t c) s -> p t (c s)", t=TT)
        own_pair = at(13120, 2, A_SIZE)
        sortedT = at(0, KC, NPOS + SLOT)
        pairT = at(4608, 2, KC, 2 * SLOT)
        gtanh = at(6656, 2, DE)
        hidden = at(7168, 2, DE)
        hiddenT = at(7680, 2, P)
        sel = at(7936, 2, TT, 2 * SLOT)
        selT = at(8448, 2, SEQ)
        down = at(8960, D)
        perm = at(9984, TT, NPOS)
        rt = at(11008, 24, TT, NE)
        roff = sb("roff", [P, PASSES, NE], I32)
        rmany = sb("rmany", [P, DEPTH], I32)
        pos_i = sb("pos_i", [P, TT], I32)
        logits = at(12544, TT, ROUTE)
        expo_in = at(12624, TT, EG + 1)
        expo = at(12640, TT, EG + 1)
        r8 = at(12656, 10, TT, EPG)
        r4 = at(12816, 4, TT, EG)
        r1 = at(12848, 16, TT)
        count = at(12880, 3, NE)

        psum = ctx.enter_context(nc.psum_tensor("psum", [P, 8, 512], F32))

        def bank(i, lo=0, hi=512):
            return psum[:, i, lo:hi]

        def banks(i, n):
            return psum[:, i:i + n, :].rearrange("p b n -> p (b n)")

        w_in = t["w_in"].rearrange("l (p c) n -> l p c n", c=KC)
        w_uq = t["w_uq"].rearrange("l (p c) n -> l p c n", c=QC)
        w_ukv = t["w_ukv"].rearrange("l (p c) n -> l p c n", c=KVC)
        w_ap = t["w_attn_proj"].rearrange("l (c p) n -> l p c n", p=P)
        w_glu = t["w_glu"].rearrange("l (c p) n -> l p c n", p=P)
        w_out = t["w_out"].rearrange("l (p c) n -> l p c n", c=KC)
        w_gate = t["w_exp_gate"].rearrange("l e (p c) n -> (l e) p (c n)", c=KC)
        w_up = t["w_exp_up"].rearrange("l e (p c) n -> (l e) p (c n)", c=KC)
        w_down = t["w_exp_down"].rearrange("l e (p c) n -> (l e) p (c n)", c=2)

        def layer_of(ap, l):
            ap = ap[bass.ds(l, 1)]
            names = " ".join("bcdef"[:ap.ndim - 1])
            first_, rest = names.split(" ", 1) if " " in names else (names, "")
            return ap.rearrange(f"a {names} -> (a {first_}) {rest}")

        def slotA(a):
            return ringA[:, a % A_SLOTS, :]

        def slotA_kc(a):
            return slotA(a).rearrange("p (c n) -> p c n", c=KC)

        wtail = slotA(A_TAIL)[:, 0:KC * (U0 - 512)].rearrange("p (c n) -> p c n", c=KC)
        wuq = slotA(A_TAIL)[:, KC * (U0 - 512):KC * (U0 - 512) + QC * HEADS * QKD].rearrange("p (c n) -> p c n", c=QC)
        wukv = ringB[:, 0, :].rearrange("p (c n) -> p c n", c=KVC)

        def b_use(l, s, it):
            per = NE // B_SLOTS
            return l * (per + 1) + it + 1 if s == 0 else l * per + it

        def leave_layer(eng, l, clears=False):
            eng.drain().then_inc(layer_left, 1)
            if clears:
                eng.wait_ge(layer_left, l * 4 + 4)
                eng.sem_inc(held, 1)
                eng.sem_clear(range(nums[0], nums[-1] + 1))
                eng.drain().then_inc(layer_open, 1)
            eng.wait_ge(layer_open, l + 2)
            eng.sem_inc(held, 1)

        def crowded(eng, l):
            eng.wait_ge(counted, l + 1)
            eng.sem_inc(held, 1)
            return eng.value_load(rmany[0:1, bass.ds(l, 1)], min_val=0, max_val=1)

        def further_steps(eng, step, each_pass=None):
            with eng.Fori(1, PASSES) as r:
                if each_pass:
                    each_pass(r)
                with eng.Fori(0, NPAIR) as pair:
                    step(r * NPAIR + pair, pair, r)

        block = ctx.enter_context(nc.Block())

        @block.sync
        def _(sp):
            for tt in range(TT):
                sp.dma_start(x[:, tt, :], t["x"][0, tt * P:(tt + 1) * P, :]).then_inc(first_x_loaded, 16)
            with sp.Fori(0, DEPTH) as l:
                layer_at = {k: layer_of(v, l) for k, v in (("in", w_in), ("uq", w_uq), ("ukv", w_ukv),
                                                           ("ap", w_ap), ("glu", w_glu), ("out", w_out))}

                def load_a(a, dst0, src0, dst1, src1):
                    s = a % A_SLOTS
                    sp.wait_ge(free_a[s], l * A_USES[s] + a // A_SLOTS + 1)
                    sp.sem_inc(held, 1)
                    sp.dma_start(dst0, src0).then_inc(loaded_a[s], 16)
                    sp.dma_start(dst1, src1).then_inc(loaded_a[s], 16)

                def load_a_cols(a, w, c0):
                    v = slotA_kc(a)
                    load_a(a, v[:, 0:KC // 2, :], w[:, 0:KC // 2, c0:c0 + 512],
                           v[:, KC // 2:KC, :], w[:, KC // 2:KC, c0:c0 + 512])

                load_a_cols(A_U, layer_at["in"], U0)
                load_a_cols(A_Q, layer_at["in"], 0)
                load_a(A_TAIL, wtail, layer_at["in"][:, :, 512:U0], wuq, layer_at["uq"])
                sp.wait_ge(free_b[0], l * (NE // B_SLOTS + 1) + 1)
                sp.sem_inc(held, 1)
                sp.dma_start(wukv, layer_at["ukv"]).then_inc(loaded_b[0], 16)
                load_a_cols(A_G, layer_at["in"], G0)
                sp.wait_ge(layer_open, l + 1)
                sp.sem_inc(held, 1)
                def vec(ap, cc):
                    return ap[bass.ds(l, 1), :].rearrange("a (p c) -> (a p) c", c=cc)

                sp.dma_start(g_mix, vec(t["norm_mix_g"], KC)).then_inc(gains_loaded, 16)
                sp.dma_start(g_ffn, vec(t["norm_ffn_g"], KC)).then_inc(gains_loaded, 16)
                sp.dma_start(g_q, vec(t["q_lora_g"], QC)).then_inc(gains_loaded, 16)
                sp.dma_start(g_kv, vec(t["kv_lora_g"], KVC)).then_inc(gains_loaded, 16)
                for i, k in enumerate(("b_re", "b_im")):
                    sp.dma_start(braw[:, i, :, :], layer_of(t[k], l).rearrange("(j g) p i -> (g p) j i", g=2)).then_inc(b_loaded, 16)
                for i, k in enumerate(("c_re", "c_im")):
                    for half in range(2):
                        sp.dma_start(craw[:, i, :, half, :], layer_of(t[k], l).rearrange("(m g) i p -> (g i) m p", m=CH_T)).then_inc(c_loaded, 16)
                sp.dma_start(dskip[:, :], layer_of(t["d_skip"], l).rearrange("(m g) i -> (g i) m", m=CH_T), allow_slow_non_contiguous=True).then_inc(d_loaded, 16)
                for i, k in enumerate(("q_head_g", "k_head_g")):
                    g = t[k][bass.ds(l, 1), :]
                    sp.dma_start(head_gain[:, i, :], g[:, NOPE:].broadcast_to([P, ROPE])).then_inc(head_gains_loaded, 16)
                    sp.dma_start(nope_gain[0:NOPE, i:i + 1], g[:, 0:NOPE].rearrange("a n -> n a"),
                                 allow_slow_non_contiguous=True).then_inc(nope_gains_loaded, 16)
                sp.dma_start(wroute[:, :, 0:EG], layer_of(t["w_router_group"], l).rearrange("(p c) n -> p c n", c=KC)).then_inc(router_loaded, 16)
                sp.dma_start(wroute[:, :, EG:], layer_of(t["w_router_expert"], l).rearrange("(p c) n -> p c n", c=KC)).then_inc(router_loaded, 16)
                for g in range(1, 4):
                    load_a_cols(A_G + g, layer_at["in"], G0 + g * 512)
                for g in range(2):
                    v = slotA(A_GLU + g).rearrange("p (c n) -> p c n", c=CH_T)
                    src = layer_at["glu"][:, :, (1 - g) * D:(2 - g) * D]
                    load_a(A_GLU + g, v[:, 0:2, :], src[:, 0:2, :], v[:, 2:4, :], src[:, 2:4, :])
                v = slotA(A_AP).rearrange("p (c n) -> p c n", c=CH_T)
                load_a(A_AP, v[:, 0:2, :], layer_at["ap"][:, 0:2, :], v[:, 2:4, :], layer_at["ap"][:, 2:4, :])
                for g in range(2):
                    load_a_cols(A_OUT + g, layer_at["out"], g * 512)

                def expert(w, pair, e):
                    return w[bass.ds(l * NE + pair * 2 + e, 1)].rearrange("a p n -> (a p) n")

                def load_gate_up(pair, ring, n):
                    for e in range(2):
                        s = 2 * ring + e
                        sp.wait_ge(free_a[s], l * A_USES[s] + n + 1)
                        sp.sem_inc(held, 1)
                        sp.dma_start(ringA[:, s, 0:2048], expert(w_gate, pair, e)).then_inc(loaded_a[s], 16)
                        sp.dma_start(ringA[:, s, 2048:4096], expert(w_up, pair, e)).then_inc(loaded_a[s], 16)

                def load_down(pair, ring, n):
                    for e in range(2):
                        s = 2 * ring + e
                        sp.wait_ge(free_b[s], b_use(l, s, n) + 1)
                        sp.sem_inc(held, 1)
                        sp.dma_start(ringB[:, s, :], expert(w_down, pair, e)).then_inc(loaded_b[s], 16)

                for pair in range(2):
                    load_gate_up(pair, pair, A_FIRST)
                    load_down(pair, pair, 0)
                sp.wait_ge(mergedT_psum, 2 * TT)
                for e in range(2):
                    sp.dma_start(own_pair[:, e, 0:2048], expert(w_gate, OWN_PAIR, e)).then_inc(own_pair_loaded, 16)
                    sp.dma_start(own_pair[:, e, 2048:4096], expert(w_up, OWN_PAIR, e)).then_inc(own_pair_loaded, 16)
                with sp.Fori(0, NPAIR // 2 - 2) as i:
                    for ring in range(2):
                        load_gate_up(i * 2 + 3 + ring, ring, i + A_FIRST + 1)
                        load_down(i * 2 + 2 + ring, ring, i + 1)
                load_gate_up(NPAIR - 1, 0, A_USES[0] - 1)
                for ring in range(2):
                    load_down(NPAIR - 2 + ring, ring, NPAIR // 2 - 1)

                def reload(p, pair, r):
                    sp.wait_ge(more_free, p - (NPAIR - 1))
                    sp.sem_inc(held, 1)
                    e0 = sp.snap(l * NE + pair * 2)
                    for s in range(2):
                        src = [w[bass.ds(e0 + s, 1)].rearrange("a p n -> (a p) n") for w in (w_gate, w_up, w_down)]
                        sp.dma_start(ringA[:, s, 0:2048], src[0]).then_inc(more_loaded, 16)
                        sp.dma_start(ringA[:, s, 2048:4096], src[1]).then_inc(more_loaded, 16)
                        sp.dma_start(ringB[:, s, :], src[2]).then_inc(more_loaded, 16)

                with sp.If(crowded(sp, l) > 0):
                    further_steps(sp, reload)
                    sp.wait_ge(layer_open, l + 2)
                    sp.sem_inc(held, 1)
            for tt in range(TT):
                sp.wait_ge(first_result_ready, tt + 1)
                sp.dma_start(out[0, tt * P:(tt + 1) * P, :], x[:, tt, :]).then_inc(first_stored, 16)
            sp.wait_ge(first_stored, 16 * TT)

        @block.gpsimd
        def _(pool):
            pool.memset(ident[:, :], 0.0).then_inc(first_constants, 1)
            pool.memset(before[:, :], 1.0).then_inc(first_constants, 1)
            pool.memset(ones[:, :], 1.0).then_inc(first_constants, 1)
            pool.memset(own_group[:, :], 1.0).then_inc(first_constants, 1)
            pool.memset(amask[:, :], 0.0).then_inc(first_constants, 1)
            pool.memset(nope_gain[:, :], 1.0).then_inc(first_constants, 1)
            for j in range(HALF):
                pool.memset(inv_freq[:, j:j + 1], float(np.float32(THETA) ** np.float32(-j / HALF))).then_inc(first_constants, 1)
            pool.iota(iota[:, :], pattern=[[1, NPOS]], base=0, channel_multiplier=0,
                      allow_small_or_imprecise_dtypes=True).then_inc(first_constants, 1)
            n = 7 + HALF
            pool.wait_ge(first_constants, n)
            pool.sem_inc(layer_open, 1)
            pool.affine_select(out=ident[:, :], in_=ident[:, :], compare_op=ALU.not_equal, fill=1.0, base=0,
                               pattern=[[-1, P]], channel_multiplier=1).then_inc(first_constants, 1)
            pool.affine_select(out=before[:, :], in_=before[:, :], compare_op=ALU.is_gt, fill=0.0, base=0,
                               pattern=[[1, P]], channel_multiplier=-1).then_inc(first_constants, 1)
            pool.affine_select(out=own_group[:, 0:GRP], in_=own_group[:, 0:GRP], compare_op=ALU.is_ge, fill=0.0,
                               base=NST - 1, pattern=[[0, GRP]], channel_multiplier=-1).then_inc(first_constants, 1)
            pool.affine_select(out=own_group[:, GRP:], in_=own_group[:, GRP:], compare_op=ALU.is_ge, fill=0.0,
                               base=-NST, pattern=[[0, GRP]], channel_multiplier=1).then_inc(first_constants, 1)
            pool.affine_select(out=amask[:, :], in_=amask[:, :], compare_op=ALU.is_ge,
                               fill=MASKED, base=-CHUNK, pattern=[[0, CHUNK]], channel_multiplier=1).then_inc(first_constants, 1)

            done = Count()

            def shape(ap, n):
                return ap if n == 1 else ap.broadcast_to([P, DEPTH, STILES, n])

            def cmul(oc, os, a, b, n):
                tmp = [turn_tmp[:, i, :, :, 0:n] for i in range(4)]
                bcs = [shape(v, n) for v in b]
                pool.tensor_tensor(tmp[0], a[0], bcs[0], ALU.mult).then_inc(first_pool_chain, done.add())
                pool.tensor_tensor(tmp[1], a[1], bcs[1], ALU.mult).then_inc(first_pool_chain, done.add())
                pool.tensor_tensor(tmp[2], a[0], bcs[1], ALU.mult).then_inc(first_pool_chain, done.add())
                pool.tensor_tensor(tmp[3], a[1], bcs[0], ALU.mult).then_inc(first_pool_chain, done.add())
                pool.wait_ge(first_pool_chain, done.n)
                pool.tensor_tensor(oc, tmp[0], tmp[1], ALU.subtract).then_inc(first_pool_chain, done.add())
                pool.tensor_tensor(os, tmp[2], tmp[3], ALU.add).then_inc(first_pool_chain, done.add())
                pool.wait_ge(first_pool_chain, done.n)

            def parts(tab, b0, b1):
                return [tab[:, :, i, :, b0:b1] for i in range(2)]

            pool.wait_ge(first_theta_turned, 2)
            for tab in (turn_lo, turn_hi):
                for i in range(2):
                    pool.memset(tab[:, :, i, :, 0:1], 1.0 - i).then_inc(first_pool_chain, done.add())
            for i in range(2):
                pool.tensor_copy(turn_lo[:, :, i, :, 1:2], cossin[:, i, 0:2 * STILES].rearrange("p (l j o) -> p l j o", l=DEPTH, o=1)).then_inc(first_pool_chain, done.add())
            pool.wait_ge(first_pool_chain, done.n)
            for k, tab in enumerate((turn_lo, turn_hi)):
                for n in (2, 4, 8):
                    oc, os = parts(tab, n, n + 1)
                    cmul(oc, os, parts(tab, n // 2, n // 2 + 1), parts(tab, n // 2, n // 2 + 1), 1)
                    oc, os = parts(tab, n + 1, 2 * n)
                    cmul(oc, os, parts(tab, 1, n), parts(tab, n, n + 1), n - 1)
                if k == 0:
                    oc, os = parts(turn_hi, 1, 2)
                    cmul(oc, os, parts(tab, 8, 9), parts(tab, 8, 9), 1)

            with pool.Fori(0, DEPTH) as l:
                done = Count()

                lo = turn_lo[:, bass.ds(l, 1)].rearrange("p l i j b -> p (l i) j b")
                hi = turn_hi[:, bass.ds(l, 1)].rearrange("p l i j b -> p (l i) j b")
                for j in range(STILES):
                    if j == 0:
                        pool.wait_ge(ssm_wT_psum, 4)
                    if j >= 2:
                        pool.wait_ge(turned_back, j - 1)
                    a = bc(hi[:, :, j, :], 3, 16)
                    for k, dst in enumerate((tab_u, tab_v)):
                        b = bc(bc(lo[:, k, j, :], 1, 16), 1, 2)
                        pool.tensor_tensor(dst.rearrange("p i (a b) -> p i a b", b=16), a, b, ALU.mult).then_inc(pool_chain, done.add())
                    pool.wait_ge(pool_chain, done.n)
                    pool.tensor_tensor(turn[:, j % 2, 0, :], tab_u[:, 0, :], tab_v[:, 1, :],
                                       ALU.subtract).then_inc(table_ready, 1)
                    pool.tensor_tensor(turn[:, j % 2, 1, :], tab_u[:, 1, :], tab_v[:, 0, :],
                                       ALU.add).then_inc(table_ready, 1)
                    pool.wait_ge(table_ready, 2 * j + 2)

                pool.wait_ge(offsets_ready, 1 + PASSES)

                def copy_pair(p, par, first_uses):
                    offs = [pool.value_load(roff[0:1, 0, bass.ds(p * 2 + i, 1)], min_val=0, max_val=NPOS) for i in range(2)]
                    if first_uses:
                        pool.wait_ge(sorted_sbuf, KC)
                    else:
                        pool.wait_ge(hidden_psum, p - 1)
                        pool.sem_inc(held, 1)
                    for i, off in enumerate(offs):
                        pool.tensor_copy(pairT[:, par, :, i * SLOT:(i + 1) * SLOT],
                                         sortedT[:, :, bass.ds(off, SLOT)]).then_inc(pair_copied, 1)

                offs = [pool.value_load(roff[0:1, 0, i:i + 1], min_val=0, max_val=NPOS) for i in range(2)]
                for c in range(0, KC, 2):
                    pool.wait_ge(sorted_sbuf, c + 2)
                    for i, off in enumerate(offs):
                        last = pool.tensor_copy(pairT[:, 0, c:c + 2, i * SLOT:(i + 1) * SLOT], sortedT[:, c:c + 2, bass.ds(off, SLOT)])
                        if c == KC - 2:
                            last.then_inc(pair_copied, 1)
                copy_pair(1, 1, True)
                with pool.Fori(1, NPAIR // 2) as i:
                    for par in range(2):
                        copy_pair(i * 2 + par, par, False)

                def copy_more(p, pair, r):
                    pool.wait_ge(x_ready, (p - (NPAIR - 1)) * TT)
                    pool.sem_inc(held, 1)
                    for i in range(2):
                        off = pool.value_load(roff[0:1, bass.ds(r, 1), bass.ds(pair * 2 + i, 1)], min_val=0, max_val=NPOS)
                        pool.tensor_copy(pairT[:, 0, :, i * SLOT:(i + 1) * SLOT],
                                         sortedT[:, :, bass.ds(off, SLOT)]).then_inc(pair_copied, 1)

                with pool.If(crowded(pool, l) > 0):
                    further_steps(pool, copy_more)
                leave_layer(pool, l, clears=True)

        @block.scalar
        def _(act):
            act.dma_start(praw[0:2 * STILES, 0, :], t["lam_re"].rearrange("l (j g) p -> (l j) (g p)", g=2)).then_inc(first_params_loaded, 16)
            act.dma_start(praw[0:2 * STILES, 1, :], t["lam_im"].rearrange("l (j g) p -> (l j) (g p)", g=2)).then_inc(first_params_loaded, 16)
            act.dma_start(dtraw[0:2 * STILES, :], t["log_dt"].rearrange("l (j g) -> (l j) g", g=2)).then_inc(first_params_loaded, 16)
            act.dma_start(pos_i[:, :], t["positions"].rearrange("b (t p) -> p (b t)", p=P),
                          allow_slow_non_contiguous=True).then_inc(first_positions_loaded, 16)
            act.wait_ge(first_params_loaded, 48)
            act.activation(dtraw[0:2 * STILES, :], dtraw[0:2 * STILES, :], ACT.Exp).then_inc(first_dt_ready, 1)
            act.wait_ge(first_decay_ready, 1)
            act.activation(pwork[:, 0, :], pwork[:, 1, :], ACT.Exp).then_inc(first_rho_ready, 1)
            act.wait_ge(first_angle_ready, 1)
            act.activation(cossin[:, 1, :], pang[:, 0, :], ACT.Sin).then_inc(first_theta_turned, 1)
            act.activation(pang[:, 3, :], pang[:, 0, :], ACT.Sin, scale=0.5).then_inc(first_half_sine, 1)

            with act.Fori(0, DEPTH) as l:
                act.wait_ge(gains_loaded, 64)
                for c in range(KC):
                    act.wait_ge(hT_psum, c // 2 + 1)
                    act.activation(hT[:, c, :], bank(c // 2 % 2, c % 2 * SEQ, c % 2 * SEQ + SEQ), ACT.Copy,
                                   scale=g_mix[:, c:c + 1]).then_inc(hT_sbuf, 1)
                act.wait_ge(first_x_loaded, 16 * TT)
                for tt in range(TT):
                    act.activation(squared[:, tt, :], x[:, tt, :], ACT.Square, scale=D ** -0.5, accum_out=norm[:, 0, tt:tt + 1]).then_inc(squares, 1)
                for i in range(2):
                    act.wait_ge(ssm_wT_psum, i + 1)
                    act.activation(bT[:, i, :, :], bank(2 + i).rearrange("p (m s) -> p m s", m=CH_T), ACT.Copy).then_inc(ssm_b_sbuf, 1)

                def lora_norm():
                    for tt in range(TT):
                        act.wait_ge(qkv_sbuf, 2 * tt + 2)
                        act.activation(lora[:, tt, 0:QR], qkv[:, tt, 0:QR], ACT.Square, scale=QR ** -0.5, accum_out=norm[:, 2, tt:tt + 1]).then_inc(lora_squares, 1)
                        act.activation(lora[:, tt, QR:QR + KVR], qkv[:, tt, QR:QR + KVR], ACT.Square, scale=KVR ** -0.5, accum_out=norm[:, 2, TT + tt:TT + tt + 1]).then_inc(lora_squares, 1)

                def lora_turn():
                    for c in range(QC + KVC):
                        act.wait_ge(loraT_psum, c + 1)
                        g = g_q[:, c:c + 1] if c < QC else g_kv[:, c - QC:c - QC + 1]
                        act.activation(loraT[:, c, :], bank(6 + c % 2, 0, SEQ), ACT.Copy, scale=g).then_inc(loraT_sbuf, 1)

                def q_out(tt):
                    act.wait_ge(q_psum, tt + 1)
                    for i in range(2):
                        act.activation(qk[:, tt, 4 * i:4 * i + 4, :], bank(6 + i, 0, 4 * QKD).rearrange("p (h d) -> p h d", h=4),
                                       ACT.Copy).then_inc(q_sbuf, 1)

                def kv_out(tt):
                    act.wait_ge(kv_psum, tt + 1)
                    for i in range(2):
                        src = bank(6 + i).rearrange("p (h d) -> p h d", h=4)
                        act.activation(qk[:, tt, HEADS + 4 * i:HEADS + 4 * i + 4, 0:NOPE], src[:, :, 0:NOPE], ACT.Copy).then_inc(k_sbuf, 1)
                        act.activation(vtok[:, tt, 4 * i:4 * i + 4, :], src[:, :, NOPE:], ACT.Copy).then_inc(v_sbuf, 1)

                def qk_square():
                    act.wait_ge(k_sbuf, 4)
                    act.wait_ge(key_shared, TT)
                    act.wait_ge(q_sbuf, 4)
                    for tt in range(TT):
                        act.activation(sq[:, tt, :, :], qk[:, tt, :, :], ACT.Square, scale=QKD ** -0.5).then_inc(qk_squares, 1)

                def qkT_out(hg):
                    act.wait_ge(nope_gains_loaded, 32)
                    for i in range(4):
                        n = 4 * hg + i
                        act.wait_ge(qkT_psum, n + 1)
                        act.activation(qkT[0:QKD, i // 2, 2 * (i % 2):2 * (i % 2) + 2, :],
                                       psum[0:QKD, 6 + i % 2, :].rearrange("p (h s) -> p h s", h=2), ACT.Copy,
                                       scale=nope_gain[0:QKD, i // 2:i // 2 + 1]).then_inc(qkT_sbuf, 1)

                def exps(c, qb):
                    w = P * (qb + 1)
                    act.wait_ge(row_max_ready, c + 1)
                    for hh in range(4):
                        act.activation(probs[:, hh, 0:w], banks(6, 2)[:, hh * w:(hh + 1) * w], ACT.Exp, scale=SCALE,
                                       bias=norm[:, 2, 12 + hh:13 + hh],
                                       accum_out=norm[:, 2, 4 + hh:5 + hh]).then_inc(probs_exp, 1)

                def shares(c, qb):
                    w = P * (qb + 1)
                    act.wait_ge(row_sum_inverted, c + 1)
                    for hh in range(4):
                        act.activation(probs[:, hh, 0:w], probs[:, hh, 0:w], ACT.Copy,
                                       scale=norm[:, 2, 8 + hh:9 + hh]).then_inc(probs_ready, 1)

                def probsT_out(c, qb):
                    act.wait_ge(probsT_psum, c + 1)
                    act.activation(probsT[:, :, 0:qb + 1, :],
                                   banks(6, 2)[:, 0:4 * (qb + 1) * P].rearrange("p (h k q) -> p h k q", h=4, k=qb + 1),
                                   ACT.Copy).then_inc(probsT_sbuf, 1)

                def o_out(c, hg, qb):
                    act.wait_ge(o_psum, c + 1)
                    act.activation(oT[:, 2 * hg:2 * hg + 2, qb * P:(qb + 1) * P],
                                   bank(5, 0, 2 * P).rearrange("p (c q) -> p c q", c=2), ACT.Copy).then_inc(o_sbuf, 1)

                def gate(g):
                    act.wait_ge(gates_psum, g + 1)
                    act.wait_ge(row_scales_ready, TT)
                    act.activation(gate_t[:, g % 2, (g // 2) * 512:(g // 2 + 1) * 512], bank(4), ACT.Tanh,
                                   scale=norm[:, 7, 8 + g % 2:9 + g % 2]).then_inc(gates_sbuf, 1)

                def gelu(m):
                    act.wait_ge(gelu_arg, m + 1)
                    act.activation(gtmp, garg, ACT.Tanh, scale=math.sqrt(2.0 / math.pi)).then_inc(gelu_tanh, 1)

                lora_norm()
                for j in range(STILES):
                    for g in GATES_AT.get(j, []):
                        gate(g)
                    attention(j, dict(lora=lora_turn, q=lambda: (q_out(0), q_out(1)),
                                      kv=lambda: (kv_out(0), kv_out(1)), qk=qk_square, turn=qkT_out,
                                      scores=lambda c, hg, qb: exps(c, qb), probs=lambda c, hg, qb: (shares(c, qb), probsT_out(c, qb)),
                                      values=o_out))
                    if j % QPT == 0 and j:
                        gelu(j // QPT - 1)
                gelu(CH_T - 1)

                for tt in range(TT):
                    act.wait_ge(glu_psum, 1 + tt)
                    act.activation(glu_t[:, tt, :], banks(2 + 2 * tt, 2), ACT.Tanh, scale=0.25).then_inc(glu_gate_tanh, 1)
                for tt in range(TT):
                    for i in range(2):
                        act.wait_ge(mergedT_psum, 2 * tt + i + 1)
                        act.activation(hT[:, 4 * i:4 * i + 4, tt * P:(tt + 1) * P],
                                       bank(4 - 2 * tt + i).rearrange("p (c s) -> p c s", c=4), ACT.Copy).then_inc(mergedT_sbuf, 1)

                for tt in range(TT):
                    act.wait_ge(x_mixed, tt + 1)
                    act.activation(squared2[:, tt, :], x[:, tt, :], ACT.Square, scale=D ** -0.5, accum_out=norm[:, 1, tt:tt + 1]).then_inc(squares2, 1)
                    if tt == 0:
                        for c in range(KC):
                            act.wait_ge(h2T_psum, c // 4 + 1)
                            act.activation(hT[:, c, 0:P], bank(4 + c // 4, c % 4 * P, (c % 4 + 1) * P), ACT.Copy,
                                           scale=g_ffn[:, c:c + 1]).then_inc(h2T_sbuf, 1)
                act.wait_ge(picked, 1)
                act.activation(expo, expo_in, ACT.Exp).then_inc(expo_ready, 1)
                for c in range(KC):
                    act.wait_ge(sorted_psum, c + 1)
                    act.activation(sortedT[:, c, 0:NPOS], bank(c % 4), ACT.Copy, scale=g_ffn[:, c:c + 1]).then_inc(sorted_sbuf, 1)

                def gate_tanh(p, par):
                    act.wait_ge(hidden_psum, p + 1)
                    act.sem_inc(held, 1)
                    act.activation(gtanh[:, par, :], bank(par, 0, DE), ACT.Tanh, scale=0.5).then_inc(gate_tanh_ready, 1)

                def turned(p, par):
                    act.wait_ge(turned_psum, p + 1)
                    act.sem_inc(held, 1)
                    act.activation(hiddenT[:, :, :], bank(par, 0, 2 * P).rearrange("p (c s) -> p c s", c=2), ACT.Copy).then_inc(hiddenT_sbuf, 1)

                def down_lo(p):
                    act.wait_ge(down_psum, p + 1)
                    act.sem_inc(held, 1)
                    act.activation(down[:, 0:512], bank(2), ACT.Copy).then_inc(down_sbuf_lo, 1)

                gate_tanh(0, 0)

                def step(p, par, last=False):
                    turned(p, par)
                    down_lo(p)
                    if not last:
                        gate_tanh(p + 1, 1 - par)

                with act.Fori(0, NPAIR // 2 - 1) as i:
                    for par in range(2):
                        step(i * 2 + par, par)
                step(NPAIR - 2, 0)
                step(NPAIR - 1, 1, last=True)

                def more(p, pair, r):
                    gate_tanh(p, 0)
                    turned(p, 0)
                    down_lo(p)

                with act.If(crowded(act, l) > 0):
                    further_steps(act, more)
                leave_layer(act, l)

        @block.vector
        def _(dve):
            TS, TTN, STT = dve.tensor_scalar, dve.tensor_tensor, dve.scalar_tensor_tensor

            def rsqrt(done, dst, src):
                w = src.shape[-1]
                v, y, a = (norm[:, i, 0:w] for i in (4, 5, 6))
                TS(a, src, EPS, None, ALU.add).then_inc(dve_chain, done.add())
                dve.wait_ge(dve_chain, done.n)
                TS(v, a, -0.5, None, ALU.mult).then_inc(dve_chain, done.add())
                TS(y.bitcast(I32), a.bitcast(I32), 1, None, ALU.logical_shift_right).then_inc(dve_chain, done.add())
                dve.wait_ge(dve_chain, done.n)
                TS(y.bitcast(I32), y.bitcast(I32), -1.0, float(0x5F3759DF), ALU.mult, ALU.add).then_inc(dve_chain, done.add())
                dve.wait_ge(dve_chain, done.n)
                for k in range(3):
                    TTN(a, y, y, ALU.mult).then_inc(dve_chain, done.add())
                    dve.wait_ge(dve_chain, done.n)
                    TTN(a, a, v, ALU.mult).then_inc(dve_chain, done.add())
                    dve.wait_ge(dve_chain, done.n)
                    STT(out=dst if k == 2 else y, in0=a, scalar=1.5, in1=y, op0=ALU.add, op1=ALU.mult).then_inc(dve_chain, done.add())
                    dve.wait_ge(dve_chain, done.n)

            done = Count()
            NW = DEPTH * STILES
            dtx = praw[0:NW, 2, :].rearrange("p (g s) -> p g s", g=2)
            dve.wait_ge(first_dt_ready, 1)
            dve.tensor_copy(dtx, bc(dtraw[0:NW, :], 2, NST)).then_inc(first_dt_wide, 1)
            dve.wait_ge(first_params_turned, 1)
            dve.tensor_copy(ppar[:, :, :], bank(7, 0, 3 * NW).rearrange("p (i w) -> p i w", i=3)).then_inc(first_dve_chain, done.add())
            dve.wait_ge(first_dve_chain, done.n)
            re, im, dt = (ppar[:, i, :] for i in range(3))
            TTN(pwork[:, 1, :], re, dt, ALU.mult).then_inc(first_decay_ready, 1)
            TTN(pang[:, 1, 0:NW], im, dt, ALU.mult).then_inc(first_dve_chain, done.add())
            dve.wait_ge(first_positions_loaded, 16)
            dve.tensor_copy(pos_f, pos_i[:, :]).then_inc(first_dve_chain, done.add())
            dve.wait_ge(first_dve_chain, done.n)
            dve.wait_ge(first_constants, 7 + HALF + 5)
            TTN(pang[:, 1, NW:].rearrange("p (t f) -> p t f", t=TT), bc(pos_f, 2, HALF), bc(inv_freq[:, :], 1, TT), ALU.mult).then_inc(first_dve_chain, done.add())
            dve.wait_ge(first_dve_chain, done.n)
            ang, whole, r = pang[:, 1, :], pang[:, 2, :], pang[:, 0, :]
            TS(whole, ang, 1.0 / TWO_PI, ROUND, ALU.mult, ALU.add).then_inc(first_dve_chain, done.add())
            dve.wait_ge(first_dve_chain, done.n)
            TS(whole, whole, ROUND, None, ALU.subtract).then_inc(first_dve_chain, done.add())
            dve.wait_ge(first_dve_chain, done.n)
            src = ang
            for part in split_two_pi():
                STT(out=r, in0=whole, scalar=-part, in1=src, op0=ALU.mult, op1=ALU.add).then_inc(first_dve_chain, done.add())
                dve.wait_ge(first_dve_chain, done.n)
                src = r
            pi = float(np.nextafter(np.float32(math.pi), np.float32(0)))
            TS(r, r, pi, -pi, ALU.min, ALU.max).then_inc(first_angle_ready, 1)
            dve.wait_ge(first_half_sine, 1)
            TTN(pang[:, 2, :], pang[:, 3, :], pang[:, 3, :], ALU.mult).then_inc(first_dve_chain, done.add())
            dve.wait_ge(first_dve_chain, done.n)
            TS(cossin[:, 0, :], pang[:, 2, :], -2.0, 1.0, ALU.mult, ALU.add).then_inc(first_theta_turned, 1)
            dve.wait_ge(first_theta_turned, 2)
            dve.wait_ge(first_rho_ready, 1)
            rho = pwork[:, 0, :]
            lr, li, den, t0, t1 = (pwork[:, i, :] for i in range(2, 7))

            def par_of(i):
                return ssm_par[:, :, i, :]

            def lj(ap):
                return ap.rearrange("p (l j) -> p l j", l=DEPTH)

            dve.tensor_copy(par_of(0), lj(rho)).then_inc(first_dve_chain, done.add())
            TTN(lr, rho, cossin[:, 0, 0:NW], ALU.mult).then_inc(first_dve_chain, done.add())
            TTN(li, rho, cossin[:, 1, 0:NW], ALU.mult).then_inc(first_dve_chain, done.add())
            TTN(t0, re, re, ALU.mult).then_inc(first_dve_chain, done.add())
            TTN(t1, im, im, ALU.mult).then_inc(first_dve_chain, done.add())
            dve.wait_ge(first_dve_chain, done.n)
            TTN(den, t0, t1, ALU.add).then_inc(first_dve_chain, done.add())
            TS(lr, lr, 1.0, None, ALU.subtract).then_inc(first_dve_chain, done.add())
            dve.wait_ge(first_dve_chain, done.n)
            dve.reciprocal(den, den).then_inc(first_dve_chain, done.add())
            TTN(t0, lr, re, ALU.mult).then_inc(first_dve_chain, done.add())
            TTN(t1, li, im, ALU.mult).then_inc(first_dve_chain, done.add())
            dve.wait_ge(first_dve_chain, done.n)
            TTN(t0, t0, t1, ALU.add).then_inc(first_dve_chain, done.add())
            dve.wait_ge(first_dve_chain, done.n)
            TTN(par_of(1), lj(t0), lj(den), ALU.mult).then_inc(first_dve_chain, done.add())
            dve.wait_ge(first_dve_chain, done.n)
            TTN(t0, li, re, ALU.mult).then_inc(first_dve_chain, done.add())
            TTN(t1, lr, im, ALU.mult).then_inc(first_dve_chain, done.add())
            dve.wait_ge(first_dve_chain, done.n)
            TTN(t0, t0, t1, ALU.subtract).then_inc(first_dve_chain, done.add())
            dve.wait_ge(first_dve_chain, done.n)
            TTN(par_of(2), lj(t0), lj(den), ALU.mult).then_inc(first_dve_chain, done.add())
            dve.wait_ge(first_dve_chain, done.n)

            with dve.Fori(0, DEPTH) as l:
                done = Count()

                dve.tensor_copy(ssm_now[:, :, :], ssm_par[:, bass.ds(l, 1), :, :].rearrange("p a i j -> p (a i) j")).then_inc(dve_chain, done.add())
                dve.wait_ge(squares, TT)
                rsqrt(done, norm[:, 7, 0:TT], norm[:, 0, 0:TT])
                TS(norm[:, 7, 8:8 + TT], norm[:, 7, 0:TT], 0.5, None, ALU.mult).then_inc(dve_chain, done.add())
                for tt in range(TT):
                    TS(diag[:, tt, :], ident[:, :], norm[:, 7, tt:tt + 1], None, ALU.mult).then_inc(row_scales_ready, 1)

                dve.wait_ge(b_loaded, 32)
                f_re, f_im = (bc(ssm_now[:, i, :], 2, GRP) for i in (1, 2))
                b_re, b_im = braw[:, 0, :, :], braw[:, 1, :, :]
                for dst, fa, fb, op in ((0, f_re, f_im, ALU.subtract), (1, f_im, f_re, ALU.add)):
                    TTN(bbar[:, dst, :, :], b_re, fa, ALU.mult).then_inc(dve_chain, done.add())
                    TTN(btmp[:, dst, :, :], b_im, fb, ALU.mult).then_inc(dve_chain, done.add())
                    dve.wait_ge(dve_chain, done.n)
                    TTN(bbar[:, dst, :, :], bbar[:, dst, :, :], btmp[:, dst, :, :], op).then_inc(dve_chain, done.add())
                    dve.wait_ge(dve_chain, done.n)
                    TTN(bwide[:, dst, :, :].rearrange("p j (g i) -> p j g i", g=2), bc(bbar[:, dst, :, :], 2, 2),
                        bc(own_group[:, :].rearrange("p (g i) -> p g i", g=2), 1, STILES), ALU.mult).then_inc(b_scaled, 1)

                dve.wait_ge(scale_row_psum, 1)
                dve.tensor_copy(scale_row, bank(0, 0, SEQ)).then_inc(scale_row_sbuf, 1)
                dve.wait_ge(scale_row_sbuf, 1)
                for m in range(CH_T):
                    dve.wait_ge(u_psum, m + 1)
                    TTN(uT[:, m, :], bank(2 + m, 0, SEQ), scale_row, ALU.mult).then_inc(u_sbuf, 1)

                dve.wait_ge(head_gains_loaded, 32)
                for i in range(2):
                    for tt in range(TT):
                        TTN(turn_gain[:, i, tt, :, :].rearrange("p w (i f) -> p w i f", i=2), head_gain[:, :, :].rearrange("p w (i f) -> p w i f", i=2),
                            bc(bc(rope[:, i, tt, :], 1, 2), 1, 2), ALU.mult).then_inc(dve_chain, done.add())
                for tt in range(TT):
                    dve.wait_ge(qkv_psum, tt + 1)
                    b0 = (6, 0)[tt]
                    TS(qkv[:, tt, 0:512], bank(b0), norm[:, 7, tt:tt + 1], None, ALU.mult).then_inc(qkv_sbuf, 1)
                    TS(qkv[:, tt, 512:U0], bank(b0 + 1, 0, U0 - 512), norm[:, 7, tt:tt + 1], None, ALU.mult).then_inc(qkv_sbuf, 1)

                own = bc(own_group[:, :], 1, CH_T * QPT)
                for i in range(2):
                    dve.wait_ge(ssm_wT_psum, 3 + i)
                    src = bank(4 + i).rearrange("p (q s) -> p q s", s=2 * GRP)
                    dst = cT[:, 2 * i, :, :].rearrange("p m (q s) -> p (m q) s", s=2 * GRP)
                    STT(out=dst, in0=src, scalar=1.0 - 2 * i, in1=own, op0=ALU.mult, op1=ALU.mult).then_inc(ssm_c_sbuf, 1)
                dve.wait_ge(ssm_c_sbuf, 1)
                TS(cT[:, 1, :, :], cT[:, 0, :, :], -1.0, None, ALU.mult).then_inc(ssm_c_sbuf, 1)

                def lora_scale():
                    dve.wait_ge(lora_squares, 2 * TT)
                    rsqrt(done, norm[:, 7, 2:6], norm[:, 2, 0:4])
                    for tt in range(TT):
                        TS(lora[:, tt, 0:QR], qkv[:, tt, 0:QR], norm[:, 7, 2 + tt:3 + tt], None, ALU.mult).then_inc(lora_ready, 1)
                        TS(lora[:, tt, QR:QR + KVR], qkv[:, tt, QR:QR + KVR], norm[:, 7, 4 + tt:5 + tt], None, ALU.mult).then_inc(lora_ready, 1)

                def shared_key():
                    dve.wait_ge(hT_psum, 4)
                    for tt in range(TT):
                        dve.tensor_copy(qk[:, tt, HEADS:, NOPE:], bc(qkv[:, tt, QR + KVR:U0], 1, HEADS)).then_inc(key_shared, 1)
                    for tt in range(TT):
                        dve.wait_ge(qk_squares, tt + 1)
                        dve.tensor_reduce(norm[:, 2, tt * 16:tt * 16 + 16], sq[:, tt, :, :], AXX, ALU.add).then_inc(dve_chain, done.add())
                    dve.wait_ge(dve_chain, done.n)
                    W = TT * 2 * HEADS
                    rsqrt(done, norm[:, 3, 0:W], norm[:, 2, 0:W])
                    for tt in range(TT):
                        TTN(qk[:, tt, :, :], qk[:, tt, :, :], bc(norm[:, 3, tt * 16:tt * 16 + 16], 2, QKD), ALU.mult).then_inc(dve_chain, done.add())
                    dve.wait_ge(dve_chain, done.n)
                    for tt in range(TT):
                        half = qk[:, tt, :, NOPE:].rearrange("p h (i f) -> p h i f", i=2)
                        ca = sq[:, 0, :, 0:ROPE].rearrange("p h (i f) -> p h i f", i=2)
                        sa = sq[:, 1, :, 0:ROPE].rearrange("p h (i f) -> p h i f", i=2)
                        for i in range(2):
                            TTN(sq[:, i, :, 0:ROPE].rearrange("p (w h) d -> p w h d", w=2), qk[:, tt, :, NOPE:].rearrange("p (w h) d -> p w h d", w=2),
                                bc(turn_gain[:, i, tt, :, :], 2, HEADS), ALU.mult).then_inc(dve_chain, done.add())
                        dve.wait_ge(dve_chain, done.n)
                        TTN(half[:, :, 0, :], ca[:, :, 0, :], sa[:, :, 1, :], ALU.subtract).then_inc(dve_chain, done.add())
                        TTN(half[:, :, 1, :], ca[:, :, 1, :], sa[:, :, 0, :], ALU.add).then_inc(dve_chain, done.add())
                        dve.wait_ge(dve_chain, done.n)
                    dve.engine_nop().then_inc(qk_ready, 1)

                def row_max(c, hg, qb):
                    w = P * (qb + 1)
                    sc = banks(6, 2)[:, 0:4 * w].rearrange("p (h k) -> p h k", h=4)
                    dve.wait_ge(scores_psum, c + 1)
                    dve.tensor_reduce(norm[:, 2, 0:4], sc, AXX, ALU.max).then_inc(dve_chain, done.add())
                    dve.wait_ge(dve_chain, done.n)
                    TS(norm[:, 2, 12:16], norm[:, 2, 0:4], -SCALE, None, ALU.mult).then_inc(row_max_ready, 1)

                def row_sum(c, hg, qb):
                    dve.wait_ge(probs_exp, 4 * (c + 1))
                    dve.reciprocal(norm[:, 2, 8:12], norm[:, 2, 4:8]).then_inc(row_sum_inverted, 1)

                def drive(j):
                    bu = bank(j % 2).rearrange("p (i s) -> p i s", i=2)
                    cos, sin = (bc(turn[:, j % 2, i, :], 1, 2) for i in range(2))
                    dve.wait_ge(table_ready, 2 * j + 2)
                    dve.wait_ge(bu_psum, j + 1)
                    TTN(mulc, bu, cos, ALU.mult).then_inc(dve_chain, done.add())
                    TTN(muls, bu, sin, ALU.mult).then_inc(dve_chain, done.add())
                    dve.wait_ge(dve_chain, done.n)
                    TTN(driven[:, 0, :], mulc[:, 0, :], muls[:, 1, :], ALU.add).then_inc(modulated, 1)
                    TTN(driven[:, 1, :], mulc[:, 1, :], muls[:, 0, :], ALU.subtract).then_inc(modulated, 1)
                    dve.wait_ge(modulated, 2 * j + 2)
                    decay = ssm_now[:, 0, j:j + 1].broadcast_to([P, SEQ])
                    for i in range(2):
                        dve.tensor_tensor_scan(state[:, i, :], decay, driven[:, i, :], 0.0, ALU.mult, ALU.add).then_inc(dve_chain, done.add())
                    dve.wait_ge(dve_chain, done.n)

                def back(j):
                    cos, sin = (bc(turn[:, j % 2, i, :], 1, 2) for i in range(2))
                    if j >= 2:
                        dve.wait_ge(y_used, j - 1)
                    TTN(backc[:, j % 2, :, :], state, cos, ALU.mult).then_inc(dve_chain, done.add())
                    TTN(backs[:, j % 2, :, :], state, sin, ALU.mult).then_inc(turned_back, 1)

                def skip(m):
                    dve.wait_ge(y_psum, m + 1)
                    dve.wait_ge(d_loaded, 16)
                    y = uT[:, m, :]
                    STT(out=y, in0=y, scalar=dskip[:, m:m + 1], in1=bank(2 + m % 2, 0, SEQ), op0=ALU.mult, op1=ALU.add).then_inc(dve_chain, done.add())
                    dve.wait_ge(dve_chain, done.n)
                    TTN(garg, y, y, ALU.mult).then_inc(dve_chain, done.add())
                    dve.wait_ge(dve_chain, done.n)
                    TS(garg, garg, 0.044715, 1.0, ALU.mult, ALU.add).then_inc(dve_chain, done.add())
                    dve.wait_ge(dve_chain, done.n)
                    TTN(garg, garg, y, ALU.mult).then_inc(gelu_arg, 1)

                def gelu(m):
                    dve.wait_ge(gelu_tanh, m + 1)
                    STT(out=uT[:, m, :], in0=gtmp, scalar=1.0, in1=uT[:, m, :], op0=ALU.add, op1=ALU.mult).then_inc(gelu_ready, 1)

                for j in range(STILES):
                    drive(j)
                    attention(j, dict(probs=row_sum))
                    back(j)
                    attention(j, dict(lora=lora_scale, qk=shared_key, scores=row_max))
                    if j % QPT == 0 and j:
                        skip(j // QPT - 1)
                    if j % QPT == 1 and j > 1:
                        gelu(j // QPT - 1)
                skip(CH_T - 1)
                gelu(CH_T - 1)

                for tt in range(TT):
                    vbank, abank = ((0, 6), (2, 0))[tt]
                    dve.wait_ge(glu_gate_tanh, tt + 1)
                    dve.wait_ge(glu_psum, 3 + tt)
                    STT(out=merged[:, tt, :], in0=glu_t[:, tt, :], scalar=1.0, in1=banks(vbank, 2), op0=ALU.add, op1=ALU.mult).then_inc(glu_read, 1)
                    dve.wait_ge(gates_sbuf, 8)
                    dve.wait_ge(attn_proj_psum, tt + 1)
                    if tt:
                        dve.wait_ge(merged_ready, tt)
                    STT(out=attn_m, in0=gate_t[:, tt, 0:D], scalar=1.0, in1=banks(abank, 2), op0=ALU.add, op1=ALU.mult).then_inc(dve_chain, done.add())
                    dve.wait_ge(glu_read, tt + 1)
                    STT(out=merged[:, tt, :], in0=gate_t[:, tt, D:], scalar=1.0, in1=merged[:, tt, :], op0=ALU.add, op1=ALU.mult).then_inc(dve_chain, done.add())
                    dve.wait_ge(dve_chain, done.n)
                    STT(out=merged[:, tt, :], in0=merged[:, tt, :], scalar=0.25, in1=attn_m, op0=ALU.mult, op1=ALU.add).then_inc(merged_ready, 1)
                for tt in range(TT):
                    dve.wait_ge(out_psum, tt + 1)
                    STT(out=x[:, tt, :], in0=banks((6, 0)[tt], 2), scalar=0.5, in1=x[:, tt, :], op0=ALU.mult, op1=ALU.add).then_inc(x_mixed, 1)
                for c in range(KC):
                    dve.wait_ge(h2T_psum, 2 + c // 4 + 1)
                    TS(hT[:, c, P:], bank(2 + c // 4, c % 4 * P, (c % 4 + 1) * P), g_ffn[:, c:c + 1], None, ALU.mult).then_inc(h2T_sbuf_second, 1)
                dve.wait_ge(squares2, TT)
                rsqrt(done, norm[:, 7, 6:6 + TT], norm[:, 1, 0:TT])

                def red(dst, src, op):
                    dve.tensor_reduce(dst, src, AXX, op).then_inc(dve_chain, done.add())
                    dve.wait_ge(dve_chain, done.n)

                def first_of(dst, is_it, tmp, least, n):
                    idx = bc(iota[:, 0:n], 1, TT)
                    STT(out=tmp, in0=idx, scalar=-64.0, in1=is_it, op0=ALU.add, op1=ALU.mult).then_inc(dve_chain, done.add())
                    dve.wait_ge(dve_chain, done.n)
                    red(least, tmp, ALU.min)
                    STT(out=dst, in0=idx, scalar=-64.0, in1=bc(least, 2, n), op0=ALU.add, op1=ALU.is_equal).then_inc(dve_chain, done.add())
                    dve.wait_ge(dve_chain, done.n)

                dve.memset(sortedT[:, :, NPOS:], 0.0).then_inc(offsets_ready, 1)
                dve.wait_ge(logits_psum, 1)
                for tt in range(TT):
                    TS(logits[:, tt, :], bank(0, tt * 64, tt * 64 + ROUTE), norm[:, 7, 6 + tt:7 + tt], None, ALU.mult).then_inc(dve_chain, done.add())
                dve.wait_ge(dve_chain, done.n)
                lg, le = logits[:, :, 0:EG], logits[:, :, EG:].rearrange("p t (g e) -> p t g e", g=EG)
                v = [r1[:, i, :] for i in range(16)]
                red(v[0], lg, ALU.max)
                TTN(expo_in[:, :, 0:EG], lg, bc(v[0], 2, EG), ALU.subtract).then_inc(dve_chain, done.add())
                TTN(r4[:, 0, :, :], lg, bc(v[0], 2, EG), ALU.is_equal).then_inc(dve_chain, done.add())
                dve.wait_ge(dve_chain, done.n)
                group = r4[:, 2, :, :]
                first_of(group, r4[:, 0, :, :], r4[:, 1, :, :], v[1], EG)
                big = rt[:, 0, :, :].rearrange("p t (g e) -> p t g e", g=EG)
                TTN(big, le, bc(group, 3, EPG), ALU.mult).then_inc(dve_chain, done.add())
                dve.wait_ge(dve_chain, done.n)
                el, second = r8[:, 0, :, :], r8[:, 5, :, :]
                red(el, rt[:, 0, :, :].rearrange("p t (g e) -> p t e g", g=EG), ALU.add)
                red(v[2], el, ALU.max)
                TTN(r8[:, 1, :, :], el, bc(v[2], 2, EPG), ALU.subtract).then_inc(dve_chain, done.add())
                TTN(r8[:, 2, :, :], el, bc(v[2], 2, EPG), ALU.is_equal).then_inc(dve_chain, done.add())
                dve.wait_ge(dve_chain, done.n)
                top1, top2 = r8[:, 3, :, :], r8[:, 4, :, :]
                first_of(top1, r8[:, 2, :, :], r8[:, 6, :, :], v[3], EPG)
                STT(out=second, in0=top1, scalar=MASKED, in1=r8[:, 1, :, :], op0=ALU.mult, op1=ALU.add).then_inc(dve_chain, done.add())
                dve.wait_ge(dve_chain, done.n)
                red(v[4], second, ALU.max)
                dve.tensor_copy(expo_in[:, :, EG:EG + 1], v[4].unsqueeze(2)).then_inc(dve_chain, done.add())
                dve.wait_ge(dve_chain, done.n)
                dve.engine_nop().then_inc(picked, 1)
                TTN(r8[:, 7, :, :], second, bc(v[4], 2, EPG), ALU.is_equal).then_inc(dve_chain, done.add())
                dve.wait_ge(dve_chain, done.n)
                first_of(top2, r8[:, 7, :, :], r8[:, 6, :, :], v[5], EPG)
                oh1, oh2, routed, weight, place, tmp, rank1 = (rt[:, i, :, :] for i in range(1, 8))

                def over(ap):
                    return ap.rearrange("p t (g e) -> p t g e", g=EG)

                TTN(over(oh1), bc(group, 3, EPG), bc(top1, 2, EG), ALU.mult).then_inc(dve_chain, done.add())
                TTN(over(oh2), bc(group, 3, EPG), bc(top2, 2, EG), ALU.mult).then_inc(dve_chain, done.add())
                dve.wait_ge(dve_chain, done.n)
                TTN(routed, oh1, oh2, ALU.add).then_inc(routes_ready, 1)
                dve.wait_ge(expo_ready, 1)
                red(v[6], expo[:, :, 0:EG], ALU.add)
                TS(v[7], expo[:, :, EG:EG + 1].rearrange("p t o -> p (t o)"), 1.0, None, ALU.add).then_inc(dve_chain, done.add())
                dve.wait_ge(dve_chain, done.n)
                TTN(v[8], v[6], v[7], ALU.mult).then_inc(dve_chain, done.add())
                dve.wait_ge(dve_chain, done.n)
                dve.reciprocal(v[9], v[8]).then_inc(dve_chain, done.add())
                dve.wait_ge(dve_chain, done.n)
                TTN(v[10], v[9], expo[:, :, EG:EG + 1].rearrange("p t o -> p (t o)"), ALU.mult).then_inc(dve_chain, done.add())
                dve.wait_ge(dve_chain, done.n)
                TTN(weight, oh1, bc(v[9], 2, NE), ALU.mult).then_inc(dve_chain, done.add())
                TTN(tmp, oh2, bc(v[10], 2, NE), ALU.mult).then_inc(dve_chain, done.add())
                dve.wait_ge(dve_chain, done.n)
                TTN(weight, weight, tmp, ALU.add).then_inc(dve_chain, done.add())
                dve.wait_ge(rank_psum, 1)
                rank = bank(1, 0, TT * NE).rearrange("p (t e) -> p t e", t=TT)
                dve.tensor_copy(count[:, 0, :], bank(1, TT * NE, TT * NE + NE)).then_inc(dve_chain, done.add())
                TS(rank1, rank, 1.0, None, ALU.add).then_inc(dve_chain, done.add())
                dve.wait_ge(dve_chain, done.n)
                dve.tensor_tensor_scan(count[:, 1, :], ones[:, 0:NE], count[:, 0, :], 0.0, ALU.mult, ALU.add).then_inc(dve_chain, done.add())
                dve.wait_ge(dve_chain, done.n)
                TTN(count[:, 2, :], count[:, 1, :], count[:, 0, :], ALU.subtract).then_inc(dve_chain, done.add())
                dve.wait_ge(dve_chain, done.n)
                for r in range(PASSES):
                    TS(roff[:, r, :], count[:, 2, :], float(SLOT * r), float(NPOS), ALU.add, ALU.min).then_inc(offsets_ready, 1)
                dve.tensor_reduce(v[15][:, 0:1], count[:, 0, :], AXX, ALU.max).then_inc(dve_chain, done.add())
                dve.wait_ge(dve_chain, done.n)
                TS(rmany[:, bass.ds(l, 1)], v[15][:, 0:1], float(SLOT), None, ALU.is_gt).then_inc(counted, 1)
                TTN(place, rank1, bc(count[:, 2, :], 1, TT), ALU.add).then_inc(dve_chain, done.add())
                TTN(tmp, rank1, routed, ALU.mult).then_inc(dve_chain, done.add())
                dve.wait_ge(dve_chain, done.n)
                TS(rank1, tmp, 1.0, None, ALU.subtract).then_inc(dve_chain, done.add())
                dve.wait_ge(dve_chain, done.n)
                for i, oh in enumerate((oh1, oh2)):
                    TTN(tmp, oh, place, ALU.mult).then_inc(dve_chain, done.add())
                    dve.wait_ge(dve_chain, done.n)
                    red(v[11 + i], tmp, ALU.add)
                for tt in range(TT):
                    TS(v[13][:, tt:tt + 1], v[11][:, tt:tt + 1], 1.0, None, ALU.subtract).then_inc(dve_chain, done.add())
                    TS(v[14][:, tt:tt + 1], v[12][:, tt:tt + 1], 1.0, None, ALU.subtract).then_inc(dve_chain, done.add())
                dve.wait_ge(dve_chain, done.n)
                for tt in range(TT):
                    for i, dst in enumerate((perm, perm2)):
                        TS(dst[:, tt, :], iota[:, :], v[13 + i][:, tt:tt + 1], norm[:, 7, 6 + tt:7 + tt], ALU.is_equal, ALU.mult).then_inc(dve_chain, done.add())
                    dve.wait_ge(dve_chain, done.n)
                    TTN(perm[:, tt, :], perm[:, tt, :], perm2[:, tt, :], ALU.add).then_inc(perm_ready, 1)

                def select(p, par, pair=None):
                    if pair is None and (not isinstance(p, int) or p >= 2):
                        dve.wait_ge(turned_psum, p - 1)
                        dve.sem_inc(held, 1)
                    dst = sel[:, par, :, :].rearrange("p t (e s) -> p t e s", e=2)
                    e0 = (p if pair is None else pair) * 2
                    pick = [bc(a[:, :, bass.ds(e0, 2)], 3, SLOT) for a in (rank1, weight)]
                    TTN(dst, bc(bc(iota[:, 0:SLOT], 1, 2), 1, TT), pick[0], ALU.is_equal).then_inc(sel_half, 1)
                    dve.wait_ge(sel_half, p + 1)
                    dve.sem_inc(held, 1)
                    TTN(dst, dst, pick[1], ALU.mult).then_inc(sel_ready, 1)

                def swiglu(p, par):
                    dve.wait_ge(gate_tanh_ready, p + 1)
                    dve.sem_inc(held, 1)
                    STT(out=hidden[:, par, :], in0=gtanh[:, par, :], scalar=1.0, in1=bank(par, 0, DE), op0=ALU.add, op1=ALU.mult).then_inc(hidden_half, 1)
                    dve.wait_ge(hidden_half, p + 1)
                    dve.sem_inc(held, 1)
                    STT(out=hidden[:, par, :], in0=hidden[:, par, :], scalar=0.5, in1=bank(par, DE, 2 * DE), op0=ALU.mult, op1=ALU.mult).then_inc(hidden_ready, 1)

                def sel_out(p, par):
                    dve.wait_ge(hiddenT_sbuf, p + 1)
                    dve.sem_inc(held, 1)
                    dve.tensor_copy(selT[:, par, :], bank(par, 2 * P, 4 * P)).then_inc(selT_sbuf, 1)

                def down_hi(p):
                    dve.wait_ge(down_psum, p + 1)
                    dve.sem_inc(held, 1)
                    dve.tensor_copy(down[:, 512:], bank(3)).then_inc(down_sbuf_hi, 1)

                def step(p, par, last=False):
                    if not last:
                        select(p + 1, 1 - par)
                    sel_out(p, par)
                    down_hi(p)
                    if not last:
                        swiglu(p + 1, 1 - par)

                select(0, 0)
                swiglu(0, 0)
                step(0, 0)
                with dve.Fori(0, NPAIR // 2 - 1) as i:
                    for k in range(2):
                        step(i * 2 + 1 + k, (1 + k) % 2)
                step(NPAIR - 1, 1, last=True)
                for tt in range(TT):
                    dve.wait_ge(moe_psum, tt + 1)
                    dve.tensor_copy(x[:, tt, :], banks(4 + 2 * tt, 2)).then_inc(x_ready, 1)

                def shift_ranks(r):
                    dve.wait_ge(sel_ready, r * NPAIR)
                    dve.sem_inc(held, 1)
                    dve.tensor_scalar(rank1, rank1, float(SLOT), None, ALU.subtract).then_inc(rank_shifted, 1)
                    dve.wait_ge(rank_shifted, r)
                    dve.sem_inc(held, 1)

                def more(p, pair, r):
                    select(p, 0, pair)
                    swiglu(p, 0)
                    sel_out(p, 0)
                    down_hi(p)
                    for tt in range(TT):
                        dve.wait_ge(moe_psum, (p - (NPAIR - 1)) * TT + tt + 1)
                        dve.sem_inc(held, 1)
                        dve.tensor_copy(x[:, tt, :], banks(4 + 2 * tt, 2)).then_inc(x_ready, 1)

                with dve.If(crowded(dve, l) > 0):
                    further_steps(dve, more, shift_ranks)
                leave_layer(dve, l)
            dve.drain().then_inc(first_result_ready, TT)

        @block.tensor
        def _(pe):
            mm = pe.matmul

            def group(dst, lhs, rhs, n, then=None, **kw):
                for c in range(n):
                    last = mm(dst, lhs(c), rhs(c), start=c == 0, stop=c == n - 1, **kw)
                return last

            for semaphore in free_a + free_b:
                pe.sem_inc(semaphore, 1)
            pe.wait_ge(first_constants, 7 + HALF + 5)
            pe.wait_ge(first_params_loaded, 48)
            pe.wait_ge(first_dt_wide, 1)
            NW = DEPTH * STILES
            for i in range(3):
                last = pe.transpose(bank(7, i * NW, (i + 1) * NW), praw[0:NW, i, :], ident[0:NW, 0:NW])
            last.then_inc(first_params_turned, 1)

            with pe.Fori(0, DEPTH) as l:
                def a_ready(a):
                    pe.wait_ge(loaded_a[a % A_SLOTS], (l * A_USES[a % A_SLOTS] + a // A_SLOTS + 1) * 32)
                    pe.sem_inc(held, 1)

                for i in range(KC // 2):
                    pe.wait_ge(first_x_loaded, 16 * TT)
                    if i >= 2:
                        pe.wait_ge(hT_sbuf, 2 * i - 2)
                    for c in (2 * i, 2 * i + 1):
                        for tt in range(TT):
                            last = pe.transpose(bank(i % 2, (c % 2) * SEQ + tt * P, (c % 2) * SEQ + (tt + 1) * P),
                                                x[:, tt, c::KC], ident[:, :])
                    last.then_inc(hT_psum, 1)
                pe.wait_ge(hT_sbuf, KC)
                a_ready(A_U)
                w = slotA_kc(A_U)
                for m in range(CH_T):
                    last = group(bank(2 + m, 0, SEQ), lambda c: w[:, c, m * P:(m + 1) * P], lambda c: hT[:, c, :], KC)
                    last.then_inc(u_psum, 1)
                pe.wait_ge(row_scales_ready, TT)
                for tt in range(TT):
                    last = mm(bank(0, tt * P, (tt + 1) * P), ones[:, :], diag[:, tt, :], start=True, stop=True)
                last.then_inc(scale_row_psum, 1)
                a_ready(A_Q)
                w = slotA_kc(A_Q)
                for tt in range(TT):
                    b0 = (6, 0)[tt]
                    if tt:
                        pe.wait_ge(scale_row_sbuf, 1)
                    group(bank(b0), lambda c: hT[:, c, tt * P:(tt + 1) * P], lambda c: w[:, c, :], KC)
                    if tt == 0:
                        a_ready(A_TAIL)
                    last = group(bank(b0 + 1, 0, U0 - 512), lambda c: hT[:, c, tt * P:(tt + 1) * P], lambda c: wtail[:, c, :], KC)
                    last.then_inc(qkv_psum, 1)
                pe.drain().then_inc(free_a[A_U % A_SLOTS], 1)
                pe.sem_inc(free_a[A_Q % A_SLOTS], 1)
                pe.wait_ge(u_sbuf, CH_T)
                for i in range(2):
                    pe.wait_ge(b_scaled, i + 1)
                    for m in range(CH_T):
                        last = pe.transpose(bank(2 + i, m * P, (m + 1) * P),
                                            bwide[:, i, m * QPT:(m + 1) * QPT, :].rearrange("p j s -> p (j s)"), ident[:, :])
                    last.then_inc(ssm_wT_psum, 1)
                pe.wait_ge(c_loaded, 64)
                for i in range(2):
                    for m in range(CH_T):
                        last = pe.transpose(bank(4 + i, m * P, (m + 1) * P),
                                            craw[:, i, m, :, :].rearrange("p d s -> p (d s)"), ident[:, :])
                    last.then_inc(ssm_wT_psum, 1)

                def lora_turn():
                    pe.wait_ge(lora_ready, 2 * TT)
                    pe.wait_ge(qkv_sbuf, 2 * TT)
                    for c in range(QC + KVC):
                        if c >= 2:
                            pe.wait_ge(loraT_sbuf, c - 1)
                        for tt in range(TT):
                            src = lora[:, tt, c:QR:QC] if c < QC else lora[:, tt, QR + c - QC:QR + KVR:KVC]
                            last = pe.transpose(bank(6 + c % 2, tt * P, (tt + 1) * P), src, ident[:, :])
                        last.then_inc(loraT_psum, 1)

                def q_up():
                    pe.wait_ge(loraT_sbuf, QC + KVC)
                    for tt in range(TT):
                        if tt:
                            pe.wait_ge(q_sbuf, 2 * tt)
                        for i in range(2):
                            last = group(bank(6 + i, 0, 4 * QKD), lambda c: loraT[:, c, tt * P:(tt + 1) * P],
                                         lambda c: wuq[:, c, i * 4 * QKD:(i + 1) * 4 * QKD], QC)
                        last.then_inc(q_psum, 1)
                    pe.drain().then_inc(free_a[A_TAIL % A_SLOTS], 1)

                def kv_up():
                    pe.wait_ge(loaded_b[0], (l * (NE // B_SLOTS + 1) + 1) * 16)
                    pe.sem_inc(held, 1)
                    pe.wait_ge(q_sbuf, 4)
                    for tt in range(TT):
                        if tt:
                            pe.wait_ge(k_sbuf, 2 * tt)
                            pe.wait_ge(v_sbuf, 2 * tt)
                        for i in range(2):
                            last = group(bank(6 + i), lambda c: loraT[:, QC + c, tt * P:(tt + 1) * P],
                                         lambda c: wukv[:, c, i * 512:(i + 1) * 512], KVC)
                        last.then_inc(kv_psum, 1)
                    pe.drain().then_inc(free_b[0], 1)

                def qk_turn(hg):
                    pe.wait_ge(qk_ready, 1)
                    pe.wait_ge(v_sbuf, 4)
                    for i in range(4):
                        n = 4 * hg + i
                        if i >= 2:
                            pe.wait_ge(qkT_sbuf, n - 1)
                        for k in range(2):
                            head = (i // 2) * HEADS + hg * 4 + 2 * (i % 2) + k
                            for tt in range(TT):
                                last = pe.transpose(psum[0:QKD, 6 + i % 2, k * SEQ + tt * P:k * SEQ + (tt + 1) * P],
                                                    qk[:, tt, head, :], ident[:, :])
                        last.then_inc(qkT_psum, 1)

                def scores(c, hg, qb):
                    pe.wait_ge(qkT_sbuf, 4 * hg + 4)
                    w = P * (qb + 1)
                    for hh in range(4):
                        dst = banks(6, 2)[:, hh * w:(hh + 1) * w]
                        mm(dst, qkT[0:QKD, 0, hh, qb * P:(qb + 1) * P], qkT[0:QKD, 1, hh, 0:w], start=True, stop=False)
                        last = mm(dst[:, w - CHUNK:], ident[:, :], amask[:, :], start=False, stop=True)
                    last.then_inc(scores_psum, 1)

                def probs_turn(c, hg, qb):
                    pe.wait_ge(probs_ready, 4 * (c + 1))
                    for hh in range(4):
                        for k in range(qb + 1):
                            i = hh * (qb + 1) + k
                            last = pe.transpose(banks(6, 2)[:, i * P:(i + 1) * P], probs[:, hh, k * P:(k + 1) * P], ident[:, :])
                    last.then_inc(probsT_psum, 1)

                def values(c, hg, qb):
                    pe.wait_ge(probsT_sbuf, c + 1)
                    if c:
                        pe.wait_ge(o_sbuf, c)
                    for hh in range(4):
                        lo = hh % 2 * VD
                        for k in range(qb + 1):
                            last = mm(psum[lo:lo + VD, 5, hh // 2 * P:(hh // 2 + 1) * P], vtok[:, k, hg * 4 + hh, :],
                                      probsT[:, hh, k, :], start=k == 0, stop=k == qb)
                    last.then_inc(o_psum, 1)

                def gate(g):
                    a = A_G + g // 2
                    if g % 2 == 0:
                        a_ready(a)
                    pe.wait_ge(ssm_b_sbuf, 2)
                    pe.wait_ge(ssm_c_sbuf, 3)
                    if g:
                        pe.wait_ge(gates_sbuf, g)
                    w, tt = slotA_kc(a), g % 2
                    last = group(bank(4), lambda c: hT[:, c, tt * P:(tt + 1) * P], lambda c: w[:, c, :], KC)
                    last.then_inc(gates_psum, 1)
                    if g % 2:
                        pe.drain().then_inc(free_a[a % A_SLOTS], 1)

                def inputs(j):
                    m, q = j // QPT, j % QPT
                    rows = slice(32 * q, 32 * q + 32)
                    if j >= 2:
                        pe.wait_ge(modulated, 2 * j - 2)
                    for i in range(2):
                        last = mm(bank(j % 2, i * SEQ, (i + 1) * SEQ), bT[rows, i, m, :], uT[rows, m, :], start=True, stop=True)
                    last.then_inc(bu_psum, 1)

                def outputs(j0):
                    m = j0 // QPT
                    pe.wait_ge(turned_back, j0 + 2)
                    pe.wait_ge(ssm_c_sbuf, 3)
                    if j0 % QPT == 0 and m >= 2:
                        pe.wait_ge(gelu_arg, m - 1)
                    terms = ((0, backc, 0), (1, backs, 1), (2, backc, 1), (2, backs, 0))
                    for k, (ci, src, i) in enumerate(terms):
                        for j in (j0, j0 + 1):
                            cols = slice(32 * (j % QPT), 32 * (j % QPT) + 32)
                            last = mm(psum[cols, 2 + m % 2, 0:SEQ], cT[:, ci, m, cols], src[:, j % 2, i, :], start=k == 0, stop=k == 3)
                    pe.drain().then_inc(y_used, 2)
                    if j0 % QPT == QPT - 2:
                        pe.sem_inc(y_psum, 1)

                pe.wait_ge(ssm_b_sbuf, 2)
                pe.wait_ge(qkv_sbuf, 2 * TT)
                inputs(0)
                for j in range(STILES):
                    if j + 1 < STILES:
                        inputs(j + 1)
                    for g in GATES_AT.get(j, []):
                        gate(g)
                    attention(j, dict(lora=lora_turn, q=q_up, kv=kv_up, turn=qk_turn, scores=scores, probs=probs_turn, values=values))
                    if j % 2:
                        outputs(j - 1)

                def glu(half, tt, b):
                    w = slotA(A_GLU + 1 - half).rearrange("p (c n) -> p c n", c=CH_T)
                    for i in range(2):
                        last = group(bank(b + i), lambda c: uT[:, c, tt * P:(tt + 1) * P], lambda c: w[:, c, i * 512:(i + 1) * 512], CH_T)
                    last.then_inc(glu_psum, 1)

                def attn_proj(tt, b):
                    w = slotA(A_AP).rearrange("p (c n) -> p c n", c=CH_T)
                    for i in range(2):
                        last = group(bank(b + i), lambda c: oT[:, c, tt * P:(tt + 1) * P], lambda c: w[:, c, i * 512:(i + 1) * 512], HEADS // 2)
                    last.then_inc(attn_proj_psum, 1)

                a_ready(A_AP)
                pe.wait_ge(o_sbuf, 4)
                attn_proj(0, 6)
                a_ready(A_GLU)
                a_ready(A_GLU + 1)
                pe.wait_ge(gelu_ready, CH_T)
                pe.wait_ge(gates_sbuf, 8)
                glu(1, 0, 2)
                glu(1, 1, 4)
                pe.drain().then_inc(free_a[A_GLU % A_SLOTS], 1)
                glu(0, 0, 0)
                pe.wait_ge(glu_gate_tanh, 1)
                glu(0, 1, 2)
                pe.wait_ge(glu_read, 1)
                attn_proj(1, 0)
                pe.drain().then_inc(free_a[(A_GLU + 1) % A_SLOTS], 1)
                pe.sem_inc(free_a[A_AP % A_SLOTS], 1)

                def turn4(src, tt, b, signal):
                    for i in range(2):
                        for c in range(4 * i, 4 * i + 4):
                            last = pe.transpose(bank(b + i, (c % 4) * P, (c % 4 + 1) * P), src[:, tt, c::KC], ident[:, :])
                        last.then_inc(signal, 1)

                def out_proj(tt, b):
                    for g in range(2):
                        w = slotA_kc(A_OUT + g)
                        last = group(bank(b + g), lambda c: hT[:, c, tt * P:(tt + 1) * P], lambda c: w[:, c, :], KC)
                    last.then_inc(out_psum, 1)

                pe.wait_ge(glu_gate_tanh, 2)
                pe.wait_ge(merged_ready, 1)
                turn4(merged, 0, 4, mergedT_psum)
                a_ready(A_OUT)
                a_ready(A_OUT + 1)
                pe.wait_ge(mergedT_sbuf, 2)
                out_proj(0, 6)
                pe.wait_ge(merged_ready, 2)
                turn4(merged, 1, 2, mergedT_psum)
                pe.wait_ge(mergedT_sbuf, 4)
                out_proj(1, 0)
                pe.drain().then_inc(free_a[A_OUT % A_SLOTS], 1)
                pe.sem_inc(free_a[(A_OUT + 1) % A_SLOTS], 1)

                pe.wait_ge(x_mixed, 1)
                turn4(x, 0, 4, h2T_psum)
                pe.wait_ge(x_mixed, 2)
                turn4(x, 1, 2, h2T_psum)
                pe.wait_ge(h2T_sbuf, KC)
                pe.wait_ge(h2T_sbuf_second, KC)
                pe.wait_ge(router_loaded, 32)
                for tt in range(TT):
                    last = group(bank(0, tt * 64, tt * 64 + ROUTE), lambda c: hT[:, c, tt * P:(tt + 1) * P], lambda c: wroute[:, c, :], KC)
                last.then_inc(logits_psum, 1)
                for tt in range(TT):
                    for i in range(2):
                        mm(bank(4 + 2 * tt + i), ident[:, :], x[:, tt, i * 512:(i + 1) * 512], start=True, stop=False)
                pe.wait_ge(routes_ready, 1)
                routed = rt[:, 3, :, :]
                mm(bank(1, 0, NE), before[:, :], routed[:, 0, :], start=True, stop=True)
                mm(bank(1, NE, 2 * NE), before[:, :], routed[:, 1, :], start=True, stop=False)
                mm(bank(1, NE, 2 * NE), ones[:, :], routed[:, 0, :], start=False, stop=True)
                mm(bank(1, 2 * NE, 3 * NE), ones[:, :], routed[:, 0, :], start=True, stop=False)
                mm(bank(1, 2 * NE, 3 * NE), ones[:, :], routed[:, 1, :], start=False, stop=True).then_inc(rank_psum, 1)
                pe.wait_ge(perm_ready, TT)
                for c in range(KC):
                    if c >= 4:
                        pe.wait_ge(sorted_sbuf, c - 3)
                    last = group(bank(c % 4), lambda tt: x[:, tt, c::KC], lambda tt: perm[:, tt, :], TT)
                    last.then_inc(sorted_psum, 1)

                def gate_up(p, par, weights, free=None):
                    pe.wait_ge(pair_copied, p * 2 + 2)
                    pe.sem_inc(held, 1)
                    for c in range(KC):
                        for e in range(2):
                            w = weights[:, e, :].rearrange("p (u c n) -> p u c n", u=2, c=KC)
                            last = mm(psum[e * SLOT:(e + 1) * SLOT, par, :], pairT[:, par, c, e * SLOT:(e + 1) * SLOT],
                                      w[:, :, c, :], start=c == 0, stop=c == KC - 1)
                            if c == KC - 1 and free:
                                last.then_inc(free[e], 1)
                    pe.drain().then_inc(hidden_psum, 1)

                def bank_read(p):
                    pe.wait_ge(hiddenT_sbuf, p - 1)
                    pe.sem_inc(held, 1)
                    pe.wait_ge(selT_sbuf, p - 1)
                    pe.sem_inc(held, 1)

                def gate_up_ring(p, par, ring, n):
                    slots = (2 * ring, 2 * ring + 1)
                    for s in slots:
                        pe.wait_ge(loaded_a[s], (l * A_USES[s] + n + 1) * 32)
                        pe.sem_inc(held, 1)
                    gate_up(p, par, ringA[:, 2 * ring:2 * ring + 2, :], free_a[2 * ring:2 * ring + 2])

                def turn_pair(p, par):
                    pe.wait_ge(hidden_ready, p + 1)
                    pe.sem_inc(held, 1)
                    for c in range(2):
                        pe.transpose(bank(par, c * P, (c + 1) * P), hidden[:, par, c::2], ident[:, :])
                    pe.wait_ge(sel_ready, p + 1)
                    pe.sem_inc(held, 1)
                    for tt in range(TT):
                        last = pe.transpose(bank(par, (2 + tt) * P, (3 + tt) * P), sel[:, par, tt, :], ident[:, :])
                    last.then_inc(turned_psum, 1)

                def scatter(p, par, start=False, end=False):
                    pe.wait_ge(selT_sbuf, p + 1)
                    pe.sem_inc(held, 1)
                    pe.wait_ge(down_sbuf_lo, p + 1)
                    pe.sem_inc(held, 1)
                    pe.wait_ge(down_sbuf_hi, p + 1)
                    pe.sem_inc(held, 1)
                    for tt in range(TT):
                        for i in range(2):
                            if start:
                                mm(bank(4 + 2 * tt + i), ident[:, :], x[:, tt, i * 512:(i + 1) * 512], start=True, stop=False)
                            last = mm(bank(4 + 2 * tt + i), selT[:, par, tt * P:(tt + 1) * P], down[:, i * 512:(i + 1) * 512],
                                      start=False, stop=end)
                        if end:
                            last.then_inc(moe_psum, 1)

                def down_mm(p, par, turn=None):
                    pe.wait_ge(hiddenT_sbuf, p + 1)
                    pe.sem_inc(held, 1)
                    for e in range(2 if turn is not None else 0):
                        s = 2 * par + e
                        pe.wait_ge(loaded_b[s], (b_use(l, s, turn) + 1) * 16)
                        pe.sem_inc(held, 1)
                    for i in range(2):
                        for c in range(2):
                            for e in range(2):
                                s = 2 * par + e
                                w = ringB[:, s, :].rearrange("p (c n) -> p c n", c=2)
                                last = mm(psum[e * SLOT:(e + 1) * SLOT, 2 + i, :], hiddenT[:, c, e * SLOT:(e + 1) * SLOT],
                                          w[:, c, i * 512:(i + 1) * 512], start=c == 0, stop=c == 1)
                                if i == 1 and c == 1 and turn is not None:
                                    last.then_inc(free_b[s], 1)
                    pe.drain().then_inc(down_psum, 1)

                pe.wait_ge(sorted_sbuf, KC)
                gate_up_ring(0, 0, 0, A_FIRST)
                gate_up_ring(1, 1, 1, A_FIRST)
                turn_pair(0, 0)
                down_mm(0, 0, 0)
                bank_read(OWN_PAIR)
                pe.wait_ge(own_pair_loaded, 64)
                gate_up(OWN_PAIR, 0, own_pair)
                turn_pair(1, 1)
                scatter(0, 0)
                down_mm(1, 1, 0)
                with pe.Fori(0, NPAIR // 2 - 2) as i:
                    for k in range(2):
                        p = i * 2 + 2 + k
                        bank_read(p + 1)
                        gate_up_ring(p + 1, 1 - k, k, i + A_FIRST + 1)
                        turn_pair(p, k)
                        scatter(p - 1, 1 - k)
                        down_mm(p, k, i + 1)
                bank_read(NPAIR - 1)
                gate_up_ring(NPAIR - 1, 1, 0, A_USES[0] - 1)
                turn_pair(NPAIR - 2, 0)
                scatter(NPAIR - 3, 1)
                down_mm(NPAIR - 2, 0, NPAIR // 2 - 1)
                turn_pair(NPAIR - 1, 1)
                scatter(NPAIR - 2, 0)
                down_mm(NPAIR - 1, 1, NPAIR // 2 - 1)
                scatter(NPAIR - 1, 1, end=True)

                def more(p, pair, r):
                    pe.wait_ge(x_ready, (p - (NPAIR - 1)) * TT)
                    pe.sem_inc(held, 1)
                    pe.sem_inc(more_free, 1)
                    pe.wait_ge(more_loaded, (p - (NPAIR - 1)) * 96)
                    pe.sem_inc(held, 1)
                    gate_up(p, 0, ringA[:, 0:2, :])
                    turn_pair(p, 0)
                    down_mm(p, 0)
                    scatter(p, 0, start=True, end=True)

                with pe.If(crowded(pe, l) > 0):
                    further_steps(pe, more)
                leave_layer(pe, l)


GATES_AT = {0: [0], 1: [1], 3: [2, 3, 4, 5], 5: [6], 7: [7]}


def attention(slot, do):
    stages = {0: [("lora",)], 1: [("q",)], 2: [("kv",), ("qk",)], 3: [("turn", 0)],
              4: [("scores", 0, 0, 0)], 5: [("probs", 0, 0, 0)], 6: [("values", 0, 0, 0), ("scores", 1, 0, 1)],
              7: [("probs", 1, 0, 1)], 8: [("values", 1, 0, 1), ("turn", 1)], 9: [("scores", 2, 1, 0)],
              10: [("probs", 2, 1, 0)], 11: [("values", 2, 1, 0), ("scores", 3, 1, 1)], 12: [("probs", 3, 1, 1)],
              13: [("values", 3, 1, 1)]}
    for name, *args in stages.get(slot, []):
        if name in do:
            do[name](*args)


_INS = ["x", "positions", "norm_mix_g", "w_in", "q_lora_g", "w_uq", "kv_lora_g", "w_ukv", "q_head_g", "k_head_g",
        "w_attn_proj", "lam_re", "lam_im", "log_dt", "b_re", "b_im", "c_re", "c_im", "d_skip", "w_glu", "w_out",
        "norm_ffn_g", "w_router_group", "w_router_expert", "w_exp_gate", "w_exp_up", "w_exp_down"]


def kernel(**inputs):
    import numpy as _np
    import concourse.bacc as _bacc
    from concourse import mybir as _mybir
    from concourse.bass_utils import run_bass_kernel_spmd as _run

    nc = _bacc.Bacc("TRN2", target_bir_lowering=False, num_devices=1, dynamic_dma_scratch_size=256)
    arrays, tensors = {}, {}
    for name in _INS:
        a = _np.ascontiguousarray(inputs[name])
        arrays[f"in_{name}"] = a
        tensors[name] = nc.dram_tensor(f"in_{name}", a.shape, _mybir.dt.from_np(a.dtype), kind="ExternalInput").ap()
    out = nc.dram_tensor("out_0", (1, SEQ, D), F32, kind="ExternalOutput").ap()
    build(nc, tensors, out)
    r = _run(nc, [arrays], core_ids=[0])
    return r.results[0]["out_0"]
```

```python
import math
from contextlib import ExitStack

import numpy as np

import concourse.bass as bass
from concourse import mybir

ALU = mybir.AluOpType
ACT = mybir.ActivationFunctionType
AXX = mybir.AxisListType.X
F32 = mybir.dt.float32
I32 = mybir.dt.int32

P = 128
D = 1024
SEQ = 256
DEPTH = 2
TT = SEQ // P
KC = D // P

HEADS, NOPE, ROPE = 8, 64, 32
QKD = NOPE + ROPE
VD = 64
QR, KVR = 384, 256
QC, KVC = QR // P, KVR // P
CHUNK = 64
HALF = ROPE // 2
THETA = 10000.0
SCALE = QKD ** -0.5
MASKED = -1.0e30

SSM = 512
GRP = 16
GROUPS = SSM // GRP
NST = 64
STILES = GROUPS * NST // P
CH_T = SSM // P
QPT = STILES // CH_T

COLS = QR + KVR + ROPE + SSM + 2 * D
U0 = QR + KVR + ROPE
G0 = U0 + SSM
TAIL = U0 - 512

EG, EPG = 4, 8
NE = EG * EPG
NPAIR = NE // 2
DE = 256
SLOT = 64
PASSES = SEQ // SLOT
ROUTE = EG + NE
NPOS = 2 * SEQ
EPS = 1e-6

TWO_PI = 2.0 * math.pi
ROUND = 1.5 * 2.0 ** 23


def split_two_pi():
    parts, rest = [], TWO_PI
    for step in (2.0 ** -5, 2.0 ** -14):
        part = math.floor(rest / step) * step
        parts.append(part)
        rest -= part
    return parts + [rest]


A_SLOTS, B_SLOTS = 4, 4
A_SIZE, B_SIZE = 4096, 2048
A_U, A_Q, A_TAIL, A_G, A_GLU, A_AP, A_OUT = 0, 1, 2, 3, 7, 9, 10
A_MIX = 12
A_FIRST = A_MIX // A_SLOTS
OWN_PAIR = 2
B_USES = [NPAIR // 2] * 2 + [NPAIR // 2 - 1] * 2
A_USES = [A_FIRST + n for n in B_USES]
assert A_MIX % A_SLOTS == 0


def bc(ap, axis, n):
    ap = ap.unsqueeze(axis)
    shape = list(ap.shape)
    shape[axis] = n
    return ap.broadcast_to(shape)


class Count:

    def __init__(self):
        self.n = 0

    def add(self):
        self.n += 1
        return 1


def build(nc, t, out):
    ctx = ExitStack()
    with ctx:
        def sb(name, shape, dt=F32):
            return ctx.enter_context(nc.sbuf_tensor(name, shape, dt))

        loaded_a = [ctx.enter_context(nc.semaphore(f"loaded_a{i}")) for i in range(A_SLOTS)]
        free_a = [ctx.enter_context(nc.semaphore(f"free_a{i}")) for i in range(A_SLOTS)]
        loaded_b = [ctx.enter_context(nc.semaphore(f"loaded_b{i}")) for i in range(B_SLOTS)]
        free_b = [ctx.enter_context(nc.semaphore(f"free_b{i}")) for i in range(B_SLOTS)]
        layer_left = ctx.enter_context(nc.semaphore("layer_left"))
        counted = ctx.enter_context(nc.semaphore("counted"))
        layer_open = ctx.enter_context(nc.semaphore("layer_open"))
        held = ctx.enter_context(nc.semaphore("held"))
        first_angle_ready = ctx.enter_context(nc.semaphore("first_angle_ready"))
        first_constants = ctx.enter_context(nc.semaphore("first_constants"))
        first_decay_ready = ctx.enter_context(nc.semaphore("first_decay_ready"))
        first_dt_ready = ctx.enter_context(nc.semaphore("first_dt_ready"))
        first_dt_wide = ctx.enter_context(nc.semaphore("first_dt_wide"))
        first_dve_chain = ctx.enter_context(nc.semaphore("first_dve_chain"))
        first_gains_loaded = ctx.enter_context(nc.semaphore("first_gains_loaded"))
        first_half_sine = ctx.enter_context(nc.semaphore("first_half_sine"))
        first_params_loaded = ctx.enter_context(nc.semaphore("first_params_loaded"))
        first_params_turned = ctx.enter_context(nc.semaphore("first_params_turned"))
        first_pool_chain = ctx.enter_context(nc.semaphore("first_pool_chain"))
        first_positions_loaded = ctx.enter_context(nc.semaphore("first_positions_loaded"))
        first_result_ready = ctx.enter_context(nc.semaphore("first_result_ready"))
        first_rho_ready = ctx.enter_context(nc.semaphore("first_rho_ready"))
        first_stored = ctx.enter_context(nc.semaphore("first_stored"))
        first_theta_turned = ctx.enter_context(nc.semaphore("first_theta_turned"))
        first_x_loaded = ctx.enter_context(nc.semaphore("first_x_loaded"))
        per_layer = []

        def of_layer(name):
            per_layer.append(ctx.enter_context(nc.semaphore(name)))
            return per_layer[-1]

        gains_ready = of_layer("gains_ready")
        head_gains_loaded = of_layer("head_gains_loaded")
        nope_gains_loaded = of_layer("nope_gains_loaded")
        b_loaded = of_layer("b_loaded")
        c_loaded = of_layer("c_loaded")
        d_loaded = of_layer("d_loaded")
        router_loaded = of_layer("router_loaded")
        dve_chain = of_layer("dve_chain")
        pool_chain = of_layer("pool_chain")
        squares = of_layer("squares")
        row_scales_ready = of_layer("row_scales_ready")
        scale_row_psum = of_layer("scale_row_psum")
        scale_row_sbuf = of_layer("scale_row_sbuf")
        hT_psum = of_layer("hT_psum")
        hT_sbuf = of_layer("hT_sbuf")
        hT_sbuf_high = of_layer("hT_sbuf_high")
        u_psum = of_layer("u_psum")
        u_sbuf = of_layer("u_sbuf")
        qkv_psum = of_layer("qkv_psum")
        qkv_sbuf = of_layer("qkv_sbuf")
        lora_squares = of_layer("lora_squares")
        lora_ready = of_layer("lora_ready")
        loraT_psum = of_layer("loraT_psum")
        loraT_sbuf = of_layer("loraT_sbuf")
        q_psum = of_layer("q_psum")
        kv_psum = of_layer("kv_psum")
        q_sbuf = of_layer("q_sbuf")
        v_sbuf = of_layer("v_sbuf")
        k_sbuf = of_layer("k_sbuf")
        qk_squares = of_layer("qk_squares")
        qk_ready = of_layer("qk_ready")
        qkT_psum = of_layer("qkT_psum")
        qkT_sbuf = of_layer("qkT_sbuf")
        scores_psum = of_layer("scores_psum")
        row_max_ready = of_layer("row_max_ready")
        row_sum_inverted = of_layer("row_sum_inverted")
        probs_exp = of_layer("probs_exp")
        probs_ready = of_layer("probs_ready")
        probsT_psum = of_layer("probsT_psum")
        probsT_sbuf = of_layer("probsT_sbuf")
        o_psum = of_layer("o_psum")
        o_sbuf = of_layer("o_sbuf")
        b_scaled = of_layer("b_scaled")
        ssm_wT_psum = of_layer("ssm_wT_psum")
        ssm_b_sbuf = of_layer("ssm_b_sbuf")
        ssm_c_sbuf = of_layer("ssm_c_sbuf")
        key_shared = of_layer("key_shared")
        table_ready = of_layer("table_ready")
        bu_psum = of_layer("bu_psum")
        modulated = of_layer("modulated")
        turned_back = of_layer("turned_back")
        y_used = of_layer("y_used")
        y_psum = of_layer("y_psum")
        gelu_arg = of_layer("gelu_arg")
        gelu_tanh = of_layer("gelu_tanh")
        gelu_ready = of_layer("gelu_ready")
        gates_psum = of_layer("gates_psum")
        gates_sbuf = of_layer("gates_sbuf")
        glu_psum = of_layer("glu_psum")
        glu_gate_tanh = of_layer("glu_gate_tanh")
        glu_read = of_layer("glu_read")
        attn_proj_psum = of_layer("attn_proj_psum")
        merged_ready = of_layer("merged_ready")
        mergedT_psum = of_layer("mergedT_psum")
        mergedT_sbuf = of_layer("mergedT_sbuf")
        out_psum = of_layer("out_psum")
        x_mixed = of_layer("x_mixed")
        squares2 = of_layer("squares2")
        h2T_psum = of_layer("h2T_psum")
        h2T_sbuf = of_layer("h2T_sbuf")
        h2T_sbuf_second = of_layer("h2T_sbuf_second")
        logitsT_psum = of_layer("logitsT_psum")
        logitsT_sbuf = of_layer("logitsT_sbuf")
        logits_psum = of_layer("logits_psum")
        expo_ready = of_layer("expo_ready")
        routes_ready = of_layer("routes_ready")
        picked = of_layer("picked")
        rank_psum = of_layer("rank_psum")
        perm_ready = of_layer("perm_ready")
        offsets_ready = of_layer("offsets_ready")
        sorted_psum = of_layer("sorted_psum")
        sorted_sbuf = of_layer("sorted_sbuf")
        pair_copied = of_layer("pair_copied")
        hidden_psum = of_layer("hidden_psum")
        gate_tanh_ready = of_layer("gate_tanh_ready")
        hidden_half = of_layer("hidden_half")
        hidden_ready = of_layer("hidden_ready")
        sel_half = of_layer("sel_half")
        sel_ready = of_layer("sel_ready")
        turned_psum = of_layer("turned_psum")
        hiddenT_sbuf = of_layer("hiddenT_sbuf")
        selT_sbuf = of_layer("selT_sbuf")
        down_psum = of_layer("down_psum")
        down_sbuf_lo = of_layer("down_sbuf_lo")
        down_sbuf_hi = of_layer("down_sbuf_hi")
        own_pair_loaded = of_layer("own_pair_loaded")
        own_down_loaded = of_layer("own_down_loaded")
        moe_psum = of_layer("moe_psum")
        x_ready = of_layer("x_ready")
        rank_shifted = of_layer("rank_shifted")
        more_free = of_layer("more_free")
        more_loaded = of_layer("more_loaded")
        nums = [s.num for s in per_layer]
        assert nums == list(range(nums[0], nums[0] + len(nums))), nums
        x = sb("x", [P, TT, D])
        hT = sb("hT", [P, KC, SEQ])
        ringA = sb("ringA", [P, A_SLOTS, A_SIZE])
        ringB = sb("ringB", [P, B_SLOTS, B_SIZE])
        ident = sb("ident", [P, P])
        before = sb("before", [P, P])
        ones = sb("ones", [P, P])
        iota = sb("iota", [P, NPOS])
        local = sb("local", [P, TT * NE])
        own_group = sb("own_group", [P, 2 * GRP])
        amask = sb("amask", [P, CHUNK])
        cossin = sb("cossin", [P, 2, 2 * STILES + TT * HALF])
        rope = cossin[:, :, 2 * STILES:].rearrange("p i (t f) -> p i t f", t=TT)
        inv_freq = sb("inv_freq", [P, HALF])
        ssm_par = sb("ssm_par", [P, DEPTH, 3, STILES])
        ssm_now = sb("ssm_now", [P, 3, STILES])
        turn_lo = sb("turn_lo", [P, DEPTH, 2, STILES, 16])
        turn_hi = sb("turn_hi", [P, DEPTH, 2, STILES, 16])
        ssm_w = sb("ssm_w", [P, 5, CH_T, P])
        bT, cT = ssm_w[:, 0:2, :, :], ssm_w[:, 2:5, :, :]
        gains = sb("gains", [P, 2 * KC + QC + KVC])
        all_gains = sb("all_gains", [P, DEPTH, 2 * KC + QC + KVC])
        g_mix, g_ffn = gains[:, 0:KC], gains[:, KC:2 * KC]
        g_q, g_kv = gains[:, 2 * KC:2 * KC + QC], gains[:, 2 * KC + QC:]
        dskip = sb("dskip", [P, CH_T])
        wroute = sb("wroute", [P, KC, ROUTE])
        head_gain = sb("head_gain", [P, 2, ROPE])
        turn_gain = sb("turn_gain", [P, 2, TT, 2, ROPE])
        nope_gain = sb("nope_gain", [P, 2])
        norm = sb("norm", [P, 8, 32])

        ARENA = 21312
        arena = sb("arena", [P, ARENA])

        def at(lo, *shape):
            n = int(np.prod(shape))
            assert lo + n <= ARENA
            ap = arena[:, lo:lo + n]
            names = "abcd"[:len(shape)]
            if len(shape) > 1:
                ap = ap.rearrange(f"p ({' '.join(names)}) -> p {' '.join(names)}", **dict(zip(names, shape)))
            return ap

        gate_t = at(0, TT, 2 * D)
        uT = at(4096, CH_T, SEQ)
        qkv = at(5120, TT, U0)
        vtok = at(6464, TT, HEADS, VD)
        oT = at(5120, HEADS // 2, SEQ)
        tab_v = at(7488, 2, SEQ)
        garg = at(8000, SEQ)
        gtmp = at(8256, SEQ)
        turn = at(8512, 2, 2, SEQ)
        mulc = at(9536, 2, SEQ)
        muls = at(10048, 2, SEQ)
        driven = at(10560, 2, SEQ)
        state = at(11072, 2, SEQ)
        tab_u = at(11584, 2, SEQ)
        backc = at(12096, 2, 2, SEQ)
        backs = at(13120, 2, 2, SEQ)
        turn_tmp = at(20288, 4, DEPTH, STILES, 8)
        praw = at(17216, 3, P)
        dtraw = at(17600, 2)
        ppar = at(17604, 3, DEPTH * STILES)
        pang = at(17700, 4, 2 * STILES + TT * HALF)
        pwork = at(17956, 8, DEPTH * STILES)
        pos_f = at(18212, TT)
        braw = at(8512, 2, STILES, GRP)
        bbar = at(9024, 2, STILES, GRP)
        btmp = at(9536, 2, STILES, GRP)
        bwide = at(10048, 2, STILES, 2 * GRP)
        craw = at(12096, 2, CH_T, 2, NST)
        squared = at(14144, TT, D)
        diag = at(16192, TT, P)
        scale_row = at(16448, SEQ)
        qk = at(14144, TT, 2 * HEADS, QKD)
        qkT = at(17216, 2, 4, SEQ)
        lora = at(17216, TT, U0)
        loraT = at(18560, QC + KVC, SEQ)
        sq = at(17216, TT, 2 * HEADS, QKD)
        probs = at(19264, 4, SEQ)
        probsT = at(20288, 4, 2, P)
        glu_t = at(14144, TT, D)
        merged = at(16192, TT, D)
        attn_m = at(18240, D)
        squared2 = at(8960, TT, D)
        perm2 = hT[:, 0:2 * TT, :].rearrange("p (t c) s -> p t (c s)", t=TT)
        own_pair = at(13120, 2, A_SIZE)
        own_down = [ssm_w[:, 0:4, :, :].rearrange("p i m s -> p (i m s)"), hT[:, :, :].rearrange("p c s -> p (c s)")]
        sortedT = at(0, KC, NPOS + SLOT)
        pairT = at(4608, 2, KC, 2 * SLOT)
        gtanh = at(6656, 2, DE)
        hidden = at(7168, 2, DE)
        hiddenT = at(7680, 2, P)
        sel = at(7936, 2, TT, 2 * SLOT)
        selT = at(8448, 2, SEQ)
        down = at(8960, D)
        perm = at(9984, TT, NPOS)
        rt = at(11008, 24, TT, NE)
        roff = sb("roff", [P, PASSES, NE], I32)
        rmany = sb("rmany", [P, DEPTH], I32)
        pos_i = sb("pos_i", [P, TT], I32)
        logits = at(12544, TT, ROUTE)
        logitsT = at(11904, SEQ)
        expo_in = at(12624, TT, EG + 1)
        expo = at(12640, TT, EG + 1)
        r8 = at(12656, 10, TT, EPG)
        r4 = at(12816, 4, TT, EG)
        r1 = at(12848, 16, TT)
        count = at(12880, 3, NE)

        psum = ctx.enter_context(nc.psum_tensor("psum", [P, 8, 512], F32))

        def bank(i, lo=0, hi=512):
            return psum[:, i, lo:hi]

        def banks(i, n):
            return psum[:, i:i + n, :].rearrange("p b n -> p (b n)")

        XT_BANKS = (0, 1, 6, 7)

        w_in = t["w_in"].rearrange("l (c p) n -> l p c n", c=KC)
        w_uq = t["w_uq"].rearrange("l (p c) n -> l p c n", c=QC)
        w_ukv = t["w_ukv"].rearrange("l (p c) n -> l p c n", c=KVC)
        w_ap = t["w_attn_proj"].rearrange("l (c p) n -> l p c n", p=P)
        w_glu = t["w_glu"].rearrange("l (c p) n -> l p c n", p=P)
        w_out = t["w_out"].rearrange("l (c p) n -> l p c n", c=KC)
        w_gate = t["w_exp_gate"].rearrange("l e (p c) n -> (l e) p (c n)", c=KC)
        w_up = t["w_exp_up"].rearrange("l e (p c) n -> (l e) p (c n)", c=KC)
        w_down = t["w_exp_down"].rearrange("l e (p c) n -> (l e) p (c n)", c=2)

        def layer_of(ap, l):
            ap = ap[bass.ds(l, 1)]
            names = " ".join("bcdef"[:ap.ndim - 1])
            first_, rest = names.split(" ", 1) if " " in names else (names, "")
            return ap.rearrange(f"a {names} -> (a {first_}) {rest}")

        def slotA(a):
            return ringA[:, a % A_SLOTS, :]

        def slotA_kc(a):
            return slotA(a).rearrange("p (c n) -> p c n", c=KC)

        wtail = slotA(A_TAIL)[:, 0:KC * (U0 - 512)].rearrange("p (c n) -> p c n", c=KC)
        wuq = slotA(A_TAIL)[:, KC * (U0 - 512):KC * (U0 - 512) + QC * HEADS * QKD].rearrange("p (c n) -> p c n", c=QC)
        wukv = ringB[:, 0, :].rearrange("p (c n) -> p c n", c=KVC)

        def b_use(l, s, n):
            return l * (B_USES[s] + 1) + n + 1 if s == 0 else l * B_USES[s] + n

        def leave_layer(eng, l, clears=False):
            eng.drain().then_inc(layer_left, 1)
            if clears:
                eng.wait_ge(layer_left, l * 4 + 4)
                eng.sem_inc(held, 1)
                eng.sem_clear(range(nums[0], nums[-1] + 1))
                eng.drain().then_inc(layer_open, 1)
            eng.wait_ge(layer_open, l + 2)
            eng.sem_inc(held, 1)

        def crowded(eng, l):
            eng.wait_ge(counted, l + 1)
            eng.sem_inc(held, 1)
            return eng.value_load(rmany[0:1, bass.ds(l, 1)], min_val=0, max_val=1)

        def further_steps(eng, step, each_pass=None):
            with eng.Fori(1, PASSES) as r:
                if each_pass:
                    each_pass(r)
                with eng.Fori(0, NPAIR) as pair:
                    step(r * NPAIR + pair, pair, r)

        block = ctx.enter_context(nc.Block())

        @block.sync
        def _(sp):
            sp.dma_start(praw[0:2 * STILES, 0, :], t["lam_re"].rearrange("l (j g) p -> (l j) (g p)", g=2)).then_inc(first_params_loaded, 16)
            sp.dma_start(praw[0:2 * STILES, 1, :], t["lam_im"].rearrange("l (j g) p -> (l j) (g p)", g=2)).then_inc(first_params_loaded, 16)
            sp.dma_start(dtraw[0:2 * STILES, :], t["log_dt"].rearrange("l (j g) -> (l j) g", g=2)).then_inc(first_params_loaded, 16)
            sp.dma_start(pos_i[:, :], t["positions"].rearrange("b (t p) -> p (b t)", p=P),
                          allow_slow_non_contiguous=True).then_inc(first_positions_loaded, 16)
            for tt in range(TT):
                sp.dma_start(x[:, tt, :], t["x"][0, tt * P:(tt + 1) * P, :]).then_inc(first_x_loaded, 16)
            col = 0
            for k, chunks, order in (("norm_mix_g", KC, "(c p)"), ("norm_ffn_g", KC, "(p c)"), ("q_lora_g", QC, "(p c)"),
                                     ("kv_lora_g", KVC, "(p c)")):
                for layer in range(DEPTH):
                    sp.dma_start(all_gains[:, layer, col:col + chunks], t[k][layer].rearrange(f"{order} -> p c", c=chunks),
                                 allow_slow_non_contiguous=True).then_inc(first_gains_loaded, 16)
                col += chunks
            with sp.Fori(0, DEPTH) as l:
                layer_at = {k: layer_of(v, l) for k, v in (("in", w_in), ("uq", w_uq), ("ukv", w_ukv),
                                                           ("ap", w_ap), ("glu", w_glu), ("out", w_out))}

                def load_a(a, dst0, src0, dst1, src1):
                    s = a % A_SLOTS
                    sp.wait_ge(free_a[s], l * A_USES[s] + a // A_SLOTS + 1)
                    sp.sem_inc(held, 1)
                    sp.dma_start(dst0, src0).then_inc(loaded_a[s], 16)
                    sp.dma_start(dst1, src1).then_inc(loaded_a[s], 16)

                def load_a_cols(a, w, c0):
                    v = slotA_kc(a)
                    load_a(a, v[:, 0:KC // 2, :], w[:, 0:KC // 2, c0:c0 + 512],
                           v[:, KC // 2:KC, :], w[:, KC // 2:KC, c0:c0 + 512])

                load_a_cols(A_U, layer_at["in"], U0)
                load_a_cols(A_Q, layer_at["in"], 0)
                load_a(A_TAIL, wtail, layer_at["in"][:, :, 512:U0], wuq, layer_at["uq"])
                sp.wait_ge(free_b[0], l * (B_USES[0] + 1) + 1)
                sp.sem_inc(held, 1)
                sp.dma_start(wukv, layer_at["ukv"]).then_inc(loaded_b[0], 16)
                load_a_cols(A_G, layer_at["in"], G0)
                sp.wait_ge(layer_open, l + 1)
                sp.sem_inc(held, 1)
                for i, k in enumerate(("b_re", "b_im")):
                    sp.dma_start(braw[:, i, :, :], layer_of(t[k], l).rearrange("(j g) p i -> (g p) j i", g=2)).then_inc(b_loaded, 16)
                for i, k in enumerate(("c_re", "c_im")):
                    for half in range(2):
                        sp.dma_start(craw[:, i, :, half, :], layer_of(t[k], l).rearrange("(m g) i p -> (g i) m p", m=CH_T)).then_inc(c_loaded, 16)
                sp.dma_start(dskip[:, :], layer_of(t["d_skip"], l).rearrange("(m g) i -> (g i) m", m=CH_T), allow_slow_non_contiguous=True).then_inc(d_loaded, 16)
                for i, k in enumerate(("q_head_g", "k_head_g")):
                    g = t[k][bass.ds(l, 1), :]
                    sp.dma_start(head_gain[:, i, :], g[:, NOPE:].broadcast_to([P, ROPE])).then_inc(head_gains_loaded, 16)
                    sp.dma_start(nope_gain[0:NOPE, i:i + 1], g[:, 0:NOPE].rearrange("a n -> n a"),
                                 allow_slow_non_contiguous=True).then_inc(nope_gains_loaded, 16)
                sp.dma_start(wroute[:, :, 0:EG], layer_of(t["w_router_group"], l).rearrange("(p c) n -> p c n", c=KC)).then_inc(router_loaded, 16)
                sp.dma_start(wroute[:, :, EG:], layer_of(t["w_router_expert"], l).rearrange("(p c) n -> p c n", c=KC)).then_inc(router_loaded, 16)
                for g in range(1, 4):
                    load_a_cols(A_G + g, layer_at["in"], G0 + g * 512)
                for g in range(2):
                    v = slotA(A_GLU + g).rearrange("p (c n) -> p c n", c=CH_T)
                    src = layer_at["glu"][:, :, (1 - g) * D:(2 - g) * D]
                    load_a(A_GLU + g, v[:, 0:2, :], src[:, 0:2, :], v[:, 2:4, :], src[:, 2:4, :])
                v = slotA(A_AP).rearrange("p (c n) -> p c n", c=CH_T)
                load_a(A_AP, v[:, 0:2, :], layer_at["ap"][:, 0:2, :], v[:, 2:4, :], layer_at["ap"][:, 2:4, :])
                for g in range(2):
                    load_a_cols(A_OUT + g, layer_at["out"], g * 512)

                def expert(w, pair, e):
                    return w[bass.ds(l * NE + pair * 2 + e, 1)].rearrange("a p n -> (a p) n")

                def load_gate_up(pair, ring, n):
                    for e in range(2):
                        s = 2 * ring + e
                        sp.wait_ge(free_a[s], l * A_USES[s] + n + 1)
                        sp.sem_inc(held, 1)
                        sp.dma_start(ringA[:, s, 0:2048], expert(w_gate, pair, e)).then_inc(loaded_a[s], 16)
                        sp.dma_start(ringA[:, s, 2048:4096], expert(w_up, pair, e)).then_inc(loaded_a[s], 16)

                def load_down(pair, ring, n):
                    for e in range(2):
                        s = 2 * ring + e
                        sp.wait_ge(free_b[s], b_use(l, s, n) + 1)
                        sp.sem_inc(held, 1)
                        sp.dma_start(ringB[:, s, :], expert(w_down, pair, e)).then_inc(loaded_b[s], 16)

                for pair in range(2):
                    load_gate_up(pair, pair, A_FIRST)
                    load_down(pair, pair, 0)
                sp.wait_ge(mergedT_psum, 2 * TT)
                for e in range(2):
                    sp.dma_start(own_pair[:, e, 0:2048], expert(w_gate, OWN_PAIR, e)).then_inc(own_pair_loaded, 16)
                    sp.dma_start(own_pair[:, e, 2048:4096], expert(w_up, OWN_PAIR, e)).then_inc(own_pair_loaded, 16)
                sp.dma_start(own_down[0], expert(w_down, OWN_PAIR, 0)).then_inc(own_down_loaded, 16)
                sp.wait_ge(perm_ready, TT)
                sp.dma_start(own_down[1], expert(w_down, OWN_PAIR, 1)).then_inc(own_down_loaded, 16)
                load_gate_up(3, 0, A_FIRST + 1)
                with sp.Fori(0, NPAIR // 2 - 2) as i:
                    load_gate_up(i * 2 + 4, 1, i + A_FIRST + 1)
                    load_down(i * 2 + 3, 0, i + 1)
                    load_gate_up(i * 2 + 5, 0, i + A_FIRST + 2)
                    load_down(i * 2 + 4, 1, i + 1)
                load_down(NPAIR - 1, 0, B_USES[0] - 1)

                def reload(p, pair, r):
                    sp.wait_ge(more_free, p - (NPAIR - 1))
                    sp.sem_inc(held, 1)
                    e0 = sp.snap(l * NE + pair * 2)
                    for s in range(2):
                        src = [w[bass.ds(e0 + s, 1)].rearrange("a p n -> (a p) n") for w in (w_gate, w_up, w_down)]
                        sp.dma_start(ringA[:, s, 0:2048], src[0]).then_inc(more_loaded, 16)
                        sp.dma_start(ringA[:, s, 2048:4096], src[1]).then_inc(more_loaded, 16)
                        sp.dma_start(ringB[:, s, :], src[2]).then_inc(more_loaded, 16)

                with sp.If(crowded(sp, l) > 0):
                    further_steps(sp, reload)
                    sp.wait_ge(layer_open, l + 2)
                    sp.sem_inc(held, 1)
            for tt in range(TT):
                sp.wait_ge(first_result_ready, tt + 1)
                sp.dma_start(out[0, tt * P:(tt + 1) * P, :], x[:, tt, :]).then_inc(first_stored, 16)
            sp.wait_ge(first_stored, 16 * TT)

        @block.gpsimd
        def _(pool):
            pool.memset(ident[:, :], 0.0).then_inc(first_constants, 1)
            pool.memset(before[:, :], 1.0).then_inc(first_constants, 1)
            pool.memset(ones[:, :], 1.0).then_inc(first_constants, 1)
            pool.memset(own_group[:, :], 1.0).then_inc(first_constants, 1)
            pool.memset(amask[:, :], 0.0).then_inc(first_constants, 1)
            pool.memset(nope_gain[:, :], 1.0).then_inc(first_constants, 1)
            for j in range(HALF):
                pool.memset(inv_freq[:, j:j + 1], float(np.float32(THETA) ** np.float32(-j / HALF))).then_inc(first_constants, 1)
            pool.iota(local[:, :], pattern=[[0, TT * EG], [1, EPG]], base=-64, channel_multiplier=0,
                      allow_small_or_imprecise_dtypes=True).then_inc(first_constants, 1)
            pool.iota(iota[:, :], pattern=[[1, NPOS]], base=0, channel_multiplier=0,
                      allow_small_or_imprecise_dtypes=True).then_inc(first_constants, 1)
            n = 8 + HALF
            pool.wait_ge(first_constants, n)
            pool.sem_inc(layer_open, 1)
            pool.affine_select(out=ident[:, :], in_=ident[:, :], compare_op=ALU.not_equal, fill=1.0, base=0,
                               pattern=[[-1, P]], channel_multiplier=1).then_inc(first_constants, 1)
            pool.affine_select(out=before[:, :], in_=before[:, :], compare_op=ALU.is_gt, fill=0.0, base=0,
                               pattern=[[1, P]], channel_multiplier=-1).then_inc(first_constants, 1)
            pool.affine_select(out=own_group[:, 0:GRP], in_=own_group[:, 0:GRP], compare_op=ALU.is_ge, fill=0.0,
                               base=NST - 1, pattern=[[0, GRP]], channel_multiplier=-1).then_inc(first_constants, 1)
            pool.affine_select(out=own_group[:, GRP:], in_=own_group[:, GRP:], compare_op=ALU.is_ge, fill=0.0,
                               base=-NST, pattern=[[0, GRP]], channel_multiplier=1).then_inc(first_constants, 1)
            pool.affine_select(out=amask[:, :], in_=amask[:, :], compare_op=ALU.is_ge,
                               fill=MASKED, base=-CHUNK, pattern=[[0, CHUNK]], channel_multiplier=1).then_inc(first_constants, 1)

            done = Count()

            def shape(ap, n):
                return ap if n == 1 else ap.broadcast_to([P, DEPTH, STILES, n])

            def cmul(oc, os, a, b, n):
                tmp = [turn_tmp[:, i, :, :, 0:n] for i in range(4)]
                bcs = [shape(v, n) for v in b]
                pool.tensor_tensor(tmp[0], a[0], bcs[0], ALU.mult).then_inc(first_pool_chain, done.add())
                pool.tensor_tensor(tmp[1], a[1], bcs[1], ALU.mult).then_inc(first_pool_chain, done.add())
                pool.tensor_tensor(tmp[2], a[0], bcs[1], ALU.mult).then_inc(first_pool_chain, done.add())
                pool.tensor_tensor(tmp[3], a[1], bcs[0], ALU.mult).then_inc(first_pool_chain, done.add())
                pool.wait_ge(first_pool_chain, done.n)
                pool.tensor_tensor(oc, tmp[0], tmp[1], ALU.subtract).then_inc(first_pool_chain, done.add())
                pool.tensor_tensor(os, tmp[2], tmp[3], ALU.add).then_inc(first_pool_chain, done.add())
                pool.wait_ge(first_pool_chain, done.n)

            def parts(tab, b0, b1):
                return [tab[:, :, i, :, b0:b1] for i in range(2)]

            pool.wait_ge(first_theta_turned, 2)
            for tab in (turn_lo, turn_hi):
                for i in range(2):
                    pool.memset(tab[:, :, i, :, 0:1], 1.0 - i).then_inc(first_pool_chain, done.add())
            for i in range(2):
                pool.tensor_copy(turn_lo[:, :, i, :, 1:2], cossin[:, i, 0:2 * STILES].rearrange("p (l j o) -> p l j o", l=DEPTH, o=1)).then_inc(first_pool_chain, done.add())
            pool.wait_ge(first_pool_chain, done.n)
            for k, tab in enumerate((turn_lo, turn_hi)):
                for n in (2, 4, 8):
                    oc, os = parts(tab, n, n + 1)
                    cmul(oc, os, parts(tab, n // 2, n // 2 + 1), parts(tab, n // 2, n // 2 + 1), 1)
                    oc, os = parts(tab, n + 1, 2 * n)
                    cmul(oc, os, parts(tab, 1, n), parts(tab, n, n + 1), n - 1)
                if k == 0:
                    oc, os = parts(turn_hi, 1, 2)
                    cmul(oc, os, parts(tab, 8, 9), parts(tab, 8, 9), 1)

            with pool.Fori(0, DEPTH) as l:
                done = Count()

                lo = turn_lo[:, bass.ds(l, 1)].rearrange("p l i j b -> p (l i) j b")
                hi = turn_hi[:, bass.ds(l, 1)].rearrange("p l i j b -> p (l i) j b")
                for j in range(STILES):
                    if j == 0:
                        pool.wait_ge(ssm_wT_psum, 4)
                    if j >= 2:
                        pool.wait_ge(turned_back, j - 1)
                    a = bc(hi[:, :, j, :], 3, 16)
                    for k, dst in enumerate((tab_u, tab_v)):
                        b = bc(bc(lo[:, k, j, :], 1, 16), 1, 2)
                        pool.tensor_tensor(dst.rearrange("p i (a b) -> p i a b", b=16), a, b, ALU.mult).then_inc(pool_chain, done.add())
                    pool.wait_ge(pool_chain, done.n)
                    pool.tensor_tensor(turn[:, j % 2, 0, :], tab_u[:, 0, :], tab_v[:, 1, :],
                                       ALU.subtract).then_inc(table_ready, 1)
                    pool.tensor_tensor(turn[:, j % 2, 1, :], tab_u[:, 1, :], tab_v[:, 0, :],
                                       ALU.add).then_inc(table_ready, 1)
                    pool.wait_ge(table_ready, 2 * j + 2)

                pool.wait_ge(offsets_ready, 1 + PASSES)

                def copy_pair(p, par, first_uses):
                    offs = [pool.value_load(roff[0:1, 0, bass.ds(p * 2 + i, 1)], min_val=0, max_val=NPOS) for i in range(2)]
                    if first_uses:
                        pool.wait_ge(sorted_sbuf, KC)
                    else:
                        pool.wait_ge(hidden_psum, p - 1)
                        pool.sem_inc(held, 1)
                    for i, off in enumerate(offs):
                        pool.tensor_copy(pairT[:, par, :, i * SLOT:(i + 1) * SLOT],
                                         sortedT[:, :, bass.ds(off, SLOT)]).then_inc(pair_copied, 1)

                offs = [pool.value_load(roff[0:1, 0, i:i + 1], min_val=0, max_val=NPOS) for i in range(2)]
                for c in range(0, KC, 2):
                    pool.wait_ge(sorted_sbuf, c + 2)
                    for i, off in enumerate(offs):
                        last = pool.tensor_copy(pairT[:, 0, c:c + 2, i * SLOT:(i + 1) * SLOT], sortedT[:, c:c + 2, bass.ds(off, SLOT)])
                        if c == KC - 2:
                            last.then_inc(pair_copied, 1)
                copy_pair(1, 1, True)
                with pool.Fori(1, NPAIR // 2) as i:
                    for par in range(2):
                        copy_pair(i * 2 + par, par, False)

                def copy_more(p, pair, r):
                    pool.wait_ge(x_ready, (p - (NPAIR - 1)) * TT)
                    pool.sem_inc(held, 1)
                    for i in range(2):
                        off = pool.value_load(roff[0:1, bass.ds(r, 1), bass.ds(pair * 2 + i, 1)], min_val=0, max_val=NPOS)
                        pool.tensor_copy(pairT[:, 0, :, i * SLOT:(i + 1) * SLOT],
                                         sortedT[:, :, bass.ds(off, SLOT)]).then_inc(pair_copied, 1)

                with pool.If(crowded(pool, l) > 0):
                    further_steps(pool, copy_more)
                leave_layer(pool, l, clears=True)

        @block.scalar
        def _(act):
            act.wait_ge(first_params_loaded, 48)
            act.activation(dtraw[0:2 * STILES, :], dtraw[0:2 * STILES, :], ACT.Exp).then_inc(first_dt_ready, 1)
            act.wait_ge(first_decay_ready, 1)
            act.activation(pwork[:, 0, :], pwork[:, 1, :], ACT.Exp).then_inc(first_rho_ready, 1)
            act.wait_ge(first_angle_ready, 1)
            act.activation(cossin[:, 1, :], pang[:, 0, :], ACT.Sin).then_inc(first_theta_turned, 1)
            act.activation(pang[:, 3, :], pang[:, 0, :], ACT.Sin, scale=0.5).then_inc(first_half_sine, 1)

            with act.Fori(0, DEPTH) as l:
                act.wait_ge(gains_ready, 1)
                for c in range(KC // 2):
                    act.wait_ge(hT_psum, c // 2 + 1)
                    act.activation(hT[:, c, :], bank(XT_BANKS[c // 2], c % 2 * SEQ, c % 2 * SEQ + SEQ), ACT.Copy,
                                   scale=g_mix[:, c:c + 1]).then_inc(hT_sbuf, 1)
                act.wait_ge(first_x_loaded, 16 * TT)
                for tt in range(TT):
                    act.activation(squared[:, tt, :], x[:, tt, :], ACT.Square, scale=D ** -0.5, accum_out=norm[:, 0, tt:tt + 1]).then_inc(squares, 1)
                for i in range(2):
                    act.wait_ge(ssm_wT_psum, i + 1)
                    act.activation(bT[:, i, :, :], bank(2 + i).rearrange("p (m s) -> p m s", m=CH_T), ACT.Copy).then_inc(ssm_b_sbuf, 1)

                def lora_norm():
                    for tt in range(TT):
                        act.wait_ge(qkv_sbuf, 2 * tt + 2)
                        act.activation(lora[:, tt, 0:QR], qkv[:, tt, 0:QR], ACT.Square, scale=QR ** -0.5, accum_out=norm[:, 2, tt:tt + 1]).then_inc(lora_squares, 1)
                        act.activation(lora[:, tt, QR:QR + KVR], qkv[:, tt, QR:QR + KVR], ACT.Square, scale=KVR ** -0.5, accum_out=norm[:, 2, TT + tt:TT + tt + 1]).then_inc(lora_squares, 1)

                def lora_turn():
                    for c in range(QC + KVC):
                        act.wait_ge(loraT_psum, c + 1)
                        g = g_q[:, c:c + 1] if c < QC else g_kv[:, c - QC:c - QC + 1]
                        act.activation(loraT[:, c, :], bank(6 + c % 2, 0, SEQ), ACT.Copy, scale=g).then_inc(loraT_sbuf, 1)

                def q_out(tt):
                    act.wait_ge(q_psum, tt + 1)
                    for i in range(2):
                        act.activation(qk[:, tt, 4 * i:4 * i + 4, :], bank(6 + i, 0, 4 * QKD).rearrange("p (h d) -> p h d", h=4),
                                       ACT.Copy).then_inc(q_sbuf, 1)

                def kv_out(tt):
                    act.wait_ge(kv_psum, tt + 1)
                    for i in range(2):
                        src = bank(6 + i).rearrange("p (h d) -> p h d", h=4)
                        act.activation(qk[:, tt, HEADS + 4 * i:HEADS + 4 * i + 4, 0:NOPE], src[:, :, 0:NOPE], ACT.Copy).then_inc(k_sbuf, 1)
                        act.activation(vtok[:, tt, 4 * i:4 * i + 4, :], src[:, :, NOPE:], ACT.Copy).then_inc(v_sbuf, 1)

                def qk_square():
                    act.wait_ge(k_sbuf, 4)
                    act.wait_ge(key_shared, TT)
                    act.wait_ge(q_sbuf, 4)
                    for tt in range(TT):
                        act.activation(sq[:, tt, :, :], qk[:, tt, :, :], ACT.Square, scale=QKD ** -0.5).then_inc(qk_squares, 1)

                def qkT_out(hg):
                    act.wait_ge(nope_gains_loaded, 32)
                    for i in range(4):
                        n = 4 * hg + i
                        act.wait_ge(qkT_psum, n + 1)
                        act.activation(qkT[0:QKD, i // 2, 2 * (i % 2):2 * (i % 2) + 2, :],
                                       psum[0:QKD, 6 + i % 2, :].rearrange("p (h s) -> p h s", h=2), ACT.Copy,
                                       scale=nope_gain[0:QKD, i // 2:i // 2 + 1]).then_inc(qkT_sbuf, 1)

                def exps(c, qb):
                    w = P * (qb + 1)
                    for hh in range(4):
                        act.wait_ge(row_max_ready, 2 * c + hh // 2 + 1)
                        act.activation(probs[:, hh, 0:w], bank(6 + hh // 2, hh % 2 * w, (hh % 2 + 1) * w), ACT.Exp, scale=SCALE,
                                       bias=norm[:, 2, 12 + hh:13 + hh],
                                       accum_out=norm[:, 2, 4 + hh:5 + hh]).then_inc(probs_exp, 1)

                def shares(c, qb):
                    w = P * (qb + 1)
                    act.wait_ge(row_sum_inverted, c + 1)
                    for hh in range(4):
                        act.activation(probs[:, hh, 0:w], probs[:, hh, 0:w], ACT.Copy,
                                       scale=norm[:, 2, 8 + hh:9 + hh]).then_inc(probs_ready, 1)

                def probsT_out(c, qb):
                    act.wait_ge(probsT_psum, c + 1)
                    act.activation(probsT[:, :, 0:qb + 1, :],
                                   banks(6, 2)[:, 0:4 * (qb + 1) * P].rearrange("p (h k q) -> p h k q", h=4, k=qb + 1),
                                   ACT.Copy).then_inc(probsT_sbuf, 1)

                def o_out(c, hg, qb):
                    act.wait_ge(o_psum, c + 1)
                    act.activation(oT[:, 2 * hg:2 * hg + 2, qb * P:(qb + 1) * P],
                                   bank(5, 0, 2 * P).rearrange("p (c q) -> p c q", c=2), ACT.Copy).then_inc(o_sbuf, 1)

                def gate(g):
                    act.wait_ge(gates_psum, g + 1)
                    act.wait_ge(row_scales_ready, TT)
                    act.activation(gate_t[:, g % 2, (g // 2) * 512:(g // 2 + 1) * 512], bank(gate_bank(g)), ACT.Tanh,
                                   scale=norm[:, 7, 8 + g % 2:9 + g % 2]).then_inc(gates_sbuf, 1)

                def gelu(m):
                    act.wait_ge(gelu_arg, m + 1)
                    act.activation(gtmp, garg, ACT.Tanh, scale=math.sqrt(2.0 / math.pi)).then_inc(gelu_tanh, 1)

                lora_norm()
                for j in range(STILES):
                    for g in GATES_AT.get(j, []):
                        gate(g)
                    attention(j, dict(lora=lora_turn, q=lambda: (q_out(0), q_out(1)),
                                      kv=lambda: (kv_out(0), kv_out(1)), qk=qk_square, turn=qkT_out,
                                      scores=lambda c, hg, qb: exps(c, qb), probs=lambda c, hg, qb: (shares(c, qb), probsT_out(c, qb)),
                                      values=o_out))
                    if j % QPT == 0 and j:
                        gelu(j // QPT - 1)
                gelu(CH_T - 1)

                for tt in range(TT):
                    act.wait_ge(glu_psum, 1 + tt)
                    act.activation(glu_t[:, tt, :], banks(2 + 2 * tt, 2), ACT.Tanh, scale=0.25).then_inc(glu_gate_tanh, 1)
                for tt in range(TT):
                    for i in range(2):
                        act.wait_ge(mergedT_psum, 2 * tt + i + 1)
                        act.activation(hT[:, 4 * i:4 * i + 4, tt * P:(tt + 1) * P],
                                       bank(4 - 2 * tt + i).rearrange("p (c s) -> p c s", c=4), ACT.Copy).then_inc(mergedT_sbuf, 1)

                for tt in range(TT):
                    act.wait_ge(x_mixed, tt + 1)
                    act.activation(squared2[:, tt, :], x[:, tt, :], ACT.Square, scale=D ** -0.5, accum_out=norm[:, 1, tt:tt + 1]).then_inc(squares2, 1)
                    if tt == 0:
                        for c in range(KC):
                            act.wait_ge(h2T_psum, c // 4 + 1)
                            act.activation(hT[:, c, 0:P], bank(4 + c // 4, c % 4 * P, (c % 4 + 1) * P), ACT.Copy,
                                           scale=g_ffn[:, c:c + 1]).then_inc(h2T_sbuf, 1)
                act.wait_ge(logitsT_psum, 1)
                act.activation(logitsT[0:ROUTE, :], psum[0:ROUTE, 0, 0:SEQ], ACT.Copy).then_inc(logitsT_sbuf, 1)
                act.wait_ge(picked, 1)
                act.activation(expo, expo_in, ACT.Exp).then_inc(expo_ready, 1)
                for c in range(KC):
                    act.wait_ge(sorted_psum, c + 1)
                    act.activation(sortedT[:, c, 0:NPOS], bank(c % 4), ACT.Copy, scale=g_ffn[:, c:c + 1]).then_inc(sorted_sbuf, 1)

                def gate_tanh(p, par):
                    act.wait_ge(hidden_psum, p + 1)
                    act.sem_inc(held, 1)
                    act.activation(gtanh[:, par, :], bank(par, 0, DE), ACT.Tanh, scale=0.5).then_inc(gate_tanh_ready, 1)

                def turned(p, par):
                    act.wait_ge(turned_psum, p + 1)
                    act.sem_inc(held, 1)
                    act.activation(hiddenT[:, :, :], bank(par, 0, 2 * P).rearrange("p (c s) -> p c s", c=2), ACT.Copy).then_inc(hiddenT_sbuf, 1)

                def down_lo(p):
                    act.wait_ge(down_psum, p + 1)
                    act.sem_inc(held, 1)
                    act.activation(down[:, 0:512], bank(2), ACT.Copy).then_inc(down_sbuf_lo, 1)

                gate_tanh(0, 0)

                def step(p, par, last=False):
                    turned(p, par)
                    down_lo(p)
                    if not last:
                        gate_tanh(p + 1, 1 - par)

                with act.Fori(0, NPAIR // 2 - 1) as i:
                    for par in range(2):
                        step(i * 2 + par, par)
                step(NPAIR - 2, 0)
                step(NPAIR - 1, 1, last=True)

                def more(p, pair, r):
                    gate_tanh(p, 0)
                    turned(p, 0)
                    down_lo(p)

                with act.If(crowded(act, l) > 0):
                    further_steps(act, more)
                leave_layer(act, l)

        @block.vector
        def _(dve):
            TS, TTN, STT = dve.tensor_scalar, dve.tensor_tensor, dve.scalar_tensor_tensor

            def rsqrt(done, dst, src):
                w = src.shape[-1]
                v, y, a = (norm[:, i, 0:w] for i in (4, 5, 6))
                TS(a, src, EPS, None, ALU.add).then_inc(dve_chain, done.add())
                dve.wait_ge(dve_chain, done.n)
                TS(v, a, -0.5, None, ALU.mult).then_inc(dve_chain, done.add())
                TS(y.bitcast(I32), a.bitcast(I32), 1, None, ALU.logical_shift_right).then_inc(dve_chain, done.add())
                dve.wait_ge(dve_chain, done.n)
                TS(y.bitcast(I32), y.bitcast(I32), -1.0, float(0x5F3759DF), ALU.mult, ALU.add).then_inc(dve_chain, done.add())
                dve.wait_ge(dve_chain, done.n)
                for k in range(3):
                    TTN(a, y, y, ALU.mult).then_inc(dve_chain, done.add())
                    dve.wait_ge(dve_chain, done.n)
                    TTN(a, a, v, ALU.mult).then_inc(dve_chain, done.add())
                    dve.wait_ge(dve_chain, done.n)
                    STT(out=dst if k == 2 else y, in0=a, scalar=1.5, in1=y, op0=ALU.add, op1=ALU.mult).then_inc(dve_chain, done.add())
                    dve.wait_ge(dve_chain, done.n)

            done = Count()
            NW = DEPTH * STILES
            dtx = praw[0:NW, 2, :].rearrange("p (g s) -> p g s", g=2)
            dve.wait_ge(first_dt_ready, 1)
            dve.tensor_copy(dtx, bc(dtraw[0:NW, :], 2, NST)).then_inc(first_dt_wide, 1)
            dve.wait_ge(first_params_turned, 1)
            dve.tensor_copy(ppar[:, :, :], bank(5, 0, 3 * NW).rearrange("p (i w) -> p i w", i=3)).then_inc(first_dve_chain, done.add())
            dve.wait_ge(first_dve_chain, done.n)
            re, im, dt = (ppar[:, i, :] for i in range(3))
            TTN(pwork[:, 1, :], re, dt, ALU.mult).then_inc(first_decay_ready, 1)
            TTN(pang[:, 1, 0:NW], im, dt, ALU.mult).then_inc(first_dve_chain, done.add())
            dve.wait_ge(first_positions_loaded, 16)
            dve.tensor_copy(pos_f, pos_i[:, :]).then_inc(first_dve_chain, done.add())
            dve.wait_ge(first_dve_chain, done.n)
            dve.wait_ge(first_constants, 8 + HALF + 5)
            TTN(pang[:, 1, NW:].rearrange("p (t f) -> p t f", t=TT), bc(pos_f, 2, HALF), bc(inv_freq[:, :], 1, TT), ALU.mult).then_inc(first_dve_chain, done.add())
            dve.wait_ge(first_dve_chain, done.n)
            ang, whole, r = pang[:, 1, :], pang[:, 2, :], pang[:, 0, :]
            TS(whole, ang, 1.0 / TWO_PI, ROUND, ALU.mult, ALU.add).then_inc(first_dve_chain, done.add())
            dve.wait_ge(first_dve_chain, done.n)
            TS(whole, whole, ROUND, None, ALU.subtract).then_inc(first_dve_chain, done.add())
            dve.wait_ge(first_dve_chain, done.n)
            src = ang
            for part in split_two_pi():
                STT(out=r, in0=whole, scalar=-part, in1=src, op0=ALU.mult, op1=ALU.add).then_inc(first_dve_chain, done.add())
                dve.wait_ge(first_dve_chain, done.n)
                src = r
            pi = float(np.nextafter(np.float32(math.pi), np.float32(0)))
            TS(r, r, pi, -pi, ALU.min, ALU.max).then_inc(first_angle_ready, 1)
            dve.wait_ge(first_half_sine, 1)
            TTN(pang[:, 2, :], pang[:, 3, :], pang[:, 3, :], ALU.mult).then_inc(first_dve_chain, done.add())
            dve.wait_ge(first_dve_chain, done.n)
            TS(cossin[:, 0, :], pang[:, 2, :], -2.0, 1.0, ALU.mult, ALU.add).then_inc(first_theta_turned, 1)
            dve.wait_ge(first_theta_turned, 2)
            dve.wait_ge(first_rho_ready, 1)
            rho = pwork[:, 0, :]
            lr, li, den, t0, t1 = (pwork[:, i, :] for i in range(2, 7))

            def par_of(i):
                return ssm_par[:, :, i, :]

            def lj(ap):
                return ap.rearrange("p (l j) -> p l j", l=DEPTH)

            dve.tensor_copy(par_of(0), lj(rho)).then_inc(first_dve_chain, done.add())
            TTN(lr, rho, cossin[:, 0, 0:NW], ALU.mult).then_inc(first_dve_chain, done.add())
            TTN(li, rho, cossin[:, 1, 0:NW], ALU.mult).then_inc(first_dve_chain, done.add())
            TTN(t0, re, re, ALU.mult).then_inc(first_dve_chain, done.add())
            TTN(t1, im, im, ALU.mult).then_inc(first_dve_chain, done.add())
            dve.wait_ge(first_dve_chain, done.n)
            TTN(den, t0, t1, ALU.add).then_inc(first_dve_chain, done.add())
            TS(lr, lr, 1.0, None, ALU.subtract).then_inc(first_dve_chain, done.add())
            dve.wait_ge(first_dve_chain, done.n)
            dve.reciprocal(den, den).then_inc(first_dve_chain, done.add())
            TTN(t0, lr, re, ALU.mult).then_inc(first_dve_chain, done.add())
            TTN(t1, li, im, ALU.mult).then_inc(first_dve_chain, done.add())
            dve.wait_ge(first_dve_chain, done.n)
            TTN(t0, t0, t1, ALU.add).then_inc(first_dve_chain, done.add())
            dve.wait_ge(first_dve_chain, done.n)
            TTN(par_of(1), lj(t0), lj(den), ALU.mult).then_inc(first_dve_chain, done.add())
            dve.wait_ge(first_dve_chain, done.n)
            TTN(t0, li, re, ALU.mult).then_inc(first_dve_chain, done.add())
            TTN(t1, lr, im, ALU.mult).then_inc(first_dve_chain, done.add())
            dve.wait_ge(first_dve_chain, done.n)
            TTN(t0, t0, t1, ALU.subtract).then_inc(first_dve_chain, done.add())
            dve.wait_ge(first_dve_chain, done.n)
            TTN(par_of(2), lj(t0), lj(den), ALU.mult).then_inc(first_dve_chain, done.add())
            dve.wait_ge(first_dve_chain, done.n)

            with dve.Fori(0, DEPTH) as l:
                done = Count()

                dve.wait_ge(first_gains_loaded, 64 * DEPTH)
                dve.tensor_copy(gains[:, :], all_gains[:, bass.ds(l, 1), :].rearrange("p a i -> p (a i)")).then_inc(gains_ready, 1)
                dve.tensor_copy(ssm_now[:, :, :], ssm_par[:, bass.ds(l, 1), :, :].rearrange("p a i j -> p (a i) j")).then_inc(dve_chain, done.add())
                dve.wait_ge(gains_ready, 1)
                for c in range(KC // 2, KC):
                    dve.wait_ge(hT_psum, c // 2 + 1)
                    TS(hT[:, c, :], bank(XT_BANKS[c // 2], c % 2 * SEQ, c % 2 * SEQ + SEQ), g_mix[:, c:c + 1], None, ALU.mult).then_inc(hT_sbuf_high, 1)
                dve.wait_ge(squares, TT)
                rsqrt(done, norm[:, 7, 0:TT], norm[:, 0, 0:TT])
                TS(norm[:, 7, 8:8 + TT], norm[:, 7, 0:TT], 0.5, None, ALU.mult).then_inc(dve_chain, done.add())
                for tt in range(TT):
                    TS(diag[:, tt, :], ident[:, :], norm[:, 7, tt:tt + 1], None, ALU.mult).then_inc(row_scales_ready, 1)

                dve.wait_ge(b_loaded, 32)
                f_re, f_im = (bc(ssm_now[:, i, :], 2, GRP) for i in (1, 2))
                b_re, b_im = braw[:, 0, :, :], braw[:, 1, :, :]
                for dst, fa, fb, op in ((0, f_re, f_im, ALU.subtract), (1, f_im, f_re, ALU.add)):
                    TTN(bbar[:, dst, :, :], b_re, fa, ALU.mult).then_inc(dve_chain, done.add())
                    TTN(btmp[:, dst, :, :], b_im, fb, ALU.mult).then_inc(dve_chain, done.add())
                    dve.wait_ge(dve_chain, done.n)
                    TTN(bbar[:, dst, :, :], bbar[:, dst, :, :], btmp[:, dst, :, :], op).then_inc(dve_chain, done.add())
                    dve.wait_ge(dve_chain, done.n)
                    TTN(bwide[:, dst, :, :].rearrange("p j (g i) -> p j g i", g=2), bc(bbar[:, dst, :, :], 2, 2),
                        bc(own_group[:, :].rearrange("p (g i) -> p g i", g=2), 1, STILES), ALU.mult).then_inc(b_scaled, 1)

                dve.wait_ge(scale_row_psum, 1)
                dve.tensor_copy(scale_row, bank(0, 0, SEQ)).then_inc(scale_row_sbuf, 1)
                dve.wait_ge(scale_row_sbuf, 1)
                for m in range(CH_T):
                    dve.wait_ge(u_psum, m + 1)
                    TTN(uT[:, m, :], bank(2 + m, 0, SEQ), scale_row, ALU.mult).then_inc(u_sbuf, 1)

                dve.wait_ge(head_gains_loaded, 32)
                for i in range(2):
                    for tt in range(TT):
                        TTN(turn_gain[:, i, tt, :, :].rearrange("p w (i f) -> p w i f", i=2), head_gain[:, :, :].rearrange("p w (i f) -> p w i f", i=2),
                            bc(bc(rope[:, i, tt, :], 1, 2), 1, 2), ALU.mult).then_inc(dve_chain, done.add())
                for tt in range(TT):
                    dve.wait_ge(qkv_psum, tt + 1)
                    b0 = (6, 0)[tt]
                    TS(qkv[:, tt, 0:512], bank(b0), norm[:, 7, tt:tt + 1], None, ALU.mult).then_inc(qkv_sbuf, 1)
                    TS(qkv[:, tt, 512:U0], bank(b0 + 1, 0, U0 - 512), norm[:, 7, tt:tt + 1], None, ALU.mult).then_inc(qkv_sbuf, 1)

                own = bc(own_group[:, :], 1, CH_T * QPT)
                for i in range(2):
                    dve.wait_ge(ssm_wT_psum, 3 + i)
                    src = bank(4 + i).rearrange("p (q s) -> p q s", s=2 * GRP)
                    dst = cT[:, 2 * i, :, :].rearrange("p m (q s) -> p (m q) s", s=2 * GRP)
                    STT(out=dst, in0=src, scalar=1.0 - 2 * i, in1=own, op0=ALU.mult, op1=ALU.mult).then_inc(ssm_c_sbuf, 1)
                dve.wait_ge(ssm_c_sbuf, 1)
                TS(cT[:, 1, :, :], cT[:, 0, :, :], -1.0, None, ALU.mult).then_inc(ssm_c_sbuf, 1)

                def lora_scale():
                    dve.wait_ge(lora_squares, 2 * TT)
                    rsqrt(done, norm[:, 7, 2:6], norm[:, 2, 0:4])
                    for tt in range(TT):
                        TS(lora[:, tt, 0:QR], qkv[:, tt, 0:QR], norm[:, 7, 2 + tt:3 + tt], None, ALU.mult).then_inc(lora_ready, 1)
                        TS(lora[:, tt, QR:QR + KVR], qkv[:, tt, QR:QR + KVR], norm[:, 7, 4 + tt:5 + tt], None, ALU.mult).then_inc(lora_ready, 1)

                def shared_key():
                    dve.wait_ge(hT_psum, 4)
                    for tt in range(TT):
                        dve.tensor_copy(qk[:, tt, HEADS:, NOPE:], bc(qkv[:, tt, QR + KVR:U0], 1, HEADS)).then_inc(key_shared, 1)
                    for tt in range(TT):
                        dve.wait_ge(qk_squares, tt + 1)
                        dve.tensor_reduce(norm[:, 2, tt * 16:tt * 16 + 16], sq[:, tt, :, :], AXX, ALU.add).then_inc(dve_chain, done.add())
                    dve.wait_ge(dve_chain, done.n)
                    W = TT * 2 * HEADS
                    rsqrt(done, norm[:, 3, 0:W], norm[:, 2, 0:W])
                    for tt in range(TT):
                        TTN(qk[:, tt, :, :], qk[:, tt, :, :], bc(norm[:, 3, tt * 16:tt * 16 + 16], 2, QKD), ALU.mult).then_inc(dve_chain, done.add())
                    dve.wait_ge(dve_chain, done.n)
                    for tt in range(TT):
                        half = qk[:, tt, :, NOPE:].rearrange("p h (i f) -> p h i f", i=2)
                        ca = sq[:, 0, :, 0:ROPE].rearrange("p h (i f) -> p h i f", i=2)
                        sa = sq[:, 1, :, 0:ROPE].rearrange("p h (i f) -> p h i f", i=2)
                        for i in range(2):
                            TTN(sq[:, i, :, 0:ROPE].rearrange("p (w h) d -> p w h d", w=2), qk[:, tt, :, NOPE:].rearrange("p (w h) d -> p w h d", w=2),
                                bc(turn_gain[:, i, tt, :, :], 2, HEADS), ALU.mult).then_inc(dve_chain, done.add())
                        dve.wait_ge(dve_chain, done.n)
                        TTN(half[:, :, 0, :], ca[:, :, 0, :], sa[:, :, 1, :], ALU.subtract).then_inc(dve_chain, done.add())
                        TTN(half[:, :, 1, :], ca[:, :, 1, :], sa[:, :, 0, :], ALU.add).then_inc(dve_chain, done.add())
                        dve.wait_ge(dve_chain, done.n)
                    dve.engine_nop().then_inc(qk_ready, 1)

                def row_max(c, hg, qb):
                    w = P * (qb + 1)
                    for b in range(2):
                        dve.wait_ge(scores_psum, 2 * c + b + 1)
                        dve.tensor_reduce(norm[:, 2, 2 * b:2 * b + 2], bank(6 + b, 0, 2 * w).rearrange("p (h k) -> p h k", h=2),
                                          AXX, ALU.max).then_inc(dve_chain, done.add())
                        dve.wait_ge(dve_chain, done.n)
                        TS(norm[:, 2, 12 + 2 * b:14 + 2 * b], norm[:, 2, 2 * b:2 * b + 2], -SCALE, None, ALU.mult).then_inc(row_max_ready, 1)

                def row_sum(c, hg, qb):
                    dve.wait_ge(probs_exp, 4 * (c + 1))
                    dve.reciprocal(norm[:, 2, 8:12], norm[:, 2, 4:8]).then_inc(row_sum_inverted, 1)

                def drive(j):
                    bu = bank(j % 2).rearrange("p (i s) -> p i s", i=2)
                    cos, sin = (bc(turn[:, j % 2, i, :], 1, 2) for i in range(2))
                    dve.wait_ge(table_ready, 2 * j + 2)
                    dve.wait_ge(bu_psum, j + 1)
                    TTN(mulc, bu, cos, ALU.mult).then_inc(dve_chain, done.add())
                    TTN(muls, bu, sin, ALU.mult).then_inc(dve_chain, done.add())
                    dve.wait_ge(dve_chain, done.n)
                    TTN(driven[:, 0, :], mulc[:, 0, :], muls[:, 1, :], ALU.add).then_inc(modulated, 1)
                    TTN(driven[:, 1, :], mulc[:, 1, :], muls[:, 0, :], ALU.subtract).then_inc(modulated, 1)
                    dve.wait_ge(modulated, 2 * j + 2)
                    decay = ssm_now[:, 0, j:j + 1].broadcast_to([P, SEQ])
                    for i in range(2):
                        dve.tensor_tensor_scan(state[:, i, :], decay, driven[:, i, :], 0.0, ALU.mult, ALU.add).then_inc(dve_chain, done.add())
                    dve.wait_ge(dve_chain, done.n)

                def back(j):
                    cos, sin = (bc(turn[:, j % 2, i, :], 1, 2) for i in range(2))
                    if j >= 2:
                        dve.wait_ge(y_used, j - 1)
                    TTN(backc[:, j % 2, :, :], state, cos, ALU.mult).then_inc(dve_chain, done.add())
                    TTN(backs[:, j % 2, :, :], state, sin, ALU.mult).then_inc(turned_back, 1)

                def skip(m):
                    dve.wait_ge(y_psum, m + 1)
                    dve.wait_ge(d_loaded, 16)
                    y = uT[:, m, :]
                    STT(out=y, in0=y, scalar=dskip[:, m:m + 1], in1=bank(2 + m % 2, 0, SEQ), op0=ALU.mult, op1=ALU.add).then_inc(dve_chain, done.add())
                    dve.wait_ge(dve_chain, done.n)
                    TTN(garg, y, y, ALU.mult).then_inc(dve_chain, done.add())
                    dve.wait_ge(dve_chain, done.n)
                    TS(garg, garg, 0.044715, 1.0, ALU.mult, ALU.add).then_inc(dve_chain, done.add())
                    dve.wait_ge(dve_chain, done.n)
                    TTN(garg, garg, y, ALU.mult).then_inc(gelu_arg, 1)

                def gelu(m):
                    dve.wait_ge(gelu_tanh, m + 1)
                    STT(out=uT[:, m, :], in0=gtmp, scalar=1.0, in1=uT[:, m, :], op0=ALU.add, op1=ALU.mult).then_inc(gelu_ready, 1)

                for j in range(STILES):
                    drive(j)
                    attention(j, dict(probs=row_sum))
                    back(j)
                    attention(j, dict(lora=lora_scale, qk=shared_key, scores=row_max))
                    if j % QPT == 0 and j:
                        skip(j // QPT - 1)
                    if j % QPT == 1 and j > 1:
                        gelu(j // QPT - 1)
                skip(CH_T - 1)
                gelu(CH_T - 1)

                for tt in range(TT):
                    vbank, abank = ((0, 6), (2, 0))[tt]
                    dve.wait_ge(glu_gate_tanh, tt + 1)
                    dve.wait_ge(glu_psum, 3 + tt)
                    STT(out=merged[:, tt, :], in0=glu_t[:, tt, :], scalar=1.0, in1=banks(vbank, 2), op0=ALU.add, op1=ALU.mult).then_inc(glu_read, 1)
                    dve.wait_ge(gates_sbuf, 8)
                    dve.wait_ge(attn_proj_psum, 2 * tt + 2)
                    if tt:
                        dve.wait_ge(merged_ready, tt)
                    STT(out=attn_m, in0=gate_t[:, tt, 0:D], scalar=1.0, in1=banks(abank, 2), op0=ALU.add, op1=ALU.mult).then_inc(dve_chain, done.add())
                    dve.wait_ge(glu_read, tt + 1)
                    STT(out=merged[:, tt, :], in0=gate_t[:, tt, D:], scalar=1.0, in1=merged[:, tt, :], op0=ALU.add, op1=ALU.mult).then_inc(dve_chain, done.add())
                    dve.wait_ge(dve_chain, done.n)
                    STT(out=merged[:, tt, :], in0=merged[:, tt, :], scalar=0.25, in1=attn_m, op0=ALU.mult, op1=ALU.add).then_inc(merged_ready, 1)
                for tt in range(TT):
                    dve.wait_ge(out_psum, tt + 1)
                    STT(out=x[:, tt, :], in0=banks((6, 0)[tt], 2), scalar=0.5, in1=x[:, tt, :], op0=ALU.mult, op1=ALU.add).then_inc(x_mixed, 1)
                for c in range(KC):
                    dve.wait_ge(h2T_psum, 2 + c // 4 + 1)
                    TS(hT[:, c, P:], bank(2 + c // 4, c % 4 * P, (c % 4 + 1) * P), g_ffn[:, c:c + 1], None, ALU.mult).then_inc(h2T_sbuf_second, 1)
                dve.wait_ge(squares2, TT)
                rsqrt(done, norm[:, 7, 6:6 + TT], norm[:, 1, 0:TT])

                def red(dst, src, op):
                    dve.tensor_reduce(dst, src, AXX, op).then_inc(dve_chain, done.add())
                    dve.wait_ge(dve_chain, done.n)

                dve.wait_ge(logits_psum, 1)
                for tt in range(TT):
                    TS(logits[:, tt, :], bank(0, tt * 64, tt * 64 + ROUTE), norm[:, 7, 6 + tt:7 + tt], None, ALU.mult).then_inc(dve_chain, done.add())
                dve.wait_ge(dve_chain, done.n)
                lg, le = logits[:, :, 0:EG], logits[:, :, EG:].rearrange("p t (g e) -> p t g e", g=EG)
                v = [r1[:, i, :] for i in range(16)]
                def over(ap):
                    return ap.rearrange("p t (g e) -> p t g e", g=EG)

                everywhere = [rt[:, i, :, :].rearrange("p t (g e) -> p (t g) e", g=EG) for i in range(16, 23)]
                shifted, is1, is2, without, low, first1, first2 = everywhere
                best1, best2, least1, least2 = (r4[:, i, :, :].rearrange("p t g -> p (t g)") for i in range(4))
                idx4 = bc(iota[:, 0:EG], 1, TT)
                idx8 = local[:, :].rearrange("p (x e) -> p x e", e=EPG)
                group, at_max, low4, v_group = (r8[:, i, :, 0:EG] for i in range(4))
                dve.tensor_reduce(v[0], lg, AXX, ALU.max).then_inc(dve_chain, done.add())
                dve.tensor_reduce(r4[:, 0, :, :], le, AXX, ALU.max).then_inc(dve_chain, done.add())
                dve.wait_ge(dve_chain, done.n)
                TTN(at_max, lg, bc(v[0], 2, EG), ALU.is_equal).then_inc(dve_chain, done.add())
                TTN(over(rt[:, 17, :, :]), le, bc(r4[:, 0, :, :], 3, EPG), ALU.is_equal).then_inc(dve_chain, done.add())
                TTN(expo_in[:, :, 0:EG], lg, bc(v[0], 2, EG), ALU.subtract).then_inc(dve_chain, done.add())
                TTN(over(rt[:, 16, :, :]), le, bc(r4[:, 0, :, :], 3, EPG), ALU.subtract).then_inc(dve_chain, done.add())
                dve.wait_ge(dve_chain, done.n)
                STT(out=low4, in0=idx4, scalar=-64.0, in1=at_max, op0=ALU.add, op1=ALU.mult).then_inc(dve_chain, done.add())
                TTN(low, idx8, is1, ALU.mult).then_inc(dve_chain, done.add())
                dve.wait_ge(dve_chain, done.n)
                dve.tensor_reduce(v[1], low4, AXX, ALU.min).then_inc(dve_chain, done.add())
                dve.tensor_reduce(least1, low, AXX, ALU.min).then_inc(dve_chain, done.add())
                dve.wait_ge(dve_chain, done.n)
                STT(out=group, in0=idx4, scalar=-64.0, in1=bc(v[1], 2, EG), op0=ALU.add, op1=ALU.is_equal).then_inc(dve_chain, done.add())
                TTN(first1, idx8, bc(least1, 2, EPG), ALU.is_equal).then_inc(dve_chain, done.add())
                dve.wait_ge(dve_chain, done.n)
                STT(out=without, in0=first1, scalar=MASKED, in1=shifted, op0=ALU.mult, op1=ALU.add).then_inc(dve_chain, done.add())
                dve.wait_ge(dve_chain, done.n)
                dve.tensor_reduce(best2, without, AXX, ALU.max).then_inc(dve_chain, done.add())
                dve.wait_ge(dve_chain, done.n)
                TTN(is2, without, bc(best2, 2, EPG), ALU.is_equal).then_inc(dve_chain, done.add())
                TTN(v_group, r4[:, 1, :, :], group, ALU.mult).then_inc(dve_chain, done.add())
                dve.wait_ge(dve_chain, done.n)
                TTN(low, idx8, is2, ALU.mult).then_inc(dve_chain, done.add())
                dve.tensor_reduce(expo_in[:, :, EG:EG + 1].rearrange("p t o -> p (t o)"), v_group, AXX, ALU.add).then_inc(picked, 1)
                dve.wait_ge(dve_chain, done.n)
                dve.tensor_reduce(least2, low, AXX, ALU.min).then_inc(dve_chain, done.add())
                dve.wait_ge(dve_chain, done.n)
                TTN(first2, idx8, bc(least2, 2, EPG), ALU.is_equal).then_inc(dve_chain, done.add())
                dve.wait_ge(dve_chain, done.n)
                oh1, oh2, routed, weight, place, tmp, rank1 = (rt[:, i, :, :] for i in range(1, 8))

                TTN(over(oh1), over(rt[:, 21, :, :]), bc(group, 3, EPG), ALU.mult).then_inc(dve_chain, done.add())
                TTN(over(oh2), over(rt[:, 22, :, :]), bc(group, 3, EPG), ALU.mult).then_inc(dve_chain, done.add())
                dve.wait_ge(dve_chain, done.n)
                TTN(routed, oh1, oh2, ALU.add).then_inc(routes_ready, 1)
                dve.wait_ge(expo_ready, 1)
                red(v[6], expo[:, :, 0:EG], ALU.add)
                TS(v[7], expo[:, :, EG:EG + 1].rearrange("p t o -> p (t o)"), 1.0, None, ALU.add).then_inc(dve_chain, done.add())
                dve.wait_ge(dve_chain, done.n)
                TTN(v[8], v[6], v[7], ALU.mult).then_inc(dve_chain, done.add())
                dve.wait_ge(dve_chain, done.n)
                dve.reciprocal(v[9], v[8]).then_inc(dve_chain, done.add())
                dve.wait_ge(dve_chain, done.n)
                TTN(v[10], v[9], expo[:, :, EG:EG + 1].rearrange("p t o -> p (t o)"), ALU.mult).then_inc(dve_chain, done.add())
                dve.wait_ge(dve_chain, done.n)
                TTN(weight, oh1, bc(v[9], 2, NE), ALU.mult).then_inc(dve_chain, done.add())
                TTN(tmp, oh2, bc(v[10], 2, NE), ALU.mult).then_inc(dve_chain, done.add())
                dve.wait_ge(dve_chain, done.n)
                TTN(weight, weight, tmp, ALU.add).then_inc(dve_chain, done.add())
                dve.wait_ge(rank_psum, 1)
                rank = bank(1, 0, TT * NE).rearrange("p (t e) -> p t e", t=TT)
                dve.tensor_reduce(count[:, 0, :], bank(1, TT * NE, 2 * TT * NE).rearrange("p (t e) -> p e t", t=TT), AXX, ALU.add).then_inc(dve_chain, done.add())
                dve.wait_ge(dve_chain, done.n)
                dve.tensor_tensor_scan(count[:, 1, :], ones[:, 0:NE], count[:, 0, :], 0.0, ALU.mult, ALU.add).then_inc(dve_chain, done.add())
                STT(out=rank1, in0=rank, scalar=1.0, in1=routed, op0=ALU.add, op1=ALU.mult).then_inc(dve_chain, done.add())
                dve.wait_ge(dve_chain, done.n)
                TTN(count[:, 2, :], count[:, 1, :], count[:, 0, :], ALU.subtract).then_inc(dve_chain, done.add())
                dve.wait_ge(dve_chain, done.n)
                TTN(place, rank, bc(count[:, 2, :], 1, TT), ALU.add).then_inc(dve_chain, done.add())
                dve.wait_ge(dve_chain, done.n)
                chosen = [rt[:, i, :, :] for i in (8, 9)]
                for i, oh in enumerate((oh1, oh2)):
                    TTN(chosen[i], oh, place, ALU.mult).then_inc(dve_chain, done.add())
                dve.wait_ge(dve_chain, done.n)
                for i in range(2):
                    dve.tensor_reduce(v[11 + i], chosen[i], AXX, ALU.add).then_inc(dve_chain, done.add())
                dve.wait_ge(dve_chain, done.n)
                for tt in range(TT):
                    for i, dst in enumerate((perm, perm2)):
                        TS(dst[:, tt, :], iota[:, :], v[11 + i][:, tt:tt + 1], norm[:, 7, 6 + tt:7 + tt], ALU.is_equal, ALU.mult).then_inc(dve_chain, done.add())
                    dve.wait_ge(dve_chain, done.n)
                    TTN(perm[:, tt, :], perm[:, tt, :], perm2[:, tt, :], ALU.add).then_inc(perm_ready, 1)
                dve.memset(sortedT[:, :, NPOS:], 0.0).then_inc(offsets_ready, 1)
                for r in range(PASSES):
                    TS(roff[:, r, :], count[:, 2, :], float(SLOT * r), float(NPOS), ALU.add, ALU.min).then_inc(offsets_ready, 1)
                dve.tensor_reduce(v[15][:, 0:1], count[:, 0, :], AXX, ALU.max).then_inc(dve_chain, done.add())
                dve.wait_ge(dve_chain, done.n)
                TS(rmany[:, bass.ds(l, 1)], v[15][:, 0:1], float(SLOT), None, ALU.is_gt).then_inc(counted, 1)
                TS(rank1, rank1, 1.0, None, ALU.subtract).then_inc(dve_chain, done.add())
                dve.wait_ge(dve_chain, done.n)

                def select(p, par, pair=None):
                    if pair is None and (not isinstance(p, int) or p >= 2):
                        dve.wait_ge(turned_psum, p - 1)
                        dve.sem_inc(held, 1)
                    dst = sel[:, par, :, :].rearrange("p t (e s) -> p t e s", e=2)
                    e0 = (p if pair is None else pair) * 2
                    pick = [bc(a[:, :, bass.ds(e0, 2)], 3, SLOT) for a in (rank1, weight)]
                    TTN(dst, bc(bc(iota[:, 0:SLOT], 1, 2), 1, TT), pick[0], ALU.is_equal).then_inc(sel_half, 1)
                    dve.wait_ge(sel_half, p + 1)
                    dve.sem_inc(held, 1)
                    TTN(dst, dst, pick[1], ALU.mult).then_inc(sel_ready, 1)

                def swiglu(p, par):
                    dve.wait_ge(gate_tanh_ready, p + 1)
                    dve.sem_inc(held, 1)
                    STT(out=hidden[:, par, :], in0=gtanh[:, par, :], scalar=1.0, in1=bank(par, 0, DE), op0=ALU.add, op1=ALU.mult).then_inc(hidden_half, 1)
                    dve.wait_ge(hidden_half, p + 1)
                    dve.sem_inc(held, 1)
                    STT(out=hidden[:, par, :], in0=hidden[:, par, :], scalar=0.5, in1=bank(par, DE, 2 * DE), op0=ALU.mult, op1=ALU.mult).then_inc(hidden_ready, 1)

                def sel_out(p, par):
                    dve.wait_ge(hiddenT_sbuf, p + 1)
                    dve.sem_inc(held, 1)
                    dve.tensor_copy(selT[:, par, :], bank(par, 2 * P, 4 * P)).then_inc(selT_sbuf, 1)

                def down_hi(p):
                    dve.wait_ge(down_psum, p + 1)
                    dve.sem_inc(held, 1)
                    dve.tensor_copy(down[:, 512:], bank(3)).then_inc(down_sbuf_hi, 1)

                def step(p, par, last=False):
                    if not last:
                        select(p + 1, 1 - par)
                    sel_out(p, par)
                    down_hi(p)
                    if not last:
                        swiglu(p + 1, 1 - par)

                select(0, 0)
                swiglu(0, 0)
                step(0, 0)
                with dve.Fori(0, NPAIR // 2 - 1) as i:
                    for k in range(2):
                        step(i * 2 + 1 + k, (1 + k) % 2)
                step(NPAIR - 1, 1, last=True)
                for tt in range(TT):
                    dve.wait_ge(moe_psum, tt + 1)
                    dve.tensor_copy(x[:, tt, :], banks(4 + 2 * tt, 2)).then_inc(x_ready, 1)

                def shift_ranks(r):
                    dve.wait_ge(sel_ready, r * NPAIR)
                    dve.sem_inc(held, 1)
                    dve.tensor_scalar(rank1, rank1, float(SLOT), None, ALU.subtract).then_inc(rank_shifted, 1)
                    dve.wait_ge(rank_shifted, r)
                    dve.sem_inc(held, 1)

                def more(p, pair, r):
                    select(p, 0, pair)
                    swiglu(p, 0)
                    sel_out(p, 0)
                    down_hi(p)
                    for tt in range(TT):
                        dve.wait_ge(moe_psum, (p - (NPAIR - 1)) * TT + tt + 1)
                        dve.sem_inc(held, 1)
                        dve.tensor_copy(x[:, tt, :], banks(4 + 2 * tt, 2)).then_inc(x_ready, 1)

                with dve.If(crowded(dve, l) > 0):
                    further_steps(dve, more, shift_ranks)
                leave_layer(dve, l)
            dve.drain().then_inc(first_result_ready, TT)

        @block.tensor
        def _(pe):
            mm = pe.matmul

            def group(dst, lhs, rhs, n, then=None, **kw):
                for c in range(n):
                    last = mm(dst, lhs(c), rhs(c), start=c == 0, stop=c == n - 1, **kw)
                return last

            for semaphore in free_a + free_b:
                pe.sem_inc(semaphore, 1)
            pe.wait_ge(first_constants, 8 + HALF + 5)
            pe.wait_ge(first_params_loaded, 48)
            pe.wait_ge(first_dt_wide, 1)
            NW = DEPTH * STILES
            for i in range(3):
                last = pe.transpose(bank(5, i * NW, (i + 1) * NW), praw[0:NW, i, :], ident[0:NW, 0:NW])
            last.then_inc(first_params_turned, 1)

            with pe.Fori(0, DEPTH) as l:
                def a_ready(a):
                    pe.wait_ge(loaded_a[a % A_SLOTS], (l * A_USES[a % A_SLOTS] + a // A_SLOTS + 1) * 32)
                    pe.sem_inc(held, 1)

                for i in range(KC // 2):
                    pe.wait_ge(first_x_loaded, 16 * TT)
                    for c in (2 * i, 2 * i + 1):
                        for tt in range(TT):
                            last = pe.transpose(bank(XT_BANKS[i], (c % 2) * SEQ + tt * P, (c % 2) * SEQ + (tt + 1) * P),
                                                x[:, tt, c * P:(c + 1) * P], ident[:, :])
                    last.then_inc(hT_psum, 1)
                a_ready(A_U)
                w = slotA_kc(A_U)
                for m in range(CH_T):
                    for c in range(KC):
                        if m == 0 and c < KC // 2:
                            pe.wait_ge(hT_sbuf, c + 1)
                        elif m == 0:
                            pe.wait_ge(hT_sbuf_high, c - KC // 2 + 1)
                        last = mm(bank(2 + m, 0, SEQ), w[:, c, m * P:(m + 1) * P], hT[:, c, :], start=c == 0, stop=c == KC - 1)
                    last.then_inc(u_psum, 1)
                pe.wait_ge(row_scales_ready, TT)
                for tt in range(TT):
                    last = mm(bank(0, tt * P, (tt + 1) * P), ones[:, :], diag[:, tt, :], start=True, stop=True)
                last.then_inc(scale_row_psum, 1)
                a_ready(A_Q)
                w = slotA_kc(A_Q)
                for tt in range(TT):
                    b0 = (6, 0)[tt]
                    if tt:
                        pe.wait_ge(scale_row_sbuf, 1)
                    group(bank(b0), lambda c: hT[:, c, tt * P:(tt + 1) * P], lambda c: w[:, c, :], KC)
                    if tt == 0:
                        a_ready(A_TAIL)
                    last = group(bank(b0 + 1, 0, U0 - 512), lambda c: hT[:, c, tt * P:(tt + 1) * P], lambda c: wtail[:, c, :], KC)
                    last.then_inc(qkv_psum, 1)
                pe.drain().then_inc(free_a[A_U % A_SLOTS], 1)
                pe.sem_inc(free_a[A_Q % A_SLOTS], 1)
                pe.wait_ge(u_sbuf, CH_T)
                for i in range(2):
                    pe.wait_ge(b_scaled, i + 1)
                    for m in range(CH_T):
                        last = pe.transpose(bank(2 + i, m * P, (m + 1) * P),
                                            bwide[:, i, m * QPT:(m + 1) * QPT, :].rearrange("p j s -> p (j s)"), ident[:, :])
                    last.then_inc(ssm_wT_psum, 1)
                pe.wait_ge(c_loaded, 64)
                for i in range(2):
                    for m in range(CH_T):
                        last = pe.transpose(bank(4 + i, m * P, (m + 1) * P),
                                            craw[:, i, m, :, :].rearrange("p d s -> p (d s)"), ident[:, :])
                    last.then_inc(ssm_wT_psum, 1)

                def lora_turn():
                    pe.wait_ge(lora_ready, 2 * TT)
                    pe.wait_ge(qkv_sbuf, 2 * TT)
                    for c in range(QC + KVC):
                        if c >= 2:
                            pe.wait_ge(loraT_sbuf, c - 1)
                        for tt in range(TT):
                            src = lora[:, tt, c:QR:QC] if c < QC else lora[:, tt, QR + c - QC:QR + KVR:KVC]
                            last = pe.transpose(bank(6 + c % 2, tt * P, (tt + 1) * P), src, ident[:, :])
                        last.then_inc(loraT_psum, 1)

                def q_up():
                    pe.wait_ge(loraT_sbuf, QC + KVC)
                    for tt in range(TT):
                        if tt:
                            pe.wait_ge(q_sbuf, 2 * tt)
                        for i in range(2):
                            last = group(bank(6 + i, 0, 4 * QKD), lambda c: loraT[:, c, tt * P:(tt + 1) * P],
                                         lambda c: wuq[:, c, i * 4 * QKD:(i + 1) * 4 * QKD], QC)
                        last.then_inc(q_psum, 1)
                    pe.drain().then_inc(free_a[A_TAIL % A_SLOTS], 1)

                def kv_up():
                    pe.wait_ge(loaded_b[0], (l * (B_USES[0] + 1) + 1) * 16)
                    pe.sem_inc(held, 1)
                    pe.wait_ge(q_sbuf, 4)
                    for tt in range(TT):
                        if tt:
                            pe.wait_ge(k_sbuf, 2 * tt)
                            pe.wait_ge(v_sbuf, 2 * tt)
                        for i in range(2):
                            last = group(bank(6 + i), lambda c: loraT[:, QC + c, tt * P:(tt + 1) * P],
                                         lambda c: wukv[:, c, i * 512:(i + 1) * 512], KVC)
                        last.then_inc(kv_psum, 1)
                    pe.drain().then_inc(free_b[0], 1)

                def qk_turn(hg):
                    pe.wait_ge(qk_ready, 1)
                    pe.wait_ge(v_sbuf, 4)
                    for i in range(4):
                        n = 4 * hg + i
                        if i >= 2:
                            pe.wait_ge(qkT_sbuf, n - 1)
                        for k in range(2):
                            head = (i // 2) * HEADS + hg * 4 + 2 * (i % 2) + k
                            for tt in range(TT):
                                last = pe.transpose(psum[0:QKD, 6 + i % 2, k * SEQ + tt * P:k * SEQ + (tt + 1) * P],
                                                    qk[:, tt, head, :], ident[:, :])
                        last.then_inc(qkT_psum, 1)

                def scores(c, hg, qb):
                    pe.wait_ge(qkT_sbuf, 4 * hg + 4)
                    w = P * (qb + 1)
                    for hh in range(4):
                        dst = bank(6 + hh // 2, hh % 2 * w, (hh % 2 + 1) * w)
                        mm(dst, qkT[0:QKD, 0, hh, qb * P:(qb + 1) * P], qkT[0:QKD, 1, hh, 0:w], start=True, stop=False)
                        last = mm(dst[:, w - CHUNK:], ident[:, :], amask[:, :], start=False, stop=True)
                        if hh % 2:
                            last.then_inc(scores_psum, 1)

                def probs_turn(c, hg, qb):
                    for hh in range(4):
                        pe.wait_ge(probs_ready, 4 * c + hh + 1)
                        for k in range(qb + 1):
                            i = hh * (qb + 1) + k
                            last = pe.transpose(banks(6, 2)[:, i * P:(i + 1) * P], probs[:, hh, k * P:(k + 1) * P], ident[:, :])
                    last.then_inc(probsT_psum, 1)

                def values(c, hg, qb):
                    pe.wait_ge(probsT_sbuf, c + 1)
                    if c:
                        pe.wait_ge(o_sbuf, c)
                    for hh in range(4):
                        lo = hh % 2 * VD
                        for k in range(qb + 1):
                            last = mm(psum[lo:lo + VD, 5, hh // 2 * P:(hh // 2 + 1) * P], vtok[:, k, hg * 4 + hh, :],
                                      probsT[:, hh, k, :], start=k == 0, stop=k == qb)
                    last.then_inc(o_psum, 1)

                def gate(g):
                    a = A_G + g // 2
                    if g % 2 == 0:
                        a_ready(a)
                    pe.wait_ge(ssm_b_sbuf, 2)
                    pe.wait_ge(ssm_c_sbuf, 3)
                    if g >= 2:
                        pe.wait_ge(gates_sbuf, g - 1 if g < 6 else g)
                    w, tt = slotA_kc(a), g % 2
                    last = group(bank(gate_bank(g)), lambda c: hT[:, c, tt * P:(tt + 1) * P], lambda c: w[:, c, :], KC)
                    last.then_inc(gates_psum, 1)
                    if g % 2:
                        pe.drain().then_inc(free_a[a % A_SLOTS], 1)

                def inputs(j):
                    m, q = j // QPT, j % QPT
                    rows = slice(32 * q, 32 * q + 32)
                    if j >= 2:
                        pe.wait_ge(modulated, 2 * j - 2)
                    for i in range(2):
                        last = mm(bank(j % 2, i * SEQ, (i + 1) * SEQ), bT[rows, i, m, :], uT[rows, m, :], start=True, stop=True)
                    last.then_inc(bu_psum, 1)

                def outputs(j0):
                    m = j0 // QPT
                    pe.wait_ge(turned_back, j0 + 2)
                    pe.wait_ge(ssm_c_sbuf, 3)
                    if j0 % QPT == 0 and m >= 2:
                        pe.wait_ge(gelu_arg, m - 1)
                    terms = ((0, backc, 0), (1, backs, 1), (2, backc, 1), (2, backs, 0))
                    for k, (ci, src, i) in enumerate(terms):
                        for j in (j0, j0 + 1):
                            cols = slice(32 * (j % QPT), 32 * (j % QPT) + 32)
                            last = mm(psum[cols, 2 + m % 2, 0:SEQ], cT[:, ci, m, cols], src[:, j % 2, i, :], start=k == 0, stop=k == 3)
                    pe.drain().then_inc(y_used, 2)
                    if j0 % QPT == QPT - 2:
                        pe.sem_inc(y_psum, 1)

                def attn_proj(tt, b, halves=(0, 1)):
                    w = slotA(A_AP).rearrange("p (c n) -> p c n", c=CH_T)
                    for i in halves:
                        last = group(bank(b + i), lambda c: oT[:, c, tt * P:(tt + 1) * P], lambda c: w[:, c, i * 512:(i + 1) * 512], HEADS // 2)
                        last.then_inc(attn_proj_psum, 1)

                pe.wait_ge(ssm_b_sbuf, 2)
                pe.wait_ge(qkv_sbuf, 2 * TT)
                inputs(0)
                for j in range(STILES):
                    if j + 1 < STILES:
                        inputs(j + 1)
                    for g in GATES_AT.get(j, []):
                        gate(g)
                    attention(j, dict(lora=lora_turn, q=q_up, kv=kv_up, turn=qk_turn, scores=scores, probs=probs_turn, values=values))
                    if j == STILES - 1:
                        a_ready(A_AP)
                        pe.wait_ge(o_sbuf, 4)
                        attn_proj(0, 6, (0,))
                    if j % 2:
                        outputs(j - 1)

                def glu(half, tt, b):
                    w = slotA(A_GLU + 1 - half).rearrange("p (c n) -> p c n", c=CH_T)
                    for i in range(2):
                        last = group(bank(b + i), lambda c: uT[:, c, tt * P:(tt + 1) * P], lambda c: w[:, c, i * 512:(i + 1) * 512], CH_T)
                    last.then_inc(glu_psum, 1)

                attn_proj(0, 6, (1,))
                a_ready(A_GLU)
                a_ready(A_GLU + 1)
                pe.wait_ge(gelu_ready, CH_T)
                pe.wait_ge(gates_sbuf, 8)
                glu(1, 0, 2)
                glu(1, 1, 4)
                pe.drain().then_inc(free_a[A_GLU % A_SLOTS], 1)
                glu(0, 0, 0)
                pe.wait_ge(glu_gate_tanh, 1)
                glu(0, 1, 2)
                pe.wait_ge(glu_read, 1)
                attn_proj(1, 0)
                pe.drain().then_inc(free_a[(A_GLU + 1) % A_SLOTS], 1)
                pe.sem_inc(free_a[A_AP % A_SLOTS], 1)

                def turn4(chunk, b, signal):
                    for i in range(2):
                        for c in range(4 * i, 4 * i + 4):
                            last = pe.transpose(bank(b + i, (c % 4) * P, (c % 4 + 1) * P), chunk(c), ident[:, :])
                        last.then_inc(signal, 1)

                def out_proj(tt, b):
                    for g in range(2):
                        w = slotA_kc(A_OUT + g)
                        for c in range(KC):
                            if c % 4 == 0:
                                pe.wait_ge(mergedT_sbuf, 2 * tt + c // 4 + 1)
                            last = mm(bank(b + g), hT[:, c, tt * P:(tt + 1) * P], w[:, c, :], start=c == 0, stop=c == KC - 1)
                    last.then_inc(out_psum, 1)

                pe.wait_ge(glu_gate_tanh, 2)
                pe.wait_ge(merged_ready, 1)
                turn4(lambda c: merged[:, 0, c * P:(c + 1) * P], 4, mergedT_psum)
                a_ready(A_OUT)
                a_ready(A_OUT + 1)
                out_proj(0, 6)
                pe.wait_ge(merged_ready, 2)
                turn4(lambda c: merged[:, 1, c * P:(c + 1) * P], 2, mergedT_psum)
                out_proj(1, 0)
                pe.drain().then_inc(free_a[A_OUT % A_SLOTS], 1)
                pe.sem_inc(free_a[(A_OUT + 1) % A_SLOTS], 1)

                pe.wait_ge(x_mixed, 1)
                turn4(lambda c: x[:, 0, c::KC], 4, h2T_psum)
                pe.wait_ge(x_mixed, 2)
                turn4(lambda c: x[:, 1, c::KC], 2, h2T_psum)
                pe.wait_ge(router_loaded, 32)
                for c in range(KC):
                    pe.wait_ge(h2T_sbuf, c + 1)
                    pe.wait_ge(h2T_sbuf_second, c + 1)
                    last = mm(psum[0:ROUTE, 0, 0:SEQ], wroute[:, c, :], hT[:, c, :], start=c == 0, stop=c == KC - 1)
                last.then_inc(logitsT_psum, 1)
                pe.wait_ge(logitsT_sbuf, 1)
                for tt in range(TT):
                    last = pe.transpose(bank(0, tt * 64, tt * 64 + ROUTE), logitsT[0:ROUTE, tt * P:(tt + 1) * P], ident[0:ROUTE, 0:ROUTE])
                last.then_inc(logits_psum, 1)
                def residual(tt):
                    for i in range(2):
                        mm(bank(4 + 2 * tt + i), ident[:, :], x[:, tt, i * 512:(i + 1) * 512], start=True, stop=False)

                residual(0)
                residual(1)
                pe.wait_ge(routes_ready, 1)
                routed = rt[:, 3, :, :]
                both = rt[:, 3, :, :].rearrange("p t e -> p (t e)")
                mm(bank(1, 0, TT * NE), before[:, :], both, start=True, stop=False)
                mm(bank(1, NE, 2 * NE), ones[:, :], routed[:, 0, :], start=False, stop=True)
                mm(bank(1, 2 * NE, 4 * NE), ones[:, :], both, start=True, stop=True).then_inc(rank_psum, 1)
                for c in range(KC):
                    if c >= 4:
                        pe.wait_ge(sorted_sbuf, c - 3)
                    for tt in range(TT):
                        pe.wait_ge(perm_ready, tt + 1)
                        last = mm(bank(c % 4), x[:, tt, c::KC], perm[:, tt, :], start=tt == 0, stop=tt == TT - 1)
                    last.then_inc(sorted_psum, 1)

                def gate_up(p, par, weights, free=None):
                    pe.wait_ge(pair_copied, p * 2 + 2)
                    pe.sem_inc(held, 1)
                    for c in range(KC):
                        for e in range(2):
                            w = weights[:, e, :].rearrange("p (u c n) -> p u c n", u=2, c=KC)
                            last = mm(psum[e * SLOT:(e + 1) * SLOT, par, :], pairT[:, par, c, e * SLOT:(e + 1) * SLOT],
                                      w[:, :, c, :], start=c == 0, stop=c == KC - 1)
                            if c == KC - 1 and free:
                                last.then_inc(free[e], 1)
                    pe.drain().then_inc(hidden_psum, 1)

                def bank_read(p):
                    pe.wait_ge(hiddenT_sbuf, p - 1)
                    pe.sem_inc(held, 1)
                    pe.wait_ge(selT_sbuf, p - 1)
                    pe.sem_inc(held, 1)

                def gate_up_ring(p, par, ring, n):
                    slots = (2 * ring, 2 * ring + 1)
                    for s in slots:
                        pe.wait_ge(loaded_a[s], (l * A_USES[s] + n + 1) * 32)
                        pe.sem_inc(held, 1)
                    gate_up(p, par, ringA[:, 2 * ring:2 * ring + 2, :], free_a[2 * ring:2 * ring + 2])

                def turn_pair(p, par):
                    pe.wait_ge(hidden_ready, p + 1)
                    pe.sem_inc(held, 1)
                    for c in range(2):
                        pe.transpose(bank(par, c * P, (c + 1) * P), hidden[:, par, c::2], ident[:, :])
                    pe.wait_ge(sel_ready, p + 1)
                    pe.sem_inc(held, 1)
                    for tt in range(TT):
                        last = pe.transpose(bank(par, (2 + tt) * P, (3 + tt) * P), sel[:, par, tt, :], ident[:, :])
                    last.then_inc(turned_psum, 1)

                def scatter(p, par, start=False, end=False):
                    pe.wait_ge(selT_sbuf, p + 1)
                    pe.sem_inc(held, 1)
                    pe.wait_ge(down_sbuf_lo, p + 1)
                    pe.sem_inc(held, 1)
                    pe.wait_ge(down_sbuf_hi, p + 1)
                    pe.sem_inc(held, 1)
                    for tt in range(TT):
                        for i in range(2):
                            if start:
                                mm(bank(4 + 2 * tt + i), ident[:, :], x[:, tt, i * 512:(i + 1) * 512], start=True, stop=False)
                            last = mm(bank(4 + 2 * tt + i), selT[:, par, tt * P:(tt + 1) * P], down[:, i * 512:(i + 1) * 512],
                                      start=False, stop=end)
                        if end:
                            last.then_inc(moe_psum, 1)

                def down_mm(p, weights, free=None):
                    pe.wait_ge(hiddenT_sbuf, p + 1)
                    pe.sem_inc(held, 1)
                    for i in range(2):
                        for c in range(2):
                            for e in range(2):
                                w = weights[e].rearrange("p (c n) -> p c n", c=2)
                                last = mm(psum[e * SLOT:(e + 1) * SLOT, 2 + i, :], hiddenT[:, c, e * SLOT:(e + 1) * SLOT],
                                          w[:, c, i * 512:(i + 1) * 512], start=c == 0, stop=c == 1)
                                if i == 1 and c == 1 and free:
                                    last.then_inc(free[e], 1)
                    pe.drain().then_inc(down_psum, 1)

                def down_ring(p, ring, n):
                    slots = (2 * ring, 2 * ring + 1)
                    for s in slots:
                        pe.wait_ge(loaded_b[s], (b_use(l, s, n) + 1) * 16)
                        pe.sem_inc(held, 1)
                    down_mm(p, [ringB[:, s, :] for s in slots], free_b[2 * ring:2 * ring + 2])

                gate_up_ring(0, 0, 0, A_FIRST)
                gate_up_ring(1, 1, 1, A_FIRST)
                turn_pair(0, 0)
                down_ring(0, 0, 0)
                bank_read(OWN_PAIR)
                pe.wait_ge(own_pair_loaded, 64)
                gate_up(OWN_PAIR, 0, own_pair)
                turn_pair(1, 1)
                scatter(0, 0)
                down_ring(1, 1, 0)
                bank_read(3)
                gate_up_ring(3, 1, 0, A_FIRST + 1)
                turn_pair(OWN_PAIR, 0)
                scatter(1, 1)
                pe.wait_ge(own_down_loaded, 32)
                down_mm(OWN_PAIR, own_down)
                with pe.Fori(0, NPAIR // 2 - 2) as i:
                    for k in range(2):
                        p = i * 2 + 3 + k
                        bank_read(p + 1)
                        gate_up_ring(p + 1, k, 1 - k, i + A_FIRST + 1 + k)
                        turn_pair(p, 1 - k)
                        scatter(p - 1, k)
                        down_ring(p, k, i + 1)
                turn_pair(NPAIR - 1, 1)
                scatter(NPAIR - 2, 0)
                down_ring(NPAIR - 1, 0, B_USES[0] - 1)
                scatter(NPAIR - 1, 1, end=True)

                def more(p, pair, r):
                    pe.wait_ge(x_ready, (p - (NPAIR - 1)) * TT)
                    pe.sem_inc(held, 1)
                    pe.sem_inc(more_free, 1)
                    pe.wait_ge(more_loaded, (p - (NPAIR - 1)) * 96)
                    pe.sem_inc(held, 1)
                    gate_up(p, 0, ringA[:, 0:2, :])
                    turn_pair(p, 0)
                    down_mm(p, [ringB[:, e, :] for e in range(2)])
                    scatter(p, 0, start=True, end=True)

                with pe.If(crowded(pe, l) > 0):
                    further_steps(pe, more)
                leave_layer(pe, l)


def gate_bank(g):
    return 5 if g in (1, 3, 5) else 4


GATES_AT = {0: [0, 1], 3: [2, 3, 4, 5], 5: [6], 7: [7]}


def attention(slot, do):
    stages = {0: [("lora",)], 1: [("q",)], 2: [("kv",), ("qk",)], 3: [("turn", 0)],
              4: [("scores", 0, 0, 0)], 5: [("probs", 0, 0, 0)], 6: [("values", 0, 0, 0), ("scores", 1, 0, 1)],
              7: [("probs", 1, 0, 1)], 8: [("values", 1, 0, 1), ("turn", 1)], 9: [("scores", 2, 1, 0)],
              10: [("probs", 2, 1, 0)], 11: [("values", 2, 1, 0), ("scores", 3, 1, 1)], 12: [("probs", 3, 1, 1)],
              13: [("values", 3, 1, 1)]}
    for name, *args in stages.get(slot, []):
        if name in do:
            do[name](*args)


_INS = ["x", "positions", "norm_mix_g", "w_in", "q_lora_g", "w_uq", "kv_lora_g", "w_ukv", "q_head_g", "k_head_g",
        "w_attn_proj", "lam_re", "lam_im", "log_dt", "b_re", "b_im", "c_re", "c_im", "d_skip", "w_glu", "w_out",
        "norm_ffn_g", "w_router_group", "w_router_expert", "w_exp_gate", "w_exp_up", "w_exp_down"]


def kernel(**inputs):
    import numpy as _np
    import concourse.bacc as _bacc
    from concourse import mybir as _mybir
    from concourse.bass_utils import run_bass_kernel_spmd as _run

    nc = _bacc.Bacc("TRN2", target_bir_lowering=False, num_devices=1, dynamic_dma_scratch_size=256)
    arrays, tensors = {}, {}
    for name in _INS:
        a = _np.ascontiguousarray(inputs[name])
        arrays[f"in_{name}"] = a
        tensors[name] = nc.dram_tensor(f"in_{name}", a.shape, _mybir.dt.from_np(a.dtype), kind="ExternalInput").ap()
    out = nc.dram_tensor("out_0", (1, SEQ, D), F32, kind="ExternalOutput").ap()
    build(nc, tensors, out)
    r = _run(nc, [arrays], core_ids=[0])
    return r.results[0]["out_0"]
```
